# Optimizing a Trainium2 kernel written in Bass

```python
import jax, jax.numpy as jnp
from jax import lax
import numpy as np
import math

D_MODEL = 1024
BATCH = 1
SEQ = 512
DEPTH = 1

PLE_DIM = 256
HEAD_DIM = 64
FOX_HEADS = 8
SB_HEADS = 8
FOX_WIDTH = FOX_HEADS * HEAD_DIM
SB_WIDTH = SB_HEADS * HEAD_DIM
D_FF = 2816
Q_BLOCK = 128
EPS = 1e-6
FORGET_BIAS_INIT = 2.0
IN_SIZES = (FOX_WIDTH, FOX_WIDTH, FOX_WIDTH, FOX_HEADS, SB_WIDTH, SB_WIDTH, SB_WIDTH, D_MODEL, D_MODEL)
IN_WIDTH = 3 * FOX_WIDTH + FOX_HEADS + 3 * SB_WIDTH + 2 * D_MODEL


def rms_norm(x, g):
    xf = x.astype(jnp.float32)
    y = xf * lax.rsqrt(jnp.mean(xf * xf, axis=-1, keepdims=True) + EPS)
    return (y * g.astype(jnp.float32)).astype(x.dtype)

def swiglu(h, w_gate, w_up, w_down):
    return (jax.nn.silu(h @ w_gate) * (h @ w_up)) @ w_down

def to_blocks(t):
    b, s = t.shape[0], t.shape[1]
    return jnp.moveaxis(t.reshape(b, s // Q_BLOCK, Q_BLOCK, *t.shape[2:]), 1, 0)

def from_blocks(t):
    nb, b = t.shape[0], t.shape[1]
    return jnp.moveaxis(t, 0, 1).reshape(b, nb * Q_BLOCK, -1)

def forgetting_attention(q, k, v, log_f):
    s_len = q.shape[1]
    scale = HEAD_DIM ** -0.5
    F = jnp.cumsum(log_f, axis=1)
    Fk = jnp.transpose(F, (0, 2, 1))[:, :, None, :]
    kpos = jnp.arange(s_len)
    qpos = kpos.reshape(s_len // Q_BLOCK, Q_BLOCK)

    def one_block(args):
        qi, Fi, pi = args
        logits = jnp.einsum('bqhd,bkhd->bhqk', qi, k).astype(jnp.float32) * scale
        logits = logits + jnp.transpose(Fi, (0, 2, 1))[..., None] - Fk
        mask = pi[:, None] >= kpos[None, :]
        logits = jnp.where(mask, logits, -jnp.inf)
        w = jax.nn.softmax(logits, axis=-1)
        return jnp.einsum('bhqk,bkhd->bqhd', w.astype(v.dtype), v)

    out = lax.map(one_block, (to_blocks(q), to_blocks(F), qpos))
    return from_blocks(out)

def stick_breaking_attention(q, k, v):
    s_len = q.shape[1]
    scale = HEAD_DIM ** -0.5
    kpos = jnp.arange(s_len)
    qpos = kpos.reshape(s_len // Q_BLOCK, Q_BLOCK)

    def one_block(args):
        qi, pi = args
        z = jnp.einsum('bqhd,bkhd->bhqk', qi, k).astype(jnp.float32) * scale
        mask = kpos[None, :] < pi[:, None]
        log_beta = jax.nn.log_sigmoid(z)
        log_1m = jnp.where(mask, jax.nn.log_sigmoid(-z), 0.0)
        after = lax.cumsum(log_1m, axis=3, reverse=True) - log_1m
        a = jnp.where(mask, jnp.exp(log_beta + after), 0.0)
        return jnp.einsum('bhqk,bkhd->bqhd', a.astype(v.dtype), v)

    out = lax.map(one_block, (to_blocks(q), qpos))
    return from_blocks(out)

def split_columns(t):
    outs, start = [], 0
    for size in IN_SIZES:
        outs.append(t[..., start:start + size])
        start += size
    return outs

def first_inputs(seed: int = 0) -> dict:
    key = jax.random.key(seed)
    ks = jax.random.split(key, 24)

    def w(k, shape, fan_in):
        return jax.random.normal(k, shape, jnp.float32) * (fan_in ** -0.5)

    def gain(k, shape):
        return 1.0 + 0.05 * jax.random.normal(k, shape, jnp.float32)

    L = DEPTH
    return {
        "x": jax.random.normal(ks[0], (BATCH, SEQ, D_MODEL), jnp.float32),
        "p": jax.random.normal(ks[1], (DEPTH, BATCH, SEQ, PLE_DIM), jnp.float32),
        "ffn1_norm": gain(ks[2], (L, D_MODEL)),
        "ffn1_w_gate": w(ks[3], (L, D_MODEL, D_FF), D_MODEL),
        "ffn1_w_up": w(ks[4], (L, D_MODEL, D_FF), D_MODEL),
        "ffn1_w_down": w(ks[5], (L, D_FF, D_MODEL), D_FF),
        "mix_norm": gain(ks[6], (L, D_MODEL)),
        "w_in": w(ks[7], (L, D_MODEL, IN_WIDTH), D_MODEL),
        "forget_bias": FORGET_BIAS_INIT + 0.1 * jax.random.normal(ks[8], (L, FOX_HEADS), jnp.float32),
        "q_norm": gain(ks[9], (L, HEAD_DIM)),
        "k_norm": gain(ks[10], (L, HEAD_DIM)),
        "w_branch_fox": w(ks[11], (L, FOX_WIDTH, D_MODEL), FOX_WIDTH),
        "w_branch_sb": w(ks[12], (L, SB_WIDTH, D_MODEL), SB_WIDTH),
        "w_out": w(ks[13], (L, D_MODEL, D_MODEL), D_MODEL),
        "ffn2_norm": gain(ks[14], (L, D_MODEL)),
        "ffn2_w_gate": w(ks[15], (L, D_MODEL, D_FF), D_MODEL),
        "ffn2_w_up": w(ks[16], (L, D_MODEL, D_FF), D_MODEL),
        "ffn2_w_down": w(ks[17], (L, D_FF, D_MODEL), D_FF),
        "ple_norm": gain(ks[18], (L, D_MODEL)),
        "w_ple_gate": w(ks[19], (L, D_MODEL, D_MODEL), D_MODEL),
        "w_ple_proj": w(ks[20], (L, PLE_DIM, D_MODEL), PLE_DIM),
    }

def first_block(x, p, ffn1_norm, ffn1_w_gate, ffn1_w_up, ffn1_w_down, mix_norm, w_in,
              forget_bias, q_norm, k_norm, w_branch_fox, w_branch_sb, w_out,
              ffn2_norm, ffn2_w_gate, ffn2_w_up, ffn2_w_down, ple_norm,
              w_ple_gate, w_ple_proj):
    b, s_len, _ = x.shape
    for i in range(DEPTH):
        x = x + 0.5 * swiglu(rms_norm(x, ffn1_norm[i]), ffn1_w_gate[i], ffn1_w_up[i], ffn1_w_down[i])

        h = rms_norm(x, mix_norm[i])
        fq, fk, fv, f_logit, sq, sk, sv, g_fox, g_sb = split_columns(h @ w_in[i])
        fq = rms_norm(fq.reshape(b, s_len, FOX_HEADS, HEAD_DIM), q_norm[i])
        fk = rms_norm(fk.reshape(b, s_len, FOX_HEADS, HEAD_DIM), k_norm[i])
        fv = fv.reshape(b, s_len, FOX_HEADS, HEAD_DIM)
        log_f = jax.nn.log_sigmoid((f_logit + forget_bias[i]).astype(jnp.float32))
        y_fox = forgetting_attention(fq, fk, fv, log_f)

        sq = sq.reshape(b, s_len, SB_HEADS, HEAD_DIM)
        sk = sk.reshape(b, s_len, SB_HEADS, HEAD_DIM)
        sv = sv.reshape(b, s_len, SB_HEADS, HEAD_DIM)
        y_sb = stick_breaking_attention(sq, sk, sv)

        merged = (jax.nn.sigmoid(g_fox) * (y_fox @ w_branch_fox[i])
                  + jax.nn.sigmoid(g_sb) * (y_sb @ w_branch_sb[i]))
        x = x + merged @ w_out[i]

        x = x + 0.5 * swiglu(rms_norm(x, ffn2_norm[i]), ffn2_w_gate[i], ffn2_w_up[i], ffn2_w_down[i])

        x = x + jax.nn.sigmoid(rms_norm(x, ple_norm[i]) @ w_ple_gate[i]) * (p[i] @ w_ple_proj[i])
    return x


HY_WIDTH = 512
HY_ORDER = 2
SHORT_CONV = 3
FILTER_EMB = 33
FILTER_HIDDEN = 64
DECAY_TARGET = 1e-2
FAST_DECAY = 0.3
SLOW_DECAY = 1.5
MIN_DECAY = math.log(DECAY_TARGET) / SLOW_DECAY
MAX_DECAY = math.log(DECAY_TARGET) / FAST_DECAY

MLA_HEADS = 8
QK_NOPE = 64
QK_ROPE = 32
QK_DIM = QK_NOPE + QK_ROPE
V_DIM = 64
Q_LORA = 384
KV_LORA = 256
ATTN_WIDTH = MLA_HEADS * V_DIM
ROPE_THETA = 10000.0

IN_COLS = 4 * HY_WIDTH + Q_LORA + KV_LORA + QK_ROPE + ATTN_WIDTH + 2 * D_MODEL


def rms_norm_2(x, g):
    xf = x.astype(jnp.float32)
    y = xf * lax.rsqrt(jnp.mean(xf * xf, axis=-1, keepdims=True) + EPS)
    return (y * g.astype(jnp.float32)).astype(x.dtype)

def short_conv(u, w, b):
    L = u.shape[1]
    pad = SHORT_CONV // 2
    up = jnp.pad(u, ((0, 0), (pad, pad), (0, 0)))
    return sum(up[:, j:j + L] * w[j] for j in range(SHORT_CONV)) + b

def hyena_filter_spectra(L, w_f1, b_f1, freq_1, w_f2, b_f2, freq_2, w_f3):
    t = jnp.linspace(0.0, 1.0, L, dtype=jnp.float32)[:, None]
    bands = (FILTER_EMB - 1) // 2
    f = jnp.linspace(1e-4, bands - 1, bands, dtype=jnp.float32)
    ang = (2.0 * jnp.pi / L) * jnp.arange(L, dtype=jnp.float32)[:, None] * f[None, :]
    z = jnp.concatenate([t, jnp.cos(ang), -jnp.sin(ang)], axis=-1)
    h = jnp.sin(freq_1 * (z @ w_f1 + b_f1))
    h = jnp.sin(freq_2 * (h @ w_f2 + b_f2))
    k = (h @ w_f3).reshape(L, HY_ORDER, 2, HY_WIDTH)
    deltas = jnp.abs(jnp.linspace(MIN_DECAY, MAX_DECAY, HY_WIDTH, dtype=jnp.float32))
    decay = jnp.exp(-t * deltas)
    k = k * decay[:, None, None, :]
    k_full = jnp.concatenate([k[:, :, 0], k[::-1, :, 1]], axis=0)
    return jnp.fft.rfft(k_full.astype(jnp.float32), axis=0)

def long_conv(u, k_spec, bias):
    L = u.shape[1]
    uf = u.astype(jnp.float32)
    y = jnp.fft.irfft(jnp.fft.rfft(uf, n=2 * L, axis=1) * k_spec[None], n=2 * L, axis=1)[:, :L]
    return (y + uf * bias.astype(jnp.float32)).astype(u.dtype)

def rotary(t, cos, sin):
    t1, t2 = jnp.split(t, 2, axis=-1)
    c = cos[:, None, :].astype(t.dtype)
    s = sin[:, None, :].astype(t.dtype)
    return jnp.concatenate([t1 * c - t2 * s, t1 * s + t2 * c], axis=-1)

def dense_bidirectional_attention(q, k, v):
    B, L, H, Dk = q.shape
    nb = L // Q_BLOCK
    scale = 1.0 / math.sqrt(Dk)
    kt = k.transpose(0, 2, 1, 3)
    vt = v.transpose(0, 2, 1, 3)
    qb = q.reshape(B, nb, Q_BLOCK, H, Dk).transpose(1, 0, 3, 2, 4)

    def one_block(qblk):
        s = jnp.einsum('bhqd,bhkd->bhqk', qblk, kt).astype(jnp.float32) * scale
        p = jax.nn.softmax(s, axis=-1).astype(vt.dtype)
        return jnp.einsum('bhqk,bhkd->bqhd', p, vt)

    o = lax.map(one_block, qb)
    return o.transpose(1, 0, 2, 3, 4).reshape(B, L, H * v.shape[-1])

def second_inputs(seed: int = 0) -> dict:
    key = jax.random.key(seed)
    ks = jax.random.split(key, 24)
    f32 = jnp.float32

    def nrm(k, shape, scale):
        return jax.random.normal(k, shape, f32) * scale

    n = DEPTH
    return {
        'x': nrm(ks[0], (BATCH, SEQ, D_MODEL), 1.0),
        'g_norm': 1.0 + nrm(ks[1], (n, D_MODEL), 0.02),
        'w_in': nrm(ks[2], (n, D_MODEL, IN_COLS), D_MODEL ** -0.5),
        'b_gate': nrm(ks[3], (n, 2 * D_MODEL), 0.02),
        'w_short': nrm(ks[4], (n, SHORT_CONV, 3 * HY_WIDTH), SHORT_CONV ** -0.5),
        'b_short': nrm(ks[5], (n, 3 * HY_WIDTH), 0.02),
        'w_f1': nrm(ks[6], (n, FILTER_EMB, FILTER_HIDDEN), FILTER_EMB ** -0.5),
        'b_f1': nrm(ks[7], (n, FILTER_HIDDEN), 0.02),
        'freq_1': 1.0 + nrm(ks[8], (n, FILTER_HIDDEN), 0.02),
        'w_f2': nrm(ks[9], (n, FILTER_HIDDEN, FILTER_HIDDEN), FILTER_HIDDEN ** -0.5),
        'b_f2': nrm(ks[10], (n, FILTER_HIDDEN), 0.02),
        'freq_2': 1.0 + nrm(ks[11], (n, FILTER_HIDDEN), 0.02),
        'w_f3': nrm(ks[12], (n, FILTER_HIDDEN, HY_ORDER * 2 * HY_WIDTH), 2.0 * (FILTER_HIDDEN * SEQ) ** -0.5),
        'hy_bias': nrm(ks[13], (n, HY_ORDER, HY_WIDTH), 0.1),
        'w_hy_out': nrm(ks[14], (n, HY_WIDTH, D_MODEL), HY_WIDTH ** -0.5),
        'g_cq': 1.0 + nrm(ks[15], (n, Q_LORA), 0.02),
        'w_uq': nrm(ks[16], (n, Q_LORA, MLA_HEADS * QK_DIM), Q_LORA ** -0.5),
        'g_ckv': 1.0 + nrm(ks[17], (n, KV_LORA), 0.02),
        'w_ukv': nrm(ks[18], (n, KV_LORA, MLA_HEADS * (QK_NOPE + V_DIM)), KV_LORA ** -0.5),
        'g_qn': 1.0 + nrm(ks[19], (n, QK_DIM), 0.02),
        'g_kn': 1.0 + nrm(ks[20], (n, QK_DIM), 0.02),
        'w_attn_out': nrm(ks[21], (n, ATTN_WIDTH, D_MODEL), ATTN_WIDTH ** -0.5),
        'w_out': nrm(ks[22], (n, D_MODEL, D_MODEL), D_MODEL ** -0.5),
    }

def second_block(x, g_norm, w_in, b_gate, w_short, b_short, w_f1, b_f1, freq_1, w_f2, b_f2, freq_2,
              w_f3, hy_bias, w_hy_out, g_cq, w_uq, g_ckv, w_ukv, g_qn, g_kn, w_attn_out, w_out):
    B, L, _ = x.shape
    pos = jnp.arange(L, dtype=jnp.float32)
    inv_freq = ROPE_THETA ** (-jnp.arange(0, QK_ROPE, 2, dtype=jnp.float32) / QK_ROPE)
    ang = pos[:, None] * inv_freq[None, :]
    cos, sin = jnp.cos(ang), jnp.sin(ang)

    split_at = list(np.cumsum([3 * HY_WIDTH, HY_WIDTH, Q_LORA, KV_LORA, QK_ROPE, ATTN_WIDTH, D_MODEL]))

    for l in range(DEPTH):
        h = rms_norm_2(x, g_norm[l])
        proj = h @ w_in[l]
        hy_in, z_hy, c_q, c_kv, k_rope, z_attn, gate_hy, gate_attn = jnp.split(proj, split_at, axis=-1)

        u = short_conv(hy_in, w_short[l], b_short[l])
        v_h, x1, x2 = jnp.split(u, 3, axis=-1)
        k_spec = hyena_filter_spectra(L, w_f1[l], b_f1[l], freq_1[l], w_f2[l], b_f2[l], freq_2[l], w_f3[l])
        zc = v_h
        for o, gate in enumerate((x1, x2)):
            zc = gate * long_conv(zc, k_spec[:, o], hy_bias[l, o])
        u_hy = (zc * jax.nn.silu(z_hy)) @ w_hy_out[l]

        q = (rms_norm_2(c_q, g_cq[l]) @ w_uq[l]).reshape(B, L, MLA_HEADS, QK_DIM)
        kv = (rms_norm_2(c_kv, g_ckv[l]) @ w_ukv[l]).reshape(B, L, MLA_HEADS, QK_NOPE + V_DIM)
        k_nope, v_a = kv[..., :QK_NOPE], kv[..., QK_NOPE:]
        k_r = jnp.broadcast_to(k_rope[:, :, None, :], (B, L, MLA_HEADS, QK_ROPE))
        k = jnp.concatenate([k_nope, k_r], axis=-1)
        q = rms_norm_2(q, g_qn[l])
        k = rms_norm_2(k, g_kn[l])
        q = jnp.concatenate([q[..., :QK_NOPE], rotary(q[..., QK_NOPE:], cos, sin)], axis=-1)
        k = jnp.concatenate([k[..., :QK_NOPE], rotary(k[..., QK_NOPE:], cos, sin)], axis=-1)
        attn = dense_bidirectional_attention(q, k, v_a)
        u_attn = (attn * jax.nn.silu(z_attn)) @ w_attn_out[l]

        gates = jax.nn.sigmoid(jnp.concatenate([gate_hy, gate_attn], axis=-1) + b_gate[l])
        g_hy, g_at = jnp.split(gates, 2, axis=-1)
        merged = g_hy * u_hy + g_at * u_attn
        x = x + merged @ w_out[l]
    return x


def setup_inputs(seed=0):
    out = dict(first_inputs(seed))
    for name, value in second_inputs(seed + 1).items():
        if name != "x":
            out[name + "_2"] = value
    return out


def reference(
    x, p, ffn1_norm, ffn1_w_gate, ffn1_w_up, ffn1_w_down, mix_norm, w_in, forget_bias, q_norm,
    k_norm, w_branch_fox, w_branch_sb, w_out, ffn2_norm, ffn2_w_gate, ffn2_w_up, ffn2_w_down,
    ple_norm, w_ple_gate, w_ple_proj, g_norm_2, w_in_2, b_gate_2, w_short_2, b_short_2, w_f1_2,
    b_f1_2, freq_1_2, w_f2_2, b_f2_2, freq_2_2, w_f3_2, hy_bias_2, w_hy_out_2, g_cq_2, w_uq_2,
    g_ckv_2, w_ukv_2, g_qn_2, g_kn_2, w_attn_out_2, w_out_2,
):
    x = first_block(
        x, p, ffn1_norm, ffn1_w_gate, ffn1_w_up, ffn1_w_down, mix_norm, w_in, forget_bias,
        q_norm, k_norm, w_branch_fox, w_branch_sb, w_out, ffn2_norm, ffn2_w_gate, ffn2_w_up,
        ffn2_w_down, ple_norm, w_ple_gate, w_ple_proj,
    )
    return second_block(
        x, g_norm_2, w_in_2, b_gate_2, w_short_2, b_short_2, w_f1_2, b_f1_2, freq_1_2, w_f2_2,
        b_f2_2, freq_2_2, w_f3_2, hy_bias_2, w_hy_out_2, g_cq_2, w_uq_2, g_ckv_2, w_ukv_2,
        g_qn_2, g_kn_2, w_attn_out_2, w_out_2,
    )


_drawn_inputs = setup_inputs


def setup_inputs(seed=0):
    import zlib

    import numpy as np

    out = dict(_drawn_inputs(seed))
    spreads = {}
    factors = {'ffn1_norm': 2.677,
     'forget_bias': 33.728,
     'q_norm': 7.198,
     'k_norm': 7.061,
     'ffn2_norm': 3.365,
     'ple_norm': 26.434,
     'g_norm_2': 8.0,
     'b_gate_2': 21.549,
     'b_short_2': 8.0,
     'b_f1_2': 8.0,
     'freq_1_2': 8.0,
     'b_f2_2': 8.0,
     'freq_2_2': 8.0,
     'hy_bias_2': 3.904,
     'g_cq_2': 64.0,
     'w_uq_2': 2.817,
     'g_ckv_2': 64.0,
     'g_qn_2': 64.0,
     'g_kn_2': 64.0}
    for name, (base, spread) in spreads.items():
        noise = np.random.default_rng([zlib.crc32(name.encode()), seed]).standard_normal(out[name].shape)
        drawn = base * np.exp(spread * noise) if base else spread * noise
        out[name] = __import__('jax').numpy.asarray(drawn.astype(out[name].dtype))
    for name, factor in factors.items():
        out[name] = (out[name] * factor).astype(out[name].dtype)
    return out
```

```python
from contextlib import ExitStack
import math

import numpy as np

import concourse.bass as bass
from concourse import mybir

F32 = mybir.dt.float32
F32R = mybir.dt.float32r
ACT = mybir.ActivationFunctionType
ALU = mybir.AluOpType
AXX = mybir.AxisListType.X

P = 128
D = 1024
T = 512
DT = D // P
TT = T // P
DFF = 2816
FH = DFF // P // 2
HEADS = 8
HD = 64
EPS = 1e-6
NEG = -1.0e30
BIG = float(1.5 * 2 ** 23)
ROPE_THETA = 10000.0
ROPE = 32
QKD = 96

WIDTH = {"k": 1024, "d": FH * P, "p": 10 * P}
SEGMENTS = [
    ("ffn1_up0", 22, "k"), ("ffn1_down0", 8, "d"), ("ffn1_up1", 22, "k"), ("ffn1_down1", 8, "d"),
    ("fox_q", 4, "k"), ("fox_k", 4, "k"), ("fox_f", 1, "k"), ("fox_v", 4, "k"),
    ("sb_q", 4, "k"), ("sb_k", 4, "k"), ("sb_v", 4, "k"), ("merge1", 24, "k"), ("out1", 8, "k"),
    ("ffn2_up0", 22, "k"), ("ffn2_down0", 8, "d"), ("ffn2_up1", 22, "k"), ("ffn2_down1", 8, "d"),
    ("ple", 8, "p"),
    ("mla_cq", 3, "k"), ("mla_ckv", 2, "k"), ("mla_kr", 1, "k"), ("mla_qk", 8, "k"), ("mla_v", 1, "k"),
    ("mla_z", 4, "k"),
    ("spectra", 16, "k"), ("hy_in", 12, "k"), ("hy_z", 4, "k"),
    ("fwd0", 4, "k"), ("inv0", 4, "k"), ("fwd1", 4, "k"), ("inv1", 4, "k"),
    ("merge2", 24, "k"), ("out2", 8, "k"),
]
BASE, RUNS = {}, []
_u = 0
_at = {"k": 0, "d": 0, "p": 0}
for _name, _n, _c in SEGMENTS:
    BASE[_name] = _u
    if RUNS and RUNS[-1][1] == _c:
        RUNS[-1][3] += _n
    else:
        RUNS.append([_u, _c, _at[_c], _n])
    _u += _n
    _at[_c] += _n
UNITS = _u

VEC = {}
_v = 0
for _name, _n in [("ffn1_norm", 8), ("mix_norm", 8), ("ffn2_norm", 8), ("ple_norm", 8), ("g_norm", 8),
                  ("q_norm", 1), ("k_norm", 1), ("forget_bias", 1), ("no_bias", 18), ("b_gate", 18),
                  ("w_short", 36), ("b_short", 12), ("g_cq", 3), ("g_ckv", 2),
                  ("g_qn", 1), ("g_qn_swapped", 1), ("g_kn", 1), ("g_kn_swapped", 1),
                  ("b_f1", 1), ("freq_1", 1), ("b_f2", 1), ("freq_2", 1), ("eps", 1)]:
    VEC[_name] = _v
    _v += _n
NVEC = _v



AREA = {0: 0, 1: 512, 3: 896, 2: 1024}
AREA_COLS = 1280


def build(nc, wk, wd, wp, x_in, p_in, vec_in, constf_in, constr_in, sel_in, rope_in, decay_in, pos_in,
          wf1_in, wf2_in, wf3_in, hyb_in, out):
    ctx = ExitStack()

    def sem(name):
        return ctx.enter_context(nc.semaphore(name))

    with ctx:
        def keep(name, shape, dt=F32):
            return ctx.enter_context(nc.sbuf_tensor(name, shape, dt))

        xT = keep("xT", [P, DT, T])
        h_hi = keep("h_hi", [P, DT, T], F32R)
        h_lo = keep("h_lo", [P, DT, T], F32R)
        raw = [keep(f"raw{s}", [P, FH * P]) for s in range(2)]
        whi = [keep(f"whi{s}", [P, FH * P], F32R) for s in range(2)]
        wlo = [keep(f"wlo{s}", [P, FH * P], F32R) for s in range(2)]
        vec = keep("vec", [P, NVEC])
        constf = keep("constf", [P, 4, P])
        constr = keep("constr", [P, 5, P], F32R)
        sumsq = keep("sumsq", [P, T])
        square = keep("square", [P, T])
        std = keep("std", [P, T])
        rstd = keep("rstd", [P, T])
        stage32 = [keep(f"stage32_{i}", [P, T]) for i in range(2)]
        small = keep("small", [P, 32])
        psum = ctx.enter_context(nc.psum_tensor("psum", [P, 8 * 512], F32))
        ident, block_ones, ones, before = (constf[:, i, :] for i in range(4))
        ident_r, neg_tri, neg_ones, mask_qk, mask_kq = (constr[:, i, :] for i in range(5))
        head_sq = [square, sumsq]

        arena = ctx.enter_context(nc.sbuf_tensor("arena_end", [P, 109 * 256], F32))
        arena0 = nc.sbuf_base - 109 * 1024

        def at(kib, name, shape, dt=F32):
            return nc.alloc_sbuf_tensor_at(name, shape, dt, offset=arena0 + int(kib * 1024))

        mid_hi = at(0, "mid_hi", [P, FH, T], F32R)
        mid_lo = at(22, "mid_lo", [P, FH, T], F32R)
        sig = at(44, "sig", [P, T])
        silu = at(46, "silu", [P, T])
        mid32 = at(48, "mid32", [P, T])
        constr32 = at(52, "constr32", [P, 5, P])
        ya_hi = at(0, "ya_hi", [P, 4, T], F32R)
        ya_lo = at(8, "ya_lo", [P, 4, T], F32R)
        yb_hi = at(16, "yb_hi", [P, 4, T], F32R)
        yb_lo = at(24, "yb_lo", [P, 4, T], F32R)
        q_hi = at(32, "q_hi", [P, HEADS, T], F32R)
        q_lo = at(48, "q_lo", [P, HEADS, T], F32R)
        k_hi = at(64, "k_hi", [P, 4, T], F32R)
        k_lo = at(72, "k_lo", [P, 4, T], F32R)
        v32 = at(80, "v32", [P, TT, T])
        prob = at(88, "prob", [P, TT, T])
        probT = [at(96 + 2 * i, f"probT{i}", [P, T]) for i in range(2)]
        nf_hi = at(100, "nf_hi", [P, T], F32R)
        nf_lo = at(102, "nf_lo", [P, T], F32R)
        sel = at(104, "sel", [P, HEADS, P], F32R)
        sel32 = at(80, "sel32", [P, HEADS, P])
        soft = at(88, "soft", [P, AREA_COLS])
        sp_hi = at(93, "sp_hi", [P, AREA_COLS], F32R)
        sp_lo = at(98, "sp_lo", [P, AREA_COLS], F32R)
        weight = at(103, "weight", [P, AREA_COLS])
        merged_hi = at(32, "merged_hi", [P, DT, T], F32R)
        merged_lo = at(48, "merged_lo", [P, DT, T], F32R)
        gate = [at(64 + 4 * i, f"gate{i}", [P, 2, T]) for i in range(2)]
        gated = at(72, "gated", [P, 2, T])
        sum32 = at(76, "sum32", [P, T])
        gate_bias = [at(80 + i, f"gate_bias{i}", [P, 2]) for i in range(2)]
        p32 = at(0, "p32", [P, 2, T])
        p_hi = at(4, "p_hi", [P, 2, T], F32R)
        p_lo = at(8, "p_lo", [P, 2, T], F32R)
        ple_gate = [at(12 + 2 * i, f"ple_gate{i}", [P, T]) for i in range(2)]
        ple_add = at(16, "ple_add", [P, T])
        mq_hi = at(32, "mq_hi", [P, HEADS, T], F32R)
        mq_lo = at(48, "mq_lo", [P, HEADS, T], F32R)
        mk_hi = at(64, "mk_hi", [P, HEADS, T], F32R)
        mk_lo = at(80, "mk_lo", [P, HEADS, T], F32R)
        cq_hi = at(0, "cq_hi", [P, 3, T], F32R)
        cq_lo = at(6, "cq_lo", [P, 3, T], F32R)
        ckv_hi = at(12, "ckv_hi", [P, 2, T], F32R)
        ckv_lo = at(16, "ckv_lo", [P, 2, T], F32R)
        tabs = at(20, "tabs", [P, 4, T])
        krope = at(28, "krope", [P, T])
        lat32 = at(96, "lat32", [P, 3, T])
        ckv32 = at(64, "ckv32", [P, 2, T])
        head32 = [at(96 + 2 * i, f"head32_{i}", [P, T]) for i in range(2)]
        swapped = [at(100 + 6 * i, f"swapped{i}", [P, T]) for i in range(2)]
        rope = at(102, "rope", [P, 2, T])
        mv32 = at(96, "mv32", [P, TT, T])
        mprobT = [at(104 + 2 * i, f"mprobT{i}", [P, T]) for i in range(2)]
        mprob = at(16, "mprob", [P, TT, T])
        y32 = at(24, "y32", [P, 4, T])
        spec = [at(48, "spec0", [P, 8, T]), at(32, "spec1", [P, 8, T])]
        Y_lo = at(48, "Y_lo", [P, 8, T], F32R)
        Y_hi = at(64, "Y_hi", [P, 8, T], F32R)
        kf_hi = at(64, "kf_hi", [P, 8, T], F32R)
        kf_lo = at(80, "kf_lo", [P, 8, T], F32R)
        wf3 = at(16, "wf3", [64, 4 * T])
        decay = at(24, "decay", [P, TT, T])
        hid = [at(96 + 2 * i, f"hid{i}", [64, T]) for i in range(2)]
        posT = at(100, "posT", [33, T])
        wf1 = at(102, "wf1", [33, 64])
        wf2 = at(103, "wf2", [64, 64])
        hyb = at(104, "hyb", [1, 2, T])
        turns = at(108, "turns", [1, 1])
        v_hi, v_lo = yb_hi, yb_lo
        x1tok = at(80, "x1tok", [P, TT, T])
        x2z = at(88, "x2z", [P, TT, T])
        conv = [at(96 + 2 * i, f"conv{i}", [P, T]) for i in range(2)]
        prod = [at(100 + 2 * i, f"prod{i}", [P, T]) for i in range(4)]

        def bank(b, n=512):
            return psum[:, 512 * b:512 * b + n]

        def col(name, i=0, p=P):
            return vec[0:p, VEC[name] + i:VEC[name] + i + 1]

        landed = [sem(f"landed{s}") for s in range(2)]
        hi_ready = sem("hi_ready")
        lo_ready = sem("lo_ready")
        unit_done = sem("unit_done")

        def runs():
            yield from RUNS

        def load_unit(sp, u, k, c, a):
            if not (isinstance(k, int) and u < 2):
                sp.wait_ge(lo_ready, u + k - 1)
            src = {"k": wk, "d": wd, "p": wp}[c]
            w = WIDTH[c]
            row = src[a + k] if isinstance(k, int) else src[bass.ds(a + k, 1)].rearrange("a p n -> (a p) n")
            sp.dma_start(raw[u % 2][:, 0:w], row).then_inc(landed[u % 2], 16)

        def stream_loads(sp):
            for u, c, a, n in runs():
                head = 2 if u < 2 else 0
                with sp.Fori(0, (n - head) // 2) as i:
                    for b in range(2):
                        load_unit(sp, u + head + b, i * 2, c, a + head + b)
                if (n - head) % 2:
                    load_unit(sp, u + n - 1, 0, c, a + n - 1)

        def split_lo(pool, u, k, w):
            pool.wait_ge(hi_ready, u + 1 + k)
            s = u % 2
            pool.tensor_tensor(wlo[s][:, 0:w], raw[s][:, 0:w], whi[s][:, 0:w].bitcast(F32),
                               ALU.subtract).then_inc(lo_ready, 1)

        def stream_lo(pool):
            for u, c, a, n in runs():
                with pool.Fori(0, n // 2) as i:
                    for b in range(2):
                        split_lo(pool, u + b, i * 2, WIDTH[c])
                if n % 2:
                    split_lo(pool, u + n - 1, 0, WIDTH[c])

        class_of = [c for _, n, c in SEGMENTS for _ in range(n)]
        next_hi = [0]

        def split_hi(act, u, k=0):
            s, w = u % 2, WIDTH[class_of[u]]
            act.wait_ge(landed[s], 16 * (u // 2 + 1) + k * 8)
            if not (isinstance(k, int) and u < 2):
                act.wait_ge(unit_done, u - 1 + k)
            act.activation(whi[s][:, 0:w], raw[s][:, 0:w], ACT.Copy).then_inc(hi_ready, 1)

        def split_hi_to(act, u):
            while next_hi[0] < min(u, UNITS):
                split_hi(act, next_hi[0])
                next_hi[0] += 1

        def products(pe, dst, terms, start=True, stop=True, **kw):
            n = len(terms)
            for i, (s_hi, s_lo, m_hi, m_lo) in enumerate(terms):
                pe.matmul(dst, s_hi, m_hi, start=start and i == 0, stop=False, **kw)
                pe.matmul(dst, s_hi, m_lo, start=False, stop=False, **kw)
                last = pe.matmul(dst, s_lo, m_hi, start=False, stop=stop and i == n - 1, **kw)
            return last

        def weight_chunks(u, first, n):
            s = u % 2
            for c in range(first, first + n):
                yield whi[s][:, c * P:(c + 1) * P], wlo[s][:, c * P:(c + 1) * P]

        def linear(pe, dst, u, m_hi, m_lo, n, first=0, chunk_ready=None, ready_base=0, signal=True):
            for c, (a, b) in enumerate(weight_chunks(u, first, n)):
                if chunk_ready is not None:
                    pe.wait_ge(chunk_ready, ready_base + c + 1)
                last = products(pe, dst, [(a, b, m_hi[:, c, :], m_lo[:, c, :])], start=c == 0, stop=c == n - 1)
            if signal:
                last.then_inc(unit_done, 1)

        def linear_by_token(pe, banks, u, j, of, s_hi, s_lo, chunk_ready=None):
            s = u % 2
            if chunk_ready is not None:
                pe.wait_ge(chunk_ready, 2 * j + 2)
            for t, b in enumerate(banks):
                terms = [(s_hi[:, 2 * j + c, t * P:(t + 1) * P], s_lo[:, 2 * j + c, t * P:(t + 1) * P],
                          whi[s][:, c * 512:(c + 1) * 512], wlo[s][:, c * 512:(c + 1) * 512]) for c in range(2)]
                last = products(pe, bank(b), terms, start=j == 0, stop=j == of - 1)
            last.then_inc(unit_done, 1)

        x_landed = sem("x_landed")
        vec_landed = sem("vec_landed")
        const_landed = sem("const_landed")
        constr_landed = sem("constr_landed")
        constr_ready = sem("constr_ready")

        x_updated = sem("x_updated")
        squared = sem("squared")
        summed = sem("summed")
        counts = {"x": 2, "sq": 0, "sum": 0}

        def clear_sum(dve):
            dve.memset(sumsq[:, :], 0.0).then_inc(summed, 1)
            counts["sum"] += 1

        def add_square(dve, x, k=0, i=0):
            dve.wait_ge(summed, counts["sum"] + k)
            dve.tensor_tensor(square[:, :], x, x, ALU.mult).then_inc(squared, 1)
            counts["sq"] += 1
            dve.wait_ge(squared, counts["sq"] + k)
            dve.tensor_tensor(sumsq[:, :], sumsq[:, :], square[:, :], ALU.add).then_inc(summed, 1)
            counts["sum"] += 1

        class Norm:

            signals = [sem(f"norm_{s}") for s in ("mean", "std", "rstd", "f32", "hi", "ready")]
            norms, tiles = 0, 0

            def __init__(self, x, n, gain, hi, lo, total):
                self.x, self.n, self.gain, self.hi, self.lo, self.total = x, n, gain, hi, lo, total
                self.mean, self.std, self.rstd, self.f32, self.hi_made, self.ready = Norm.signals
                self.i, self.base = Norm.norms, Norm.tiles
                Norm.norms, Norm.tiles = Norm.norms + 1, Norm.tiles + n

            def tensor(self, pe):
                pe.wait_ge(summed, self.total)
                pe.matmul(bank(7), ones, sumsq[:, :], start=True, stop=True).then_inc(self.mean, 1)

            def scalar(self, act):
                act.wait_ge(self.mean, self.i + 1)
                act.activation(std[:, :], bank(7), ACT.Sqrt, scale=1.0 / (self.n * P),
                               bias=col("eps")).then_inc(self.std, 1)
                for k in range(self.n):
                    act.wait_ge(self.f32, self.base + k + 1)
                    act.activation(self.hi[:, k, :], stage32[k % 2][:, :], ACT.Copy).then_inc(self.hi_made, 1)

            def vector(self, dve):
                dve.wait_ge(self.std, self.i + 1)
                dve.reciprocal(rstd[:, :], std[:, :]).then_inc(self.rstd, 1)
                dve.wait_ge(self.rstd, self.i + 1)
                for k in range(self.n + 1):
                    if k < self.n:
                        if k > 1:
                            dve.wait_ge(self.ready, self.base + k - 1)
                        dve.scalar_tensor_tensor(stage32[k % 2][:, :], self.x[:, k, :], col(self.gain, k),
                                                 rstd[:, :], ALU.mult, ALU.mult).then_inc(self.f32, 1)
                    if k:
                        dve.wait_ge(self.hi_made, self.base + k)
                        dve.tensor_tensor(self.lo[:, k - 1, :], stage32[(k - 1) % 2][:, :],
                                          self.hi[:, k - 1, :].bitcast(F32), ALU.subtract).then_inc(self.ready, 1)

        def update_x(dve, unit, o, k, b, scale, squares, src=None, x_at=None):
            dve.wait_ge(unit_done, unit + 1 + k)
            x = xT[:, o, :] if isinstance(k, int) else xT[:, bass.ds(o + k, 1), :].rearrange("p a t -> p (a t)")
            dve.scalar_tensor_tensor(x, bank(b), scale, x, ALU.mult, ALU.add).then_inc(x_updated, 1)
            counts["x"] += 1
            if squares:
                dve.wait_ge(x_updated, counts["x"] + k)
                add_square(dve, x, k)

        def update_loop(dve, base, banks, scale, squares):
            if squares:
                clear_sum(dve)
            dve.wait_ge(x_updated, counts["x"])
            c0 = dict(counts)
            with dve.Fori(0, DT // 2) as i:
                for b in range(2):
                    update_x(dve, base + b, b, i * 2, banks[b], scale, squares)
            done = dict(c0)
            done["x"] += DT
            if squares:
                done["sq"] += DT
                done["sum"] += DT
            counts.update(done)

        SUMS = {"ffn1": 9, "mix": 18, "ffn2": 27, "ple": 36, "block2": 45}
        XS = {"ffn1_0": 2, "out1": 18, "ffn2_0": 26, "ple": 42, "out2": 50}

        class FeedForward:
            signals = [sem(f"ffn_{s}") for s in ("sigmoid", "silu", "mid", "mid_hi", "mid_ready")]

            def __init__(self, number, norm, x_base):
                self.name, self.norm, self.x_base = f"ffn{number}", norm, x_base
                self.first = 2 * FH * (number - 1)
                self.sig, self.silu, self.mid, self.mid_hi, self.ready = FeedForward.signals

            def tensor(self, pe):
                for half in range(2):
                    up, down, f0 = BASE[f"{self.name}_up{half}"], BASE[f"{self.name}_down{half}"], self.first + half * FH

                    def hidden_tile(f, k, chunk_ready):
                        pe.wait_ge(lo_ready, up + 2 * f + 1 + k * 2)
                        if f0 + f > 0:
                            pe.wait_ge(self.silu, f0 + f + k)
                        linear(pe, bank(0), up, h_hi, h_lo, DT, chunk_ready=chunk_ready,
                               ready_base=self.norm.base)
                        pe.wait_ge(lo_ready, up + 2 * f + 2 + k * 2)
                        if f0 + f > 0:
                            pe.wait_ge(self.mid, f0 + f + k)
                        linear(pe, bank(1), up + 1, h_hi, h_lo, DT)

                    hidden_tile(0, 0, self.norm.ready if half == 0 else None)
                    with pe.Fori(0, FH - 1) as i:
                        hidden_tile(1, i, None)
                    with pe.Fori(0, DT // 2) as i:
                        for b in range(2):
                            pe.wait_ge(lo_ready, down + b + 1 + i * 2)
                            pe.wait_ge(self.ready, f0 + FH)
                            pe.wait_ge(x_updated, self.x_base + 8 * half + b - 1 + i * 2)
                            linear(pe, bank(2 + b), down + b, mid_hi, mid_lo, FH)

            def scalar(self, act):
                for half in range(2):
                    up, f0 = BASE[f"{self.name}_up{half}"], self.first + half * FH

                    def sigmoid(f, k):
                        act.wait_ge(unit_done, up + 2 * f + 1 + k * 2)
                        act.activation(sig[:, :], bank(0), ACT.Sigmoid).then_inc(self.sig, 1)

                    split_hi_to(act, up + 2)
                    sigmoid(0, 0)
                    with act.Fori(0, FH - 1) as i:
                        split_hi(act, up + 2, i * 2)
                        split_hi(act, up + 3, i * 2)
                        sigmoid(1, i)
                    next_hi[0] = up + 2 * FH
                    split_hi_to(act, up + 2 * FH + DT)

            def vector(self, dve):
                for half in range(2):
                    up, f0 = BASE[f"{self.name}_up{half}"], self.first + half * FH
                    if half:
                        dve.wait_ge(unit_done, up)
                    with dve.Fori(0, FH) as i:
                        dve.wait_ge(self.sig, f0 + 1 + i)
                        dve.tensor_tensor(silu[:, :], sig[:, :], bank(0), ALU.mult).then_inc(self.silu, 1)
                        dve.wait_ge(unit_done, up + 2 + i * 2)
                        dve.wait_ge(self.silu, f0 + 1 + i)
                        dve.tensor_tensor(mid32[:, :], silu[:, :], bank(1), ALU.mult).then_inc(self.mid, 1)
                        hi = mid_hi[:, bass.ds(i, 1), :].rearrange("p a t -> p (a t)")
                        lo = mid_lo[:, bass.ds(i, 1), :].rearrange("p a t -> p (a t)")
                        dve.wait_ge(self.mid, f0 + 1 + i)
                        dve.tensor_copy(hi, mid32[:, :]).then_inc(self.mid_hi, 1)
                        dve.wait_ge(self.mid_hi, f0 + 1 + i)
                        dve.tensor_tensor(lo, mid32[:, :], hi.bitcast(F32), ALU.subtract).then_inc(self.ready, 1)
                        dve.wait_ge(self.ready, f0 + 1 + i)
                    update_loop(dve, BASE[f"{self.name}_down{half}"], (2, 3), 0.5, half == 1)

        norm_ffn1 = Norm(xT, DT, "ffn1_norm", h_hi, h_lo, SUMS["ffn1"])
        ffn1 = FeedForward(1, norm_ffn1, XS["ffn1_0"])
        norm_mix = Norm(xT, DT, "mix_norm", h_hi, h_lo, SUMS["mix"])

        class SoftmaxAttention:

            def __init__(self, name, q, k, v, prob, probT, scale, causal, extra):
                self.q, self.k, self.v, self.prob, self.probT = q, k, v, prob, probT
                self.scale, self.causal, self.extra = scale, causal, extra
                (self.scores, self.maxed, self.neg, self.exped, self.inv, self.normed, self.turned, self.copied0,
                 self.copied1, self.summed, self.out_hi, self.out) = (
                    sem(f"{name}_{x}") for x in ("scores", "maximum", "negated", "exped", "inverse", "normed",
                                                 "transposed", "copied_even", "copied_odd", "outputs", "out_hi", "out"))

            def keys(self, t):
                return (t + 1) * P if self.causal else T

            def queries(self, s):
                return s * P if self.causal else 0

            def tensor_scores(self, pe, h):
                for t in range(TT):
                    n = self.keys(t)
                    if h:
                        pe.wait_ge(self.exped, TT * (h - 1) + t + 1)
                    (qh, ql), (kh, kl) = self.q(h), self.k(h)
                    rows = slice(t * P, (t + 1) * P)
                    last = products(pe, bank(t, n), [(qh[:, rows], ql[:, rows], kh[:, 0:n], kl[:, 0:n])],
                                    stop=not self.extra)
                    if self.extra:
                        pe.matmul(bank(t, n), sel[:, h, :], nf_hi[:, 0:n], start=False, stop=False)
                        pe.matmul(bank(t, n), sel[:, h, :], nf_lo[:, 0:n], start=False, stop=False)
                        last = pe.matmul(psum[:, 512 * t + t * P:512 * t + n], ident_r, mask_qk, start=False, stop=True)
                    last.then_inc(self.scores, 1)

            def tensor_outputs(self, pe, h):
                pe.wait_ge(self.normed, TT * (h + 1))
                for s in range(TT + 1):
                    if s < TT:
                        n = TT * h + s
                        if n >= 2:
                            pe.wait_ge((self.copied0, self.copied1)[s % 2], n // 2)
                        t0 = s if self.causal else 0
                        for t in range(t0, TT):
                            last = pe.transpose(psum[:, 512 * (4 + s % 2) + t * P:512 * (4 + s % 2) + (t + 1) * P],
                                                self.prob[:, t, s * P:(s + 1) * P], ident)
                        last.then_inc(self.turned, 1)
                    if s:
                        r = s - 1
                        pe.wait_ge((self.copied0, self.copied1)[r % 2], 2 * h + r // 2 + 1)
                        if r == 0 and h >= 2:
                            pe.wait_ge(self.out, h - 1)
                        a = self.queries(r)
                        pe.matmul(psum[:, 512 * (6 + h % 2) + a:512 * (7 + h % 2)], self.v(h, r),
                                  self.probT[r % 2][:, a:T], start=r == 0, stop=r == TT - 1,
                                  ).then_inc(self.summed, 1)

            def tensor(self, pe, ready=()):
                for semaphore, value in ready:
                    pe.wait_ge(semaphore, value)
                self.tensor_scores(pe, 0)
                for h in range(HEADS):
                    if h + 1 < HEADS:
                        self.tensor_scores(pe, h + 1)
                    self.tensor_outputs(pe, h)

            def cols(self, h, what):
                a = 12 * (h % 2) + 4 * what
                return small[:, a:a + 4]

            def scalar(self, act):
                for h in range(HEADS):
                    act.wait_ge(self.neg, h + 1)
                    if h:
                        act.wait_ge(self.turned, TT * h)
                    for t in range(TT):
                        n = self.keys(t)
                        act.activation(self.prob[:, t, 0:n], bank(t, n), ACT.Exp, scale=self.scale,
                                       bias=self.cols(h, 0)[:, t:t + 1],
                                       accum_out=self.cols(h, 1)[:, t:t + 1]).then_inc(self.exped, 1)
                    self.scalar_outputs(act, h)

            def copy_transpose(self, eng, h, s):
                n = TT * h + s
                eng.wait_ge(self.turned, n + 1)
                if n >= 2:
                    eng.wait_ge(self.summed, n - 1)
                a = self.queries(s)
                src, dst = psum[:, 512 * (4 + s % 2) + a:512 * (5 + s % 2)], self.probT[s % 2][:, a:T]
                if s % 2 == 0:
                    eng.activation(dst, src, ACT.Copy).then_inc(self.copied0, 1)
                else:
                    eng.tensor_copy(dst, src).then_inc(self.copied1, 1)

            def scalar_outputs(self, act, h):
                for s in (0, 2):
                    self.copy_transpose(act, h, s)
                act.wait_ge(self.summed, TT * (h + 1))
                rows = slice(HD * (h % 2), HD * (h % 2) + HD)
                src = bank(6 + h % 2)[rows, :]
                if self.extra:
                    act.activation(ya_hi[rows, h // 2, :], src, ACT.Copy).then_inc(self.out_hi, 1)
                else:
                    act.activation(y32[rows, h // 2, :], src, ACT.Copy).then_inc(self.out, 1)

            def vector(self, dve):
                for h in range(HEADS):
                    top, total, inverse = (self.cols(h, i) for i in range(3))
                    if h >= 2:
                        dve.wait_ge(self.exped, TT * (h - 1))
                    for t in range(TT):
                        n = self.keys(t)
                        dve.wait_ge(self.scores, TT * h + t + 1)
                        dve.tensor_reduce(top[:, t:t + 1], bank(t, n), AXX, ALU.max).then_inc(self.maxed, 1)
                    dve.wait_ge(self.maxed, TT * (h + 1))
                    dve.tensor_scalar(top, top, -self.scale, None, ALU.mult).then_inc(self.neg, 1)
                    if h:
                        self.vector_outputs(dve, h - 1)
                    dve.wait_ge(self.exped, TT * (h + 1))
                    dve.reciprocal(inverse, total).then_inc(self.inv, 1)
                    dve.wait_ge(self.inv, h + 1)
                    for t in range(TT):
                        row = self.prob[:, t, 0:self.keys(t)]
                        dve.tensor_scalar(row, row, inverse[:, t:t + 1], None, ALU.mult).then_inc(self.normed, 1)
                    self.copy_transpose(dve, h, 1)
                    self.copy_transpose(dve, h, 3)
                self.vector_outputs(dve, HEADS - 1)

            def vector_outputs(self, dve, h):
                if self.extra:
                    rows = slice(HD * (h % 2), HD * (h % 2) + HD)
                    dve.wait_ge(self.out_hi, h + 1)
                    dve.tensor_tensor(ya_lo[rows, h // 2, :], bank(6 + h % 2)[rows, :],
                                      ya_hi[rows, h // 2, :].bitcast(F32), ALU.subtract).then_inc(self.out, 1)

        fox = SoftmaxAttention("fox", lambda h: (q_hi[:, h, :], q_lo[:, h, :]),
                               lambda h: (k_hi[:, h // 2, :], k_lo[:, h // 2, :]),
                               lambda h, s: v32[:, s, (h // 2) * P:(h // 2 + 1) * P],
                               prob, probT, 1.0, True, True)

        class FoxProjections:

            def __init__(self):
                (self.sq, self.sum, self.std, self.rstd, self.f32, self.hi, self.ready, self.cleared, self.sel_landed,
                 self.sel, self.z, self.az, self.e, self.l, self.log, self.F, self.nf_hi, self.nf, self.v) = (
                    sem(f"fox_{x}") for x in ("square", "head_sum", "std", "rstd", "f32", "hi", "qk_ready", "cleared",
                                              "sel_landed", "sel", "z", "abs", "exp", "ln", "log", "F", "nf_hi",
                                              "nf", "v"))

            def tensor(self, pe, norm):
                for j in range(9):
                    if j < 8:
                        u = BASE["fox_q"] + j
                        pe.wait_ge(lo_ready, u + 1)
                        if j >= 4:
                            pe.wait_ge(self.f32, j - 3)
                        linear(pe, bank(j % 4), u, h_hi, h_lo, DT, chunk_ready=norm.ready if j == 0 else None,
                               ready_base=norm.base)
                    if j:
                        pe.wait_ge(self.sq, j)
                        if j > 2:
                            pe.wait_ge(self.std, j - 2)
                        pe.matmul(bank(4 + (j - 1) % 2), block_ones, head_sq[(j - 1) % 2][:, :], start=True,
                                  stop=True).then_inc(self.sum, 1)
                u = BASE["fox_f"]
                pe.wait_ge(lo_ready, u + 1)
                linear(pe, bank(6), u, h_hi, h_lo, DT)
                pe.wait_ge(self.std, 8)
                pe.wait_ge(self.z, 1)
                for j in range(4):
                    pe.wait_ge(lo_ready, BASE["fox_v"] + j + 1)
                    linear_by_token(pe, (4, 5, 7, 6), BASE["fox_v"] + j, j, 4, h_hi, h_lo)

            def scalar(self, act):
                act.wait_ge(self.sel_landed, 16)
                act.activation(sel[:, :, :], sel32[:, :, :], ACT.Copy).then_inc(self.sel, 1)
                for j in range(9):
                    if j < 8:
                        u = BASE["fox_q"] + j
                        split_hi_to(act, u + 2)
                        act.wait_ge(unit_done, u + 1)
                        if j >= 2:
                            act.wait_ge(self.sum, j - 1)
                        act.activation(head_sq[j % 2][:, :], bank(j % 4), ACT.Square).then_inc(self.sq, 1)
                    if j:
                        i = j - 1
                        act.wait_ge(self.sum, i + 1)
                        if i:
                            act.wait_ge(self.rstd, i)
                        act.activation(std[:, :], bank(4 + i % 2), ACT.Sqrt, scale=1.0 / HD,
                                       bias=col("eps")).then_inc(self.std, 1)
                        act.wait_ge(self.f32, i + 1)
                        src = stage32[i % 2]
                        if i < 4:
                            act.wait_ge(self.cleared, 4)
                            act.activation(q_hi[0:HD, 2 * i, :], src[0:HD, :], ACT.Copy).then_inc(self.hi, 1)
                            act.activation(q_hi[HD:P, 2 * i + 1, :], src[HD:P, :], ACT.Copy).then_inc(self.hi, 1)
                        else:
                            act.activation(k_hi[:, i - 4, :], src[:, :], ACT.Copy).then_inc(self.hi, 1)
                u = BASE["fox_f"]
                split_hi_to(act, u + 2)
                act.wait_ge(self.z, 1)
                act.activation(prob[:, 1, :], prob[:, 0, :], ACT.Abs).then_inc(self.az, 1)
                act.wait_ge(self.az, 1)
                act.activation(prob[:, 2, :], prob[:, 1, :], ACT.Exp, scale=-1.0).then_inc(self.e, 1)
                act.wait_ge(self.e, 1)
                act.activation(prob[:, 3, :], prob[:, 2, :], ACT.Ln, bias=1.0).then_inc(self.l, 1)
                split_hi_to(act, BASE["fox_v"] + 4)
                act.wait_ge(unit_done, BASE["fox_v"] + 4)
                act.wait_ge(self.sel, 1)
                for t, b in enumerate((4, 5, 7, 6)):
                    act.activation(v32[:, t, :], bank(b), ACT.Copy).then_inc(self.v, 1)
                split_hi_to(act, BASE["fox_v"] + 6)

            def vector(self, dve):
                for i, q in enumerate((q_hi, q_lo)):
                    even = q[HD:P, :, :].rearrange("p (j e) t -> p j e t", e=2)[:, :, 0, :]
                    odd = q[0:HD, :, :].rearrange("p (j e) t -> p j e t", e=2)[:, :, 1, :]
                    for half in (even, odd):
                        dve.memset(half.bitcast(F32), 0.0).then_inc(self.cleared, 1)
                dve.tensor_scalar(small[:, 31:32], col("q_norm"), HD ** -0.5, None, ALU.mult).then_inc(self.cleared, 1)
                for i in range(8):
                    dve.wait_ge(self.std, i + 1)
                    dve.reciprocal(rstd[:, :], std[:, :]).then_inc(self.rstd, 1)
                    dve.wait_ge(self.rstd, i + 1)
                    if i == 0:
                        dve.wait_ge(self.cleared, 5)
                    gain = small[:, 31:32] if i < 4 else col("k_norm")
                    dve.scalar_tensor_tensor(stage32[i % 2][:, :], bank(i % 4), gain, rstd[:, :],
                                             ALU.mult, ALU.mult).then_inc(self.f32, 1)
                    src = stage32[i % 2]
                    if i < 4:
                        dve.wait_ge(self.hi, 2 * i + 2)
                        for e, rows in enumerate((slice(0, HD), slice(HD, P))):
                            dve.tensor_tensor(q_lo[rows, 2 * i + e, :], src[rows, :],
                                              q_hi[rows, 2 * i + e, :].bitcast(F32), ALU.subtract).then_inc(self.ready, 1)
                        dve.wait_ge(self.ready, 2 * i + 2)
                    else:
                        dve.wait_ge(self.hi, 8 + i - 3)
                        dve.tensor_tensor(k_lo[:, i - 4, :], src[:, :], k_hi[:, i - 4, :].bitcast(F32),
                                          ALU.subtract).then_inc(self.ready, 1)
                        dve.wait_ge(self.ready, 8 + i - 3)
                dve.wait_ge(unit_done, BASE["fox_f"] + 1)
                dve.tensor_scalar(prob[:, 0, :], bank(6), col("forget_bias"), None, ALU.add).then_inc(self.z, 1)
                dve.wait_ge(self.z, 1)
                dve.wait_ge(self.l, 1)
                dve.scalar_tensor_tensor(probT[0][:, :], prob[:, 0, :], 0.0, prob[:, 3, :], ALU.min,
                                         ALU.subtract).then_inc(self.log, 1)
                dve.memset(prob[:, 1, :], 1.0).then_inc(self.log, 1)
                dve.wait_ge(self.log, 2)
                dve.tensor_tensor_scan(probT[1][:, :], prob[:, 1, :], probT[0][:, :], 0.0, ALU.mult,
                                       ALU.add).then_inc(self.F, 1)
                dve.wait_ge(self.F, 1)
                dve.tensor_scalar(nf_hi[:, :], probT[1][:, :], -1.0, None, ALU.mult).then_inc(self.nf_hi, 1)
                dve.wait_ge(self.nf_hi, 1)
                dve.scalar_tensor_tensor(nf_lo[:, :], probT[1][:, :], -1.0, nf_hi[:, :].bitcast(F32), ALU.mult,
                                         ALU.subtract).then_inc(self.nf, 1)
                dve.wait_ge(self.nf, 1)

        foxp = FoxProjections()

        class StickProjections:

            def __init__(self):
                self.hi, self.ready, self.v = (sem(f"stick_{x}") for x in ("hi", "qk_ready", "v"))

            def tensor(self, pe):
                for j in range(8):
                    u = BASE["sb_q"] + j
                    pe.wait_ge(lo_ready, u + 1)
                    pe.wait_ge(*((fox.exped, TT * HEADS) if j < 4 else (self.ready, 2 * (j - 3))))
                    linear(pe, bank(j % 4), u, h_hi, h_lo, DT)
                pe.wait_ge(fox.out, HEADS)
                for j in range(4):
                    pe.wait_ge(lo_ready, BASE["sb_v"] + j + 1)
                    linear_by_token(pe, (4, 5, 6, 7), BASE["sb_v"] + j, j, 4, h_hi, h_lo)

            def scalar(self, act):
                for j in range(8):
                    u = BASE["sb_q"] + j
                    split_hi_to(act, u + 2)
                    act.wait_ge(unit_done, u + 1)
                    if j < 4:
                        act.activation(q_hi[0:HD, 2 * j, :], bank(j)[0:HD, :], ACT.Copy,
                                       scale=HD ** -0.5).then_inc(self.hi, 1)
                        act.activation(q_hi[HD:P, 2 * j + 1, :], bank(j)[HD:P, :], ACT.Copy,
                                       scale=HD ** -0.5).then_inc(self.hi, 1)
                    else:
                        act.activation(k_hi[:, j - 4, :], bank(j % 4), ACT.Copy).then_inc(self.hi, 1)
                split_hi_to(act, BASE["sb_v"] + 4)
                act.wait_ge(unit_done, BASE["sb_v"] + 4)
                for t in range(TT):
                    act.activation(v32[:, t, :], bank(4 + t), ACT.Copy).then_inc(self.v, 1)
                split_hi_to(act, BASE["sb_v"] + 6)

            def vector(self, dve):
                for j in range(4):
                    dve.wait_ge(self.hi, 2 * j + 2)
                    for e, rows in enumerate((slice(0, HD), slice(HD, P))):
                        dve.scalar_tensor_tensor(q_lo[rows, 2 * j + e, :], bank(j)[rows, :], HD ** -0.5,
                                                 q_hi[rows, 2 * j + e, :].bitcast(F32), ALU.mult,
                                                 ALU.subtract).then_inc(self.ready, 1)
                for j in range(4):
                    dve.wait_ge(self.hi, 9 + j)
                    dve.tensor_tensor(k_lo[:, j, :], bank(j), k_hi[:, j, :].bitcast(F32),
                                      ALU.subtract).then_inc(self.ready, 1)

        stickp = StickProjections()

        class StickBreaking:

            def __init__(self):
                (self.z, self.az, self.e, self.l, self.sp, self.masked, self.hi, self.ready, self.sums, self.weight,
                 self.outputs, self.out_hi, self.out) = (
                    sem(f"stick_{x}") for x in ("z", "abs", "exp", "ln", "softplus", "masked", "sp_hi", "sp_ready",
                                                "sums", "weight", "outputs", "out_hi", "out"))

            def zone(self, h, s, a=0, n=None):
                o = 512 * 3 * (h % 2) + AREA[s] + a
                return psum[:, o:o + (T - s * P - a if n is None else n)]

            def whole(self, h):
                return psum[:, 512 * 3 * (h % 2):512 * 3 * (h % 2) + AREA_COLS]

            def tensor_z(self, pe, h):
                if h >= 2:
                    pe.wait_ge(self.weight, h - 1)
                for s in range(TT):
                    keys = slice(s * P, (s + 1) * P)
                    last = products(pe, self.zone(h, s), [(k_hi[:, h // 2, keys], k_lo[:, h // 2, keys],
                                                           q_hi[:, h, s * P:T], q_lo[:, h, s * P:T])],
                                    start=s != 3, stop=True, skip_group_check=True)
                last.then_inc(self.z, 1)

            def tensor_sums(self, pe, h):
                pe.wait_ge(self.ready, h + 1)
                for s in range(TT):
                    for j in range(s, TT):
                        tri = neg_tri if j == s else neg_ones
                        for sp in (sp_hi, sp_lo):
                            pe.matmul(self.zone(h, s, (j - s) * P), tri, sp[:, AREA[j]:AREA[j] + T - j * P],
                                      start=False, stop=False, skip_group_check=True)
                    last = pe.matmul(self.zone(h, s, 0, P), ident_r, mask_kq, start=False, stop=True,
                                     skip_group_check=True)
                last.then_inc(self.sums, 1)

            def tensor_outputs(self, pe, h):
                pe.wait_ge(self.weight, h + 1)
                if h >= 2:
                    pe.wait_ge(self.out, h - 1)
                for s in range(TT):
                    last = pe.matmul(psum[:, 512 * (6 + h % 2) + s * P:512 * (7 + h % 2)],
                                     v32[:, s, (h // 2) * P:(h // 2 + 1) * P],
                                     weight[:, AREA[s]:AREA[s] + T - s * P], start=s == 0, stop=s == TT - 1)
                last.then_inc(self.outputs, 1)

            def tensor(self, pe):
                pe.wait_ge(stickp.ready, 12)
                pe.wait_ge(stickp.v, TT)
                self.tensor_z(pe, 0)
                for h in range(HEADS):
                    if h + 1 < HEADS:
                        self.tensor_z(pe, h + 1)
                    if h:
                        self.tensor_outputs(pe, h - 1)
                    self.tensor_sums(pe, h)
                self.tensor_outputs(pe, HEADS - 1)

            def scalar_weight(self, act, h):
                act.wait_ge(self.sums, h + 1)
                if h:
                    act.wait_ge(self.outputs, h)
                act.activation(weight[:, :], self.whole(h), ACT.Exp).then_inc(self.weight, 1)

            def scalar_output(self, act, h):
                act.wait_ge(self.outputs, h + 1)
                rows = slice(HD * (h % 2), HD * (h % 2) + HD)
                act.activation(yb_hi[rows, h // 2, :], bank(6 + h % 2)[rows, :], ACT.Copy).then_inc(self.out_hi, 1)

            def scalar(self, act):
                for h in range(HEADS):
                    act.wait_ge(self.z, h + 1)
                    if h:
                        act.wait_ge(self.ready, h)
                    act.activation(soft[:, :], self.whole(h), ACT.Abs).then_inc(self.az, 1)
                    act.wait_ge(self.az, h + 1)
                    act.activation(soft[:, :], soft[:, :], ACT.Exp, scale=-1.0).then_inc(self.e, 1)
                    act.wait_ge(self.e, h + 1)
                    act.activation(soft[:, :], soft[:, :], ACT.Ln, bias=1.0).then_inc(self.l, 1)
                    if h:
                        self.scalar_weight(act, h - 1)
                    if h:
                        self.scalar_output(act, h - 1)
                self.scalar_weight(act, HEADS - 1)
                self.scalar_output(act, HEADS - 1)

            def vector_output(self, dve, h):
                dve.wait_ge(self.out_hi, h + 1)
                rows = slice(HD * (h % 2), HD * (h % 2) + HD)
                dve.tensor_tensor(yb_lo[rows, h // 2, :], bank(6 + h % 2)[rows, :],
                                  yb_hi[rows, h // 2, :].bitcast(F32), ALU.subtract).then_inc(self.out, 1)

            def vector(self, dve):
                for h in range(HEADS):
                    dve.wait_ge(self.l, h + 1)
                    dve.scalar_tensor_tensor(soft[:, :], self.whole(h), 0.0, soft[:, :], ALU.max,
                                             ALU.add).then_inc(self.sp, 1)
                    dve.wait_ge(self.sp, h + 1)
                    for s in range(TT):
                        diagonal = soft[:, AREA[s]:AREA[s] + P]
                        dve.tensor_tensor(diagonal, diagonal, before, ALU.mult).then_inc(self.masked, 1)
                    dve.wait_ge(self.masked, 4 * h + 4)
                    if h:
                        dve.wait_ge(self.sums, h)
                    dve.tensor_copy(sp_hi[:, :], soft[:, :]).then_inc(self.hi, 1)
                    dve.wait_ge(self.hi, h + 1)
                    dve.tensor_tensor(sp_lo[:, :], soft[:, :], sp_hi[:, :].bitcast(F32),
                                      ALU.subtract).then_inc(self.ready, 1)
                    if h:
                        self.vector_output(dve, h - 1)
                self.vector_output(dve, HEADS - 1)

        stick = StickBreaking()

        class Merge:

            signals = [sem(f"merge_{x}") for x in ("opened", "gate", "part", "sum", "hi", "ready")]

            def __init__(self, n, bias, x_base, before, squares):
                self.base, self.out_base = BASE[f"merge{n}"], BASE[f"out{n}"]
                self.bias, self.x_base, self.before, self.squares = bias, x_base, before, squares
                self.first = DT * (n - 1)
                self.opened, self.gate, self.part, self.sum, self.hi, self.ready = Merge.signals

            def tensor(self, pe):
                for s, v in self.before:
                    pe.wait_ge(s, v)
                with pe.Fori(0, DT // 2) as i:
                    for b in range(2):
                        u = self.base + 3 * b
                        pe.wait_ge(self.opened, self.first // DT * (DT + 2) + b + 1 + i * 2)
                        for g in range(2):
                            pe.wait_ge(lo_ready, u + g + 1 + i * 6)
                            linear(pe, bank(4 * b + g), u + g, h_hi, h_lo, DT)
                        pe.wait_ge(lo_ready, u + 3 + i * 6)
                        linear(pe, bank(4 * b + 2), u + 2, ya_hi, ya_lo, 4, signal=False)
                        linear(pe, bank(4 * b + 3), u + 2, yb_hi, yb_lo, 4, first=4)
                with pe.Fori(0, DT // 2) as i:
                    for b in range(2):
                        pe.wait_ge(lo_ready, self.out_base + b + 1 + i * 2)
                        pe.wait_ge(self.ready, self.first + DT)
                        pe.wait_ge(x_updated, self.x_base + b - 1 + i * 2)
                        linear(pe, bank(b), self.out_base + b, merged_hi, merged_lo, DT)

            def scalar(self, act):
                split_hi_to(act, self.base + 2)
                with act.Fori(0, DT // 2) as i:
                    for b in range(2):
                        u = self.base + 3 * b
                        for g in range(2):
                            act.wait_ge(unit_done, u + g + 1 + i * 6)
                            act.activation(gate[b][:, g, :], bank(4 * b + g), ACT.Sigmoid,
                                           bias=gate_bias[b][:, g:g + 1]).then_inc(self.gate, 1)
                            split_hi(act, u + g + 2, i * 6)
                        split_hi(act, u + 4, i * 6)
                next_hi[0] = self.base + 26
                split_hi_to(act, self.out_base + DT)

            def open_tile(self, dve, b, o, k):
                c = VEC[self.bias] + 2 * o
                src = vec[:, c:c + 2] if isinstance(k, int) else vec[:, bass.ds(c + k * 2, 2)]
                dve.tensor_copy(gate_bias[b][:, :], src).then_inc(self.opened, 1)

            def vector(self, dve):
                for b in range(2):
                    self.open_tile(dve, b, b, 0)
                with dve.Fori(0, DT // 2) as i:
                    for b in range(2):
                        u = self.base + 3 * b
                        dve.wait_ge(unit_done, u + 3 + i * 6)
                        dve.wait_ge(self.gate, 2 * self.first + 2 * b + 2 + i * 4)
                        for g in range(2):
                            dve.tensor_tensor(gated[:, g, :], gate[b][:, g, :], bank(4 * b + 2 + g),
                                              ALU.mult).then_inc(self.part, 1)
                        dve.wait_ge(self.part, 2 * self.first + 2 * b + 2 + i * 4)
                        dve.tensor_tensor(sum32[:, :], gated[:, 0, :], gated[:, 1, :], ALU.add).then_inc(self.sum, 1)
                        dve.wait_ge(self.sum, self.first + b + 1 + i * 2)
                        hi = merged_hi[:, bass.ds(i * 2 + b, 1), :].rearrange("p a t -> p (a t)")
                        lo = merged_lo[:, bass.ds(i * 2 + b, 1), :].rearrange("p a t -> p (a t)")
                        dve.tensor_copy(hi, sum32[:, :]).then_inc(self.hi, 1)
                        dve.wait_ge(self.hi, self.first + b + 1 + i * 2)
                        dve.tensor_tensor(lo, sum32[:, :], hi.bitcast(F32), ALU.subtract).then_inc(self.ready, 1)
                        dve.wait_ge(self.ready, self.first + b + 1 + i * 2)
                        self.open_tile(dve, b, b + 2, i * 2)
                update_loop(dve, self.out_base, (0, 1), 1.0, self.squares)

        merge1 = Merge(1, "no_bias", XS["out1"], [(fox.out, HEADS), (stick.out, HEADS)], True)
        norm_ffn2 = Norm(xT, DT, "ffn2_norm", h_hi, h_lo, SUMS["ffn2"])
        ffn2 = FeedForward(2, norm_ffn2, XS["ffn2_0"])


        class LayerEmbedding:

            def __init__(self, norm, x_base):
                self.norm, self.x_base, self.base = norm, x_base, BASE["ple"]
                self.landed, self.hi, self.p_ready, self.sig, self.add = (
                    sem(f"ple_{x}") for x in ("landed", "p_hi", "p_ready", "sigmoid", "add"))

            def tensor(self, pe):
                for k in range(DT):
                    pe.wait_ge(self.norm.ready, self.norm.base + k + 1)
                pe.wait_ge(self.p_ready, 1)
                with pe.Fori(0, DT // 2) as i:
                    for b in range(2):
                        pe.wait_ge(lo_ready, self.base + b + 1 + i * 2)
                        pe.wait_ge(x_updated, self.x_base + b - 1 + i * 2)
                        linear(pe, bank(b), self.base + b, h_hi, h_lo, DT, signal=False)
                        linear(pe, bank(2 + b), self.base + b, p_hi, p_lo, 2, first=DT)

            def load(self, act):
                act.wait_ge(unit_done, self.base)
                act.dma_start(p32[:, :, :], p_in).then_inc(self.landed, 16)

            def scalar(self, act):
                act.wait_ge(self.landed, 16)
                act.activation(p_hi[:, :, :], p32[:, :, :], ACT.Copy).then_inc(self.hi, 1)

                def sigmoid(b, k):
                    act.wait_ge(unit_done, self.base + b + 1 + k)
                    act.activation(ple_gate[b][:, :], bank(b), ACT.Sigmoid).then_inc(self.sig, 1)

                with act.Fori(0, DT // 2 - 1) as i:
                    for b in range(2):
                        sigmoid(b, i * 2)
                        split_hi(act, self.base + 2 + b, i * 2)
                next_hi[0] = self.base + DT
                for b in range(2):
                    sigmoid(b, DT - 2)

            def vector(self, dve):
                dve.wait_ge(self.hi, 1)
                dve.tensor_tensor(p_lo[:, :, :], p32[:, :, :], p_hi[:, :, :].bitcast(F32),
                                  ALU.subtract).then_inc(self.p_ready, 1)
                clear_sum(dve)
                dve.wait_ge(x_updated, counts["x"])
                c0 = dict(counts)
                with dve.Fori(0, DT // 2) as i:
                    for b in range(2):
                        dve.wait_ge(unit_done, self.base + b + 1 + i * 2)
                        dve.wait_ge(self.sig, b + 1 + i * 2)
                        dve.tensor_tensor(ple_add[:, :], ple_gate[b][:, :], bank(2 + b), ALU.mult).then_inc(self.add, 1)
                        dve.wait_ge(self.add, b + 1 + i * 2)
                        x = xT[:, bass.ds(i * 2 + b, 1), :].rearrange("p a t -> p (a t)")
                        dve.tensor_tensor(x, x, ple_add[:, :], ALU.add).then_inc(x_updated, 1)
                        counts["x"] += 1
                        dve.wait_ge(x_updated, counts["x"] + i * 2)
                        add_square(dve, x, i * 2)
                counts.update({"x": c0["x"] + DT, "sq": c0["sq"] + DT, "sum": c0["sum"] + DT})

        norm_ple = Norm(xT, DT, "ple_norm", h_hi, h_lo, SUMS["ple"])
        ple = LayerEmbedding(norm_ple, XS["ple"])
        norm_block2 = Norm(xT, DT, "g_norm", h_hi, h_lo, SUMS["block2"])

        norm_cq = Norm(lat32, 3, "g_cq", cq_hi, cq_lo, SUMS["block2"] + 4)
        norm_ckv = Norm(ckv32, 2, "g_ckv", ckv_hi, ckv_lo, SUMS["block2"] + 7)

        class LatentProjections:

            def __init__(self):
                (self.rope_landed, self.tabs, self.lat, self.q32, self.k32, self.sq, self.swap, self.sum, self.std, self.rstd,
                 self.cos, self.sin, self.rot, self.f32, self.hi, self.ready, self.v) = (
                    sem(f"latent_{x}") for x in ("rope_landed", "tabs", "latents", "q32", "k32", "square", "swapped", "sum",
                                                 "std", "rstd", "cos", "sin", "rotated", "f32", "hi", "ready", "v"))

            def tensor(self, pe):
                u = BASE["mla_cq"]
                for j in range(6):
                    pe.wait_ge(lo_ready, u + j + 1)
                    linear(pe, bank(j), u + j, h_hi, h_lo, DT, chunk_ready=norm_block2.ready if j == 0 else None,
                           ready_base=norm_block2.base)
                norm_cq.tensor(pe)
                norm_ckv.tensor(pe)
                pe.wait_ge(norm_cq.ready, norm_cq.base + 3)
                pe.wait_ge(norm_ckv.ready, norm_ckv.base + 2)
                pe.wait_ge(self.lat, 6)
                for h in range(HEADS + 1):
                    if h < HEADS:
                        u = BASE["mla_qk"] + h
                        pe.wait_ge(lo_ready, u + 1)
                        if h >= 2:
                            pe.wait_ge(self.q32, h - 1)
                            pe.wait_ge(self.k32, h - 1)
                        b = 2 * (h % 2)
                        linear(pe, bank(b), u, cq_hi, cq_lo, 3, signal=False)
                        linear(pe, bank(b + 1), u, ckv_hi, ckv_lo, 2, first=3)
                    if h:
                        for m in (2 * h - 2, 2 * h - 1):
                            pe.wait_ge(self.sq, m + 1)
                            if m >= 2:
                                pe.wait_ge(self.std, m - 1)
                            pe.matmul(bank(4 + m % 2), ones, head_sq[m % 2][:, :], start=True,
                                      stop=True).then_inc(self.sum, 1)
                pe.wait_ge(self.q32, HEADS)
                pe.wait_ge(self.k32, HEADS)
                pe.wait_ge(lo_ready, BASE["mla_v"] + 1)
                linear_by_token(pe, (0, 1, 2, 3), BASE["mla_v"], 0, 1, ckv_hi, ckv_lo)

            def load(self, act):
                act.wait_ge(merge1.ready, DT)
                act.dma_start(rope[:, :, :], rope_in).then_inc(self.rope_landed, 16)

            def scalar(self, act):
                u = BASE["mla_cq"]
                for j in range(6):
                    split_hi_to(act, u + j + 2)
                    act.wait_ge(unit_done, u + j + 1)
                    dst = (lat32[:, j, :] if j < 3 else ckv32[:, j - 3, :]) if j < 5 else krope[:, :]
                    act.activation(dst, bank(j), ACT.Copy).then_inc(self.lat, 1)
                norm_cq.scalar(act)
                norm_ckv.scalar(act)
                for m in range(2 * HEADS + 1):
                    if m < 2 * HEADS:
                        h, p = m // 2, m % 2
                        u = BASE["mla_qk"] + h
                        split_hi_to(act, u + 2)
                        if p == 0:
                            act.wait_ge(unit_done, u + 1)
                            if m == 0:
                                act.wait_ge(norm_cq.ready, norm_cq.base + 3)
                            else:
                                act.wait_ge(self.cos, m - 1)
                            act.activation(head32[0][:, :], bank(2 * (h % 2)), ACT.Copy).then_inc(self.q32, 1)
                        act.wait_ge(*((self.k32, h + 1) if p else (self.q32, h + 1)))
                        if m >= 2:
                            act.wait_ge(self.sum, m - 1)
                        act.activation(head_sq[p][:, :], head32[p][:, :], ACT.Square).then_inc(self.sq, 1)
                        if m >= 2:
                            act.wait_ge(self.rot, m - 1)
                        for a in (64, 96):
                            act.activation(swapped[p][a:a + 32, :], head32[p][160 - a:192 - a, :],
                                           ACT.Copy).then_inc(self.swap, 1)
                    if m:
                        i = m - 1
                        act.wait_ge(self.sum, i + 1)
                        if i:
                            act.wait_ge(self.rstd, i)
                        act.activation(std[:, :], bank(4 + i % 2), ACT.Sqrt, scale=1.0 / QKD,
                                       bias=col("eps")).then_inc(self.std, 1)
                        act.wait_ge(self.f32, i + 1)
                        dst = (mq_hi, mk_hi)[i % 2]
                        act.activation(dst[:, i // 2, :], stage32[i % 2][:, :], ACT.Copy).then_inc(self.hi, 1)
                split_hi_to(act, BASE["mla_v"] + 1)
                act.wait_ge(unit_done, BASE["mla_v"] + 1)
                act.wait_ge(self.ready, 2 * HEADS)
                for t in range(TT):
                    act.activation(mv32[:, t, :], bank(t), ACT.Copy).then_inc(self.v, 1)
                split_hi_to(act, BASE["mla_v"] + 3)

            def vector(self, dve):
                dve.wait_ge(self.rope_landed, 16)
                for i, (which, gain) in enumerate(((0, "g_qn"), (1, "g_qn_swapped"), (0, "g_kn"), (1, "g_kn_swapped"))):
                    dve.tensor_scalar(tabs[:, i, :], rope[:, which, :], col(gain), None, ALU.mult).then_inc(self.tabs, 1)
                for norm, n, x in ((norm_cq, 3, lat32), (norm_ckv, 2, ckv32)):
                    clear_sum(dve)
                    for k in range(n):
                        dve.wait_ge(self.lat, (0 if n == 3 else 3) + k + 1)
                        add_square(dve, x[:, k, :])
                    norm.vector(dve)
                dve.wait_ge(self.tabs, 4)
                dve.wait_ge(self.lat, 6)
                dve.wait_ge(norm_ckv.ready, norm_ckv.base + 2)
                for m in range(2 * HEADS):
                    h, p = m // 2, m % 2
                    if p == 0:
                        dve.wait_ge(unit_done, BASE["mla_qk"] + h + 1)
                        if h:
                            dve.wait_ge(self.sq, m)
                            dve.wait_ge(self.swap, 2 * m)
                            dve.wait_ge(self.cos, m)
                        dve.tensor_tensor(head32[1][:, :], bank(2 * (h % 2) + 1), krope[:, :],
                                          ALU.add).then_inc(self.k32, 1)
                    out32 = stage32[p]
                    dve.wait_ge(*((self.k32, h + 1) if p else (self.q32, h + 1)))
                    if m >= 2:
                        dve.wait_ge(self.ready, m - 1)
                    dve.tensor_tensor(out32[:, :], head32[p][:, :], tabs[:, 2 * p, :], ALU.mult).then_inc(self.cos, 1)
                    dve.wait_ge(self.swap, 2 * m + 2)
                    sw, rows = swapped[p], slice(64, P)
                    dve.tensor_tensor(sw[rows, :], sw[rows, :], tabs[rows, 2 * p + 1, :], ALU.mult).then_inc(self.sin, 1)
                    dve.wait_ge(self.cos, m + 1)
                    dve.wait_ge(self.sin, m + 1)
                    dve.tensor_tensor(out32[rows, :], out32[rows, :], sw[rows, :], ALU.add).then_inc(self.rot, 1)
                    dve.wait_ge(self.std, m + 1)
                    if m:
                        dve.wait_ge(self.f32, m)
                    dve.reciprocal(rstd[:, :], std[:, :]).then_inc(self.rstd, 1)
                    dve.wait_ge(self.rstd, m + 1)
                    dve.wait_ge(self.rot, m + 1)
                    dve.tensor_tensor(out32[:, :], out32[:, :], rstd[:, :], ALU.mult).then_inc(self.f32, 1)
                    hi, lo = ((mq_hi, mq_lo), (mk_hi, mk_lo))[p]
                    dve.wait_ge(self.hi, m + 1)
                    dve.tensor_tensor(lo[:, h, :], out32[:, :], hi[:, h, :].bitcast(F32),
                                      ALU.subtract).then_inc(self.ready, 1)

        latent = LatentProjections()
        mla = SoftmaxAttention("mla", lambda h: (mq_hi[:, h, :], mq_lo[:, h, :]),
                               lambda h: (mk_hi[:, h, :], mk_lo[:, h, :]),
                               lambda h, s: mv32[:, s, (h // 2) * P:(h // 2 + 1) * P],
                               mprob, mprobT, QKD ** -0.5, False, False)

        class AttentionGate:

            def __init__(self):
                self.sig, self.silu, self.f32, self.hi, self.ready = (
                    sem(f"attention_gate_{x}") for x in ("sigmoid", "silu", "f32", "hi", "ready"))

            def tensor(self, pe):
                for j in range(4):
                    u = BASE["mla_z"] + j
                    pe.wait_ge(lo_ready, u + 1)
                    pe.wait_ge(mla.exped, TT * HEADS)
                    linear(pe, bank(j), u, h_hi, h_lo, DT)

            def scalar(self, act):
                for j in range(4):
                    u = BASE["mla_z"] + j
                    split_hi_to(act, u + 2)
                    act.wait_ge(unit_done, u + 1)
                    if j >= 2:
                        act.wait_ge(self.silu, j - 1)
                    act.activation(stage32[j % 2][:, :], bank(j), ACT.Sigmoid).then_inc(self.sig, 1)
                    act.wait_ge(self.f32, j + 1)
                    act.activation(ya_hi[:, j, :], std[:, :], ACT.Copy).then_inc(self.hi, 1)

            def vector(self, dve):
                dve.wait_ge(mla.out, HEADS)
                for j in range(4):
                    dve.wait_ge(self.sig, j + 1)
                    dve.tensor_tensor(square[:, :], stage32[j % 2][:, :], bank(j), ALU.mult).then_inc(self.silu, 1)
                    dve.wait_ge(self.silu, j + 1)
                    dve.tensor_tensor(std[:, :], square[:, :], y32[:, j, :], ALU.mult).then_inc(self.f32, 1)
                    dve.wait_ge(self.hi, j + 1)
                    dve.tensor_tensor(ya_lo[:, j, :], std[:, :], ya_hi[:, j, :].bitcast(F32),
                                      ALU.subtract).then_inc(self.ready, 1)
                    dve.wait_ge(self.ready, j + 1)

        attention_gate = AttentionGate()

        class Filters:

            def __init__(self):
                (self.landed, self.layer, self.arg, self.turn, self.act, self.tile, self.f32, self.bias, self.hi,
                 self.ready, self.spec) = (
                    sem(f"filter_{x}") for x in ("landed", "layer", "argument", "turn", "sine", "tile", "f32", "bias",
                                                 "hi", "ready", "spectrum"))

            def load(self, act):
                act.wait_ge(attention_gate.ready, 4)
                for dst, src in ((posT[:, :], pos_in), (wf1[:, :], wf1_in), (wf2[:, :], wf2_in), (wf3[:, :], wf3_in),
                                 (decay[:, :, :], decay_in), (hyb[:, :, :], hyb_in)):
                    act.dma_start(dst, src).then_inc(self.landed, 16)

            def tensor(self, pe):
                pe.wait_ge(self.landed, 96)
                pe.wait_ge(mla.copied0, 2 * HEADS)
                pe.matmul(bank(4)[0:64, :], wf1[:, :], posT[:, :], start=True, stop=True).then_inc(self.layer, 1)
                pe.wait_ge(self.act, 1)
                pe.matmul(bank(4)[0:64, :], wf2[:, :], hid[0][:, :], start=True, stop=True).then_inc(self.layer, 1)
                pe.wait_ge(self.act, 2)
                for o in range(2):
                    for i in range(8):
                        n = 8 * o + i
                        if n >= 2:
                            pe.wait_ge(self.f32, n - 1)
                        c = (2 * o + i // 4) * T
                        pe.matmul(bank(4 + n % 2), hid[1][:, (i % 4) * P:(i % 4 + 1) * P], wf3[:, c:c + T],
                                  start=True, stop=True).then_inc(self.tile, 1)
                    for m in range(8):
                        n = 8 * o + m
                        u = BASE["spectra"] + n
                        pe.wait_ge(lo_ready, u + 1)
                        pe.wait_ge(*((self.spec, n - 3) if n >= 4 else (attention_gate.ready, 4)))
                        linear(pe, bank(m % 4), u, kf_hi, kf_lo, 8, chunk_ready=None if m else self.ready,
                               ready_base=8 * o)

            def scalar(self, act):
                for i in range(2):
                    act.wait_ge(self.turn, 5 * i + 5)
                    act.activation(hid[i][:, :], stage32[0][0:64, :], ACT.Sin).then_inc(self.act, 1)
                for o in range(2):
                    if o:
                        act.wait_ge(unit_done, BASE["spectra"] + 8)
                    for i in range(8):
                        n = 8 * o + i
                        act.wait_ge(self.f32, n + 1)
                        if i == 0:
                            act.wait_ge(self.bias, o + 1)
                        act.activation(kf_hi[:, i, :], stage32[n % 2][:, :], ACT.Copy).then_inc(self.hi, 1)
                    for m in range(8):
                        u = BASE["spectra"] + 8 * o + m
                        split_hi_to(act, u + 2)
                        act.wait_ge(unit_done, u + 1)
                        act.activation(spec[o][:, m, :], bank(m % 4), ACT.Copy).then_inc(self.spec, 1)

            def vector(self, dve):
                dve.wait_ge(self.landed, 96)
                a, r = stage32[1][0:64, :], stage32[0][0:64, :]
                c1 = 6.28125
                for i in range(2):
                    dve.wait_ge(self.layer, i + 1)
                    dve.tensor_scalar(a, bank(4)[0:64, :], col(f"b_f{i + 1}", p=64), col(f"freq_{i + 1}", p=64), ALU.add,
                                      ALU.mult).then_inc(self.arg, 1)
                    dve.wait_ge(self.arg, i + 1)

                    def turn(ins):
                        ins.then_inc(self.turn, 1)
                        counts["turn"] = counts.get("turn", 0) + 1
                        dve.wait_ge(self.turn, counts["turn"])

                    if i:
                        dve.wait_ge(self.act, 1)
                    turn(dve.tensor_scalar(r, a, 1.0 / (2 * math.pi), BIG, ALU.mult, ALU.add))
                    turn(dve.tensor_scalar(r, r, BIG, None, ALU.subtract))
                    turn(dve.scalar_tensor_tensor(a, r, -c1, a, ALU.mult, ALU.add))
                    turn(dve.scalar_tensor_tensor(r, r, -(2 * math.pi - c1), a, ALU.mult, ALU.add))
                    turn(dve.tensor_scalar(r, r, 3.1415925, -3.1415925, ALU.min, ALU.max))
                dve.wait_ge(self.act, 2)
                for o in range(2):
                    if o:
                        dve.wait_ge(unit_done, BASE["spectra"] + 8)
                    for i in range(9):
                        n = 8 * o + i
                        if i < 8:
                            if n >= 2:
                                dve.wait_ge(self.ready, n - 1)
                            dve.wait_ge(self.tile, n + 1)
                            f32 = stage32[n % 2]
                            dve.tensor_tensor(f32[:, :], bank(4 + n % 2), decay[:, i % 4, :],
                                              ALU.mult).then_inc(self.f32, 1)
                            if i == 0:
                                dve.wait_ge(self.f32, n + 1)
                                dve.tensor_tensor(f32[0:1, :], f32[0:1, :], hyb[0:1, o, :],
                                                  ALU.add).then_inc(self.bias, 1)
                                dve.wait_ge(self.bias, o + 1)
                        if i:
                            dve.wait_ge(self.hi, n)
                            dve.tensor_tensor(kf_lo[:, i - 1, :], stage32[(n - 1) % 2][:, :],
                                              kf_hi[:, i - 1, :].bitcast(F32), ALU.subtract).then_inc(self.ready, 1)

        filters = Filters()

        class HyenaInputs:

            def __init__(self):
                (self.mid, self.left, self.conv, self.turned, self.hi, self.copied, self.ready, self.sig, self.silu,
                 self.x2z) = (
                    sem(f"hyena_{x}") for x in ("middle", "left", "conv", "transposed", "v_hi", "x1", "v_ready",
                                                "sigmoid", "silu", "x2z"))

            def target(self, j):
                return conv[j % 2][:, :] if j < 8 else x2z[:, j - 8, :]

            def tensor(self, pe):
                for j in range(17):
                    if j < 16:
                        u = BASE["hy_in"] + j
                        pe.wait_ge(lo_ready, u + 1)
                        if j < 4:
                            pe.wait_ge(filters.spec, 13 + j)
                        elif j < 15:
                            pe.wait_ge(self.conv, j - 3)
                        if j == 15:
                            pe.wait_ge(self.conv, 12)
                        linear(pe, bank(j % 4), u, h_hi, h_lo, DT)
                    if 1 <= j <= 8:
                        i = j - 1
                        pe.wait_ge(self.conv, i + 1)
                        if i >= 2:
                            pe.wait_ge(*((self.ready, i - 1) if i < 6 else (self.copied, i - 5)))
                        for t in range(TT):
                            last = pe.transpose(psum[:, 512 * (4 + i % 2) + t * P:512 * (4 + i % 2) + (t + 1) * P],
                                                conv[i % 2][:, t * P:(t + 1) * P], ident)
                        last.then_inc(self.turned, 1)

            def by_token(self, i, x):
                return x[:, :, (i % 4) * P:(i % 4 + 1) * P]

            def turned_bank(self, i):
                return bank(4 + i % 2).rearrange("p (t c) -> p t c", t=TT)

            def scalar(self, act):
                for j in range(17):
                    if j < 12:
                        split_hi_to(act, BASE["hy_in"] + j + 2)
                        act.wait_ge(unit_done, BASE["hy_in"] + j + 1)
                        if 2 <= j < 8:
                            act.wait_ge(self.turned, j - 1)
                        if j == 0:
                            act.wait_ge(filters.ready, 16)
                        act.activation(self.target(j), bank(j % 4), ACT.Identity, scale=col("w_short", 3 * j + 1),
                                       bias=col("b_short", j)).then_inc(self.mid, 1)
                    elif j < 16:
                        i = j - 12
                        split_hi_to(act, BASE["hy_in"] + j + 2)
                        act.wait_ge(unit_done, BASE["hy_in"] + j + 1)
                        if i >= 2:
                            act.wait_ge(self.silu, i - 1)
                        act.activation(stage32[i % 2][:, :], bank(j % 4), ACT.Sigmoid).then_inc(self.sig, 1)
                    if 1 <= j <= 8:
                        i = j - 1
                        act.wait_ge(self.turned, i + 1)
                        dst = self.by_token(i, v_hi if i < 4 else x1tok)
                        act.activation(dst, self.turned_bank(i), ACT.Copy).then_inc(self.hi if i < 4 else self.copied, 1)

            def vector(self, dve):
                for j in range(17):
                    if j < 12:
                        dst, b = self.target(j), bank(j % 4)
                        dve.wait_ge(self.mid, j + 1)
                        dve.scalar_tensor_tensor(dst[:, 1:T], b[:, 0:T - 1], col("w_short", 3 * j), dst[:, 1:T],
                                                 ALU.mult, ALU.add).then_inc(self.left, 1)
                        dve.wait_ge(self.left, j + 1)
                        dve.scalar_tensor_tensor(dst[:, 0:T - 1], b[:, 1:T], col("w_short", 3 * j + 2), dst[:, 0:T - 1],
                                                 ALU.mult, ALU.add).then_inc(self.conv, 1)
                    elif j < 16:
                        i = j - 12
                        if i == 0:
                            dve.wait_ge(self.conv, 12)
                        else:
                            dve.wait_ge(self.x2z, i)
                        dve.wait_ge(self.sig, i + 1)
                        dve.tensor_tensor(square[:, :], stage32[i % 2][:, :], bank(j % 4), ALU.mult).then_inc(self.silu, 1)
                        dve.wait_ge(self.silu, i + 1)
                        dve.tensor_tensor(x2z[:, i, :], x2z[:, i, :], square[:, :], ALU.mult).then_inc(self.x2z, 1)
                    if 1 <= j <= 4:
                        i = j - 1
                        dve.wait_ge(self.hi, i + 1)
                        dve.tensor_tensor(self.by_token(i, v_lo), self.turned_bank(i),
                                          self.by_token(i, v_hi).bitcast(F32), ALU.subtract).then_inc(self.ready, 1)

        hyena_in = HyenaInputs()

        class LongConvolution:

            signals = [sem(f"long_{x}") for x in ("products", "f32", "hi", "ready", "gated", "gated_hi", "out")]

            def __init__(self, o):
                self.o = o
                self.prod, self.f32, self.hi, self.ready, self.out32, self.out_hi, self.out = LongConvolution.signals

            def tensor(self, pe, before):
                for s, v in before:
                    pe.wait_ge(s, v)
                for j in range(4):
                    u = BASE[f"fwd{self.o}"] + j
                    pe.wait_ge(lo_ready, u + 1)
                    if j >= 2:
                        pe.wait_ge(self.prod, 16 * self.o + 4 * (j - 1))
                    b = 2 * (j % 2)
                    linear(pe, bank(b), u, v_hi, v_lo, 4, signal=False)
                    linear(pe, bank(b + 1), u, v_hi, v_lo, 4, first=4)
                for j in range(4):
                    u = BASE[f"inv{self.o}"] + j
                    pe.wait_ge(lo_ready, u + 1)
                    pe.wait_ge(self.ready, 8 * self.o + 8)
                    if self.o == 0:
                        linear(pe, bank(4 + j), u, Y_hi, Y_lo, 8)
                    else:
                        linear_by_token(pe, (4, 5, 6, 7), u, j, 4, Y_hi, Y_lo)

            def scalar(self, act):
                for j in range(4):
                    split_hi_to(act, BASE[f"fwd{self.o}"] + j + 2)
                    for i in range(2):
                        act.wait_ge(self.f32, 8 * self.o + 2 * j + i + 1)
                        act.activation(Y_hi[:, 4 * i + j, :], stage32[i][:, :], ACT.Copy).then_inc(self.hi, 1)
                for j in range(4):
                    split_hi_to(act, BASE[f"inv{self.o}"] + (j + 2 if self.o == 0 else 4))
                    act.wait_ge(self.out32, 4 * self.o + j + 1)
                    act.activation(yb_hi[:, j, :], stage32[j % 2][:, :], ACT.Copy).then_inc(self.out_hi, 1)

            def vector(self, dve):
                for j in range(4):
                    dve.wait_ge(unit_done, BASE[f"fwd{self.o}"] + j + 1)
                    k_re, k_im = spec[self.o][:, j, :], spec[self.o][:, 4 + j, :]
                    u_re, u_im = bank(2 * (j % 2)), bank(2 * (j % 2) + 1)
                    if j:
                        dve.wait_ge(self.ready, 8 * self.o + 2 * j)
                    for i, (a, b) in enumerate(((k_re, u_re), (k_im, u_im), (k_re, u_im), (k_im, u_re))):
                        dve.tensor_tensor(prod[i][:, :], a, b, ALU.mult).then_inc(self.prod, 1)
                    dve.wait_ge(self.prod, 16 * self.o + 4 * j + 4)
                    for i, op in enumerate((ALU.subtract, ALU.add)):
                        dve.tensor_tensor(stage32[i][:, :], prod[2 * i][:, :], prod[2 * i + 1][:, :],
                                          op).then_inc(self.f32, 1)
                    for i in range(2):
                        dve.wait_ge(self.hi, 8 * self.o + 2 * j + i + 1)
                        dve.tensor_tensor(Y_lo[:, 4 * i + j, :], stage32[i][:, :],
                                          Y_hi[:, 4 * i + j, :].bitcast(F32), ALU.subtract).then_inc(self.ready, 1)
                dve.wait_ge(self.ready, 8 * self.o + 8)
                for j in range(5):
                    if j < 4:
                        dve.wait_ge(unit_done, BASE[f"inv{self.o}"] + (j + 1 if self.o == 0 else 4))
                        if j >= 2:
                            dve.wait_ge(self.out, 4 * self.o + j - 1)
                        gate_tile = (x1tok, x2z)[self.o][:, j, :]
                        dve.tensor_tensor(stage32[j % 2][:, :], gate_tile, bank(4 + j), ALU.mult).then_inc(self.out32, 1)
                    if j:
                        dve.wait_ge(self.out_hi, 4 * self.o + j)
                        dve.tensor_tensor(yb_lo[:, j - 1, :], stage32[(j - 1) % 2][:, :],
                                          yb_hi[:, j - 1, :].bitcast(F32), ALU.subtract).then_inc(self.out, 1)
                dve.wait_ge(self.out, 4 * self.o + 4)

        long0, long1 = LongConvolution(0), LongConvolution(1)
        merge2 = Merge(2, "b_gate", XS["out2"], [(attention_gate.ready, 4), (long1.out, 8)], False)

        block = ctx.enter_context(nc.Block())
        stored = sem("stored")

        @block.sync
        def _(sp):
            for k in range(2):
                load_unit(sp, k, 0, "k", k)
            sp.dma_start(xT[:, :, :], x_in).then_inc(x_landed, 16)
            sp.dma_start(vec[:, :], vec_in).then_inc(vec_landed, 16)
            sp.dma_start(constf[:, :, :], constf_in).then_inc(const_landed, 16)
            sp.dma_start(constr32[:, :, :], constr_in).then_inc(constr_landed, 16)
            stream_loads(sp)
            sp.wait_ge(x_updated, XS["out2"] + DT)
            sp.dma_start(out, xT[:, :, :]).then_inc(stored, 16)
            sp.wait_ge(stored, 16)

        @block.gpsimd
        def _(pool):
            stream_lo(pool)

        @block.scalar
        def _(act):
            act.wait_ge(constr_landed, 16)
            act.activation(constr[:, :, :], constr32[:, :, :], ACT.Copy).then_inc(constr_ready, 1)
            split_hi_to(act, 2)
            act.wait_ge(vec_landed, 16)
            norm_ffn1.scalar(act)
            ffn1.scalar(act)
            act.dma_start(sel32[:, :, :], sel_in).then_inc(foxp.sel_landed, 16)
            split_hi_to(act, BASE["fox_q"] + 2)
            norm_mix.scalar(act)
            foxp.scalar(act)
            fox.scalar(act)
            stickp.scalar(act)
            stick.scalar(act)
            merge1.scalar(act)
            split_hi_to(act, BASE["ffn2_up0"] + 2)
            norm_ffn2.scalar(act)
            ffn2.scalar(act)
            ple.load(act)
            split_hi_to(act, BASE["ple"] + 2)
            norm_ple.scalar(act)
            ple.scalar(act)
            latent.load(act)
            split_hi_to(act, BASE["mla_cq"] + 2)
            norm_block2.scalar(act)
            latent.scalar(act)
            mla.scalar(act)
            attention_gate.scalar(act)
            filters.load(act)
            filters.scalar(act)
            hyena_in.scalar(act)
            long0.scalar(act)
            long1.scalar(act)
            merge2.scalar(act)

        @block.vector
        def _(dve):
            dve.memset(small[:, :], 0.0).then_inc(x_updated, 2)
            clear_sum(dve)
            dve.wait_ge(x_landed, 16)
            for k in range(DT):
                add_square(dve, xT[:, k, :])
            dve.wait_ge(vec_landed, 16)
            norm_ffn1.vector(dve)
            ffn1.vector(dve)
            norm_mix.vector(dve)
            foxp.vector(dve)
            fox.vector(dve)
            stickp.vector(dve)
            stick.vector(dve)
            merge1.vector(dve)
            norm_ffn2.vector(dve)
            ffn2.vector(dve)
            norm_ple.vector(dve)
            ple.vector(dve)
            norm_block2.vector(dve)
            latent.vector(dve)
            mla.vector(dve)
            attention_gate.vector(dve)
            filters.vector(dve)
            hyena_in.vector(dve)
            long0.vector(dve)
            long1.vector(dve)
            merge2.vector(dve)

        @block.tensor
        def _(pe):
            pe.wait_ge(const_landed, 16)
            norm_ffn1.tensor(pe)
            ffn1.tensor(pe)
            norm_mix.tensor(pe)
            foxp.tensor(pe, norm_mix)
            fox.tensor(pe, [(constr_ready, 1), (foxp.sel, 1), (foxp.ready, 12), (foxp.nf, 1), (foxp.v, TT)])
            stickp.tensor(pe)
            stick.tensor(pe)
            merge1.tensor(pe)
            norm_ffn2.tensor(pe)
            ffn2.tensor(pe)
            norm_ple.tensor(pe)
            ple.tensor(pe)
            norm_block2.tensor(pe)
            latent.tensor(pe)
            mla.tensor(pe, [(latent.ready, 2 * HEADS), (latent.v, TT)])
            attention_gate.tensor(pe)
            filters.tensor(pe)
            hyena_in.tensor(pe)
            long0.tensor(pe, [(hyena_in.ready, 4), (hyena_in.silu, 4)])
            long1.tensor(pe, [(long0.out, 4)])
            merge2.tensor(pe)


def _feature_units(w):
    kk, n = w.shape
    return w.reshape(kk // P, P, n // P, P).transpose(2, 1, 0, 3).reshape(n // P, P, kk)


def _token_units(w):
    kk, n = w.shape
    return w.reshape(kk // 256, 2, P, n).transpose(0, 2, 1, 3).reshape(kk // 256, P, 2 * n)


def _wide(u, n=1024):
    out = np.zeros((u.shape[0], P, n), np.float32)
    out[:, :, :u.shape[2]] = u
    return out


def _columns(v):
    return np.ascontiguousarray(v.reshape(-1, P).T)


def _rope_rows(a, axis=0):
    a = np.moveaxis(a, axis, 0)
    out = np.zeros((P,) + a.shape[1:], np.float32)
    out[0:64] = a[0:64]
    out[64:80] = a[64:80]
    out[96:112] = a[80:96]
    return np.moveaxis(out, 0, axis)


def _constants():
    i = np.arange(P)
    eye = np.eye(P, dtype=np.float32)
    blocks = (i[:, None] // HD == i[None, :] // HD).astype(np.float32)
    before = (i[:, None] < i[None, :]).astype(np.float32)
    constf = np.stack([eye, blocks, np.ones((P, P), np.float32), before], 1)
    tri = -(i[:, None] >= i[None, :]).astype(np.float32)
    mask_qk = np.where(i[None, :] > i[:, None], np.float32(NEG), np.float32(0))
    mask_kq = np.where(i[:, None] >= i[None, :], np.float32(NEG), np.float32(0))
    constr = np.stack([eye, tri, -np.ones((P, P), np.float32), mask_qk, mask_kq], 1)
    sel = np.zeros((P, HEADS, P), np.float32)
    for h in range(HEADS):
        sel[h, h, :] = 1
    pos = np.arange(T, dtype=np.float32)
    inv = (np.float32(ROPE_THETA) ** (-np.arange(0, ROPE, 2, dtype=np.float32) / np.float32(ROPE))).astype(np.float32)
    ang = (pos[:, None] * inv[None, :]).astype(np.float32)
    c, s = np.cos(ang).T, np.sin(ang).T
    rope = np.zeros((P, 2, T), np.float32)
    rope[0:64, 0] = 1
    rope[64:80, 0], rope[96:112, 0] = c, c
    rope[64:80, 1], rope[96:112, 1] = -s, s
    t = np.linspace(0.0, 1.0, T, dtype=np.float32)
    lo, hi = math.log(1e-2) / 1.5, math.log(1e-2) / 0.3
    deltas = np.abs(np.linspace(lo, hi, T, dtype=np.float32))
    decay = np.exp(-t[:, None] * deltas).astype(np.float32).reshape(TT, P, T).transpose(1, 0, 2)
    bands = 16
    f = np.linspace(1e-4, bands - 1, bands, dtype=np.float32)
    a2 = (np.float32(2.0 * np.pi / T) * pos[:, None] * f[None, :]).astype(np.float32)
    posT = np.concatenate([t[:, None], np.cos(a2), -np.sin(a2)], -1).T.astype(np.float32)
    n = np.arange(T, dtype=np.float64)
    w = np.pi * (2 * np.arange(T) + 1) / (2 * T)
    th, th1 = n[:, None] * w, (n[:, None] + 1) * w
    fwd = np.concatenate([np.cos(th), -np.sin(th)], 1).astype(np.float32)
    neg = np.concatenate([np.cos(th1), np.sin(th1)], 1).astype(np.float32)
    inv_ = (np.concatenate([np.cos(th.T), -np.sin(th.T)], 0) / T).astype(np.float32)
    spectra = _feature_units(np.concatenate([fwd, neg], 0))
    fu = _feature_units(fwd)
    fwd_units = np.concatenate([fu[0:4], fu[4:8]], 2)
    inv_units = _feature_units(inv_)
    inv_tok = _token_units(inv_)
    return constf, constr, sel, rope, decay, posT, spectra, fwd_units, inv_units, inv_tok


def kernel(**inputs):
    import concourse.bacc as _bacc
    from concourse.bass_utils import run_bass_kernel_spmd as _run

    g = {k: np.ascontiguousarray(v) for k, v in inputs.items()}
    constf, constr, sel, rope, decay, posT, spectra, fwd_units, inv_units, inv_tok = _constants()

    def cols(w, a, n):
        return w[:, a:a + n]

    ks, ds = [], []
    for n in ("1", "2"):
        up = np.stack([_feature_units(g[f"ffn{n}_w_gate"][0]), _feature_units(g[f"ffn{n}_w_up"][0])], 1)
        down = g[f"ffn{n}_w_down"][0]
        halves = []
        for half in range(2):
            halves.append(up[half * FH:(half + 1) * FH].reshape(2 * FH, P, D))
            ds.append(_feature_units(down[half * FH * P:(half + 1) * FH * P]))
        ks.append(halves)
    w1 = g["w_in"][0]
    fq, fk, fv, fl, sq, sk, sv, gf, gs = [w1[:, a:b] for a, b in zip(
        [0, 512, 1024, 1536, 1544, 2056, 2568, 3080, 4104], [512, 1024, 1536, 1544, 2056, 2568, 3080, 4104, 5128])]
    flp = np.zeros((D, P), np.float32)
    flp[:, 0:HEADS] = fl

    def merge_units(ga, gb, ba, bb):
        both = np.concatenate([_feature_units(ba), _feature_units(bb)], 2)
        return np.stack([_feature_units(ga), _feature_units(gb), both], 1).reshape(3 * DT, P, D)

    w2 = g["w_in_2"][0]
    edges = np.cumsum([0, 1536, 512, 384, 256, 32, 512, 1024, 1024])
    hy, zh, cq, ckv, kr, za, gh, ga = [w2[:, a:b] for a, b in zip(edges[:-1], edges[1:])]
    krp = np.zeros((D, P), np.float32)
    krp[:, 64:80], krp[:, 96:112] = kr[:, 0:16], kr[:, 16:32]
    uq = _rope_rows(g["w_uq_2"][0].reshape(384, HEADS, QKD), 2)
    ukv = g["w_ukv_2"][0].reshape(256, HEADS, P)
    uk = np.zeros((256, HEADS, P), np.float32)
    uk[:, :, 0:64] = ukv[:, :, 0:64]
    qk = np.concatenate([_feature_units(uq.reshape(384, D)), _feature_units(uk.reshape(256, D))], 2)
    uv = np.ascontiguousarray(ukv[:, :, 64:128]).reshape(256, 512)
    wk = np.concatenate([
        ks[0][0], ks[0][1],
        _feature_units(fq), _feature_units(fk), _feature_units(flp), _token_units(fv),
        _feature_units(sq), _feature_units(sk), _token_units(sv),
        merge_units(gf, gs, g["w_branch_fox"][0], g["w_branch_sb"][0]), _feature_units(g["w_out"][0]),
        ks[1][0], ks[1][1],
        _feature_units(cq), _feature_units(ckv), _feature_units(krp), _wide(qk), _token_units(uv), _feature_units(za),
        spectra, spectra, _feature_units(hy), _feature_units(zh),
        fwd_units, inv_units, fwd_units, inv_tok,
        merge_units(ga, gh, g["w_attn_out_2"][0], g["w_hy_out_2"][0]), _feature_units(g["w_out_2"][0]),
    ], 0)
    assert wk.shape[0] == _at["k"]
    wd = np.concatenate(ds, 0)
    wp = np.concatenate([_feature_units(g["w_ple_gate"][0]), _feature_units(g["w_ple_proj"][0])], 2)

    vec = np.zeros((P, NVEC), np.float32)

    def put(name, v):
        vec[:v.shape[0], VEC[name]:VEC[name] + v.shape[1]] = v

    for name in ("ffn1_norm", "mix_norm", "ffn2_norm", "ple_norm"):
        put(name, _columns(g[name][0]))
    put("g_norm", _columns(g["g_norm_2"][0]))
    for name in ("q_norm", "k_norm"):
        put(name, np.concatenate([g[name][0], g[name][0]])[:, None])
    put("forget_bias", g["forget_bias"][0][:, None])
    bg = g["b_gate_2"][0]
    put("b_gate", np.stack([_columns(bg[D:]), _columns(bg[:D])], 2).reshape(P, 2 * DT))
    put("w_short", np.stack([_columns(g["w_short_2"][0][j]) for j in range(3)], 2).reshape(P, 36))
    put("b_short", _columns(g["b_short_2"][0]))
    put("g_cq", _columns(g["g_cq_2"][0]))
    put("g_ckv", _columns(g["g_ckv_2"][0]))
    for name in ("g_qn", "g_kn"):
        rows = _rope_rows(g[name + "_2"][0])
        put(name, rows[:, None])
        put(name + "_swapped", np.concatenate([rows[0:64], rows[96:128], rows[64:96]])[:, None])
    for name in ("b_f1", "freq_1", "b_f2", "freq_2"):
        put(name, g[name + "_2"][0][:, None])
    vec[:, VEC["eps"]] = EPS

    arrays = {
        "wk": wk, "wd": wd, "wp": wp,
        "x": np.ascontiguousarray(g["x"][0].T).reshape(DT, P, T).transpose(1, 0, 2),
        "p": np.ascontiguousarray(g["p"][0, 0].T).reshape(2, P, T).transpose(1, 0, 2),
        "vec": vec, "constf": constf, "constr": constr, "sel": sel, "rope": rope, "decay": decay, "pos": posT,
        "wf1": g["w_f1_2"][0], "wf2": g["w_f2_2"][0], "wf3": g["w_f3_2"][0], "hyb": g["hy_bias_2"],
    }
    arrays = {k: np.ascontiguousarray(v) for k, v in arrays.items()}
    nc = _bacc.Bacc("TRN2", target_bir_lowering=False, num_devices=1)
    args = [nc.dram_tensor(f"{k}_dram", v.shape, F32, kind="ExternalInput").ap() for k, v in arrays.items()]
    args.append(nc.dram_tensor("out_dram", (P, DT, T), F32, kind="ExternalOutput").ap())
    build(nc, *args)
    r = _run(nc, [{f"{k}_dram": v for k, v in arrays.items()}], core_ids=[0])
    got = r.results[0]["out_dram"]
    return np.ascontiguousarray(got.transpose(1, 0, 2).reshape(D, T).T).reshape(1, T, D)
```

```python
from contextlib import ExitStack
import math

import numpy as np

import concourse.bass as bass
from concourse import mybir

F32 = mybir.dt.float32
F32R = mybir.dt.float32r
ACT = mybir.ActivationFunctionType
ALU = mybir.AluOpType
AXX = mybir.AxisListType.X

P = 128
D = 1024
T = 512
DT = D // P
TT = T // P
DFF = 2816
FH = DFF // P // 2
HEADS = 8
HD = 64
EPS = 1e-6
NEG = -1.0e30
BIG = float(1.5 * 2 ** 23)
ROPE_THETA = 10000.0
ROPE = 32
QKD = 96

WIDTH = {"k": 1024, "d": FH * P, "p": 10 * P}
SEGMENTS = [
    ("ffn1_up0", 22, "k"), ("ffn1_down0", 8, "d"), ("ffn1_up1", 22, "k"), ("ffn1_down1", 8, "d"),
    ("fox_q", 4, "k"), ("fox_k", 4, "k"), ("fox_f", 1, "k"), ("fox_v", 4, "k"),
    ("sb_q", 4, "k"), ("sb_k", 4, "k"), ("sb_v", 4, "k"), ("merge1", 24, "k"), ("out1", 8, "k"),
    ("ffn2_up0", 22, "k"), ("ffn2_down0", 8, "d"), ("ffn2_up1", 22, "k"), ("ffn2_down1", 8, "d"),
    ("ple", 8, "p"),
    ("mla_cq", 3, "k"), ("mla_ckv", 2, "k"), ("mla_kr", 1, "k"), ("mla_qk", 8, "k"), ("mla_v", 1, "k"),
    ("mla_z", 4, "k"),
    ("spectra", 8, "k"), ("hy_in", 12, "k"), ("hy_z", 4, "k"),
    ("fwd0", 4, "k"), ("inv0", 4, "k"), ("fwd1", 4, "k"), ("inv1", 4, "k"),
    ("merge2", 24, "k"), ("out2", 8, "k"),
]
BASE, RUNS = {}, []
_u = 0
_at = {"k": 0, "d": 0, "p": 0}
for _name, _n, _c in SEGMENTS:
    BASE[_name] = _u
    if RUNS and RUNS[-1][1] == _c:
        RUNS[-1][3] += _n
    else:
        RUNS.append([_u, _c, _at[_c], _n])
    _u += _n
    _at[_c] += _n
UNITS = _u

VEC = {}
_v = 0
for _name, _n in [("ffn1_norm", 8), ("mix_norm", 8), ("ffn2_norm", 8), ("ple_norm", 8), ("g_norm", 8),
                  ("q_norm", 1), ("k_norm", 1), ("forget_bias", 1), ("no_bias", 18), ("b_gate", 18),
                  ("w_short", 36), ("b_short", 12), ("g_cq", 3), ("g_ckv", 2),
                  ("g_qn", 1), ("g_kn", 1),
                  ("b_f1", 1), ("freq_1", 1), ("b_f2", 1), ("freq_2", 1), ("eps", 1)]:
    VEC[_name] = _v
    _v += _n
NVEC = _v



AREA = {0: 0, 1: 512, 3: 896, 2: 1024}
AREA_COLS = 1280


def build(nc, wk, wd, wp, x_in, p_in, vec_in, constf_in, constr_in, sel_in, rope_in, decay_in, pos_in,
          wf1_in, wf2_in, wf3_in, hyb_in, out):
    ctx = ExitStack()

    def sem(name):
        return ctx.enter_context(nc.semaphore(name))

    with ctx:
        def keep(name, shape, dt=F32):
            return ctx.enter_context(nc.sbuf_tensor(name, shape, dt))

        xT = keep("xT", [P, DT, T])
        h_hi = keep("h_hi", [P, DT, T], F32R)
        h_lo = keep("h_lo", [P, DT, T], F32R)
        raw = [keep(f"raw{s}", [P, FH * P]) for s in range(2)]
        whi = [keep(f"whi{s}", [P, FH * P], F32R) for s in range(2)]
        wlo = [keep(f"wlo{s}", [P, FH * P], F32R) for s in range(2)]
        vec = keep("vec", [P, NVEC])
        constf = keep("constf", [P, 4, P])
        constr = keep("constr", [P, 5, P], F32R)
        scratch = keep("scratch", [P, 6 * T])
        sumsq, square, std, rstd, *stage32 = (scratch[:, i * T:(i + 1) * T] for i in range(6))
        small = keep("small", [P, 32])
        psum = ctx.enter_context(nc.psum_tensor("psum", [P, 8 * 512], F32))
        ident, block_ones, ones, before = (constf[:, i, :] for i in range(4))
        ident_r, neg_tri, neg_ones, mask_qk, mask_kq = (constr[:, i, :] for i in range(5))
        head_sq = [square, sumsq]

        arena = ctx.enter_context(nc.sbuf_tensor("arena_end", [P, 109 * 256], F32))
        arena0 = nc.sbuf_base - 109 * 1024

        def at(kib, name, shape, dt=F32):
            return nc.alloc_sbuf_tensor_at(name, shape, dt, offset=arena0 + int(kib * 1024))

        mid_hi = at(0, "mid_hi", [P, FH, T], F32R)
        mid_lo = at(22, "mid_lo", [P, FH, T], F32R)
        sig = at(44, "sig", [P, T])
        silu = at(46, "silu", [P, T])
        mid32 = at(48, "mid32", [P, T])
        gate32 = at(50, "gate32", [P, T])
        constr32 = at(96, "constr32", [P, 5, P])
        ya_hi = at(0, "ya_hi", [P, 4, T], F32R)
        ya_lo = at(8, "ya_lo", [P, 4, T], F32R)
        yb_hi = at(16, "yb_hi", [P, 4, T], F32R)
        yb_lo = at(24, "yb_lo", [P, 4, T], F32R)
        q_hi = at(32, "q_hi", [P, HEADS, T], F32R)
        q_lo = at(48, "q_lo", [P, HEADS, T], F32R)
        k_hi = at(64, "k_hi", [P, 4, T], F32R)
        k_lo = at(72, "k_lo", [P, 4, T], F32R)
        v32 = at(80, "v32", [P, TT, T])
        prob = at(88, "prob", [P, TT, T])
        prob_odd = at(16, "prob_odd", [P, TT, T])
        probT = [at(96 + 2 * i, f"probT{i}", [P, T]) for i in range(2)]
        nf_hi = at(100, "nf_hi", [P, T], F32R)
        nf_lo = at(102, "nf_lo", [P, T], F32R)
        sel = at(104, "sel", [P, HEADS, P], F32R)
        sel32 = at(80, "sel32", [P, HEADS, P])
        soft = [at(88, "soft", [P, AREA_COLS]), scratch[:, 0:AREA_COLS]]
        sp_hi = at(93, "sp_hi", [P, AREA_COLS], F32R)
        sp_lo = at(98, "sp_lo", [P, AREA_COLS], F32R)
        weight = [at(103, "weight", [P, AREA_COLS]), scratch[:, 3 * T:3 * T + AREA_COLS]]
        merged_hi = at(32, "merged_hi", [P, DT, T], F32R)
        merged_lo = at(48, "merged_lo", [P, DT, T], F32R)
        gate = [at(64 + 4 * i, f"gate{i}", [P, 2, T]) for i in range(2)]
        gated = at(72, "gated", [P, 2, T])
        sum32 = at(76, "sum32", [P, T])
        gate_bias = [small[:, 24 + 2 * i:26 + 2 * i] for i in range(2)]
        p32 = at(64, "p32", [P, 2, T])
        p_hi = at(68, "p_hi", [P, 2, T], F32R)
        p_lo = at(72, "p_lo", [P, 2, T], F32R)
        ple_gate = [at(76 + 2 * i, f"ple_gate{i}", [P, T]) for i in range(2)]
        ple_add = at(80, "ple_add", [P, T])
        mq_hi = at(32, "mq_hi", [P, HEADS, T], F32R)
        mq_lo = at(48, "mq_lo", [P, HEADS, T], F32R)
        mk_hi = at(64, "mk_hi", [P, HEADS, T], F32R)
        mk_lo = at(80, "mk_lo", [P, HEADS, T], F32R)
        cq_hi = at(0, "cq_hi", [P, 3, T], F32R)
        cq_lo = at(6, "cq_lo", [P, 3, T], F32R)
        ckv_hi = at(12, "ckv_hi", [P, 2, T], F32R)
        ckv_lo = at(16, "ckv_lo", [P, 2, T], F32R)
        tabs = at(20, "tabs", [P, 4, T])
        krope = at(28, "krope", [P, T])
        lat32 = at(96, "lat32", [P, 3, T])
        ckv32 = at(64, "ckv32", [P, 2, T])
        head32 = [at(96 + 2 * i, f"head32_{i}", [P, T]) for i in range(2)]
        swapped = [at(100 + 6 * i, f"swapped{i}", [P, T]) for i in range(2)]
        rope = at(102, "rope", [P, 2, T])
        head_out = [*stage32, at(102, "head_out2", [P, T])]
        mv32 = at(96, "mv32", [P, TT, T])
        mprobT = [at(104 + 2 * i, f"mprobT{i}", [P, T]) for i in range(2)]
        mprob = at(16, "mprob", [P, TT, T])
        mprob_odd = at(0, "mprob_odd", [P, TT, T])
        y32 = at(24, "y32", [P, 4, T])
        spec = [at(48, "spec0", [P, 8, T]), at(32, "spec1", [P, 8, T])]
        Y_lo = at(48, "Y_lo", [P, 8, T], F32R)
        Y_hi = at(64, "Y_hi", [P, 8, T], F32R)
        kf_hi = at(64, "kf_hi", [P, 8, T], F32R)
        kf_lo = at(80, "kf_lo", [P, 8, T], F32R)
        kf_early = [[at(16 + 2 * i if i < 7 else 82 + 2 * i, f"kf_early{i}", [P, T], F32R) for i in (a, a + 1)]
                    for a in (0, 2, 4, 6, 8)]
        wf3 = at(32, "wf3", [64, 4 * T])
        decay = at(40, "decay", [P, TT, T])
        hid = [at(48, "hid0", [64, T]), at(102, "hid1", [64, T])]
        posT = at(50, "posT", [33, T])
        wf1 = at(52, "wf1", [33, 64])
        wf2 = at(53, "wf2", [64, 64])
        hyb = at(104, "hyb", [1, 2, T])
        v_hi, v_lo = yb_hi, yb_lo
        x1tok = at(80, "x1tok", [P, TT, T])
        x2z = at(88, "x2z", [P, TT, T])
        conv = [at(96 + 2 * i, f"conv{i}", [P, T]) for i in range(2)]
        prod = [at(100 + 2 * i, f"prod{i}", [P, T]) for i in range(4)]

        def bank(b, n=512):
            return psum[:, 512 * b:512 * b + n]

        def col(name, i=0, p=P):
            return vec[0:p, VEC[name] + i:VEC[name] + i + 1]

        landed = [sem(f"landed{s}") for s in range(2)]
        hi_ready = sem("hi_ready")
        lo_ready = sem("lo_ready")
        unit_done = sem("unit_done")

        def runs():
            yield from RUNS

        def load_unit(sp, u, k, c, a):
            if not (isinstance(k, int) and u < 2):
                sp.wait_ge(lo_ready, u + k - 1)
            src = {"k": wk, "d": wd, "p": wp}[c]
            w = WIDTH[c]
            row = src[a + k] if isinstance(k, int) else src[bass.ds(a + k, 1)].rearrange("a p n -> (a p) n")
            sp.dma_start(raw[u % 2][:, 0:w], row).then_inc(landed[u % 2], 16)

        def stream_loads(sp):
            for u, c, a, n in runs():
                head = 2 if u < 2 else 0
                with sp.Fori(0, (n - head) // 2) as i:
                    for b in range(2):
                        load_unit(sp, u + head + b, i * 2, c, a + head + b)
                if (n - head) % 2:
                    load_unit(sp, u + n - 1, 0, c, a + n - 1)

        def split_lo(pool, u, k, w):
            pool.wait_ge(hi_ready, u + 1 + k)
            s = u % 2
            pool.tensor_tensor(wlo[s][:, 0:w], raw[s][:, 0:w], whi[s][:, 0:w].bitcast(F32),
                               ALU.subtract).then_inc(lo_ready, 1)

        def stream_lo(pool):
            for u, c, a, n in runs():
                with pool.Fori(0, n // 2) as i:
                    for b in range(2):
                        split_lo(pool, u + b, i * 2, WIDTH[c])
                if n % 2:
                    split_lo(pool, u + n - 1, 0, WIDTH[c])

        class_of = [c for _, n, c in SEGMENTS for _ in range(n)]
        next_hi = [0]

        def split_hi(act, u, k=0):
            s, w = u % 2, WIDTH[class_of[u]]
            act.wait_ge(landed[s], 16 * (u // 2 + 1) + k * 8)
            if not (isinstance(k, int) and u < 2):
                act.wait_ge(unit_done, u - 1 + k)
            act.activation(whi[s][:, 0:w], raw[s][:, 0:w], ACT.Copy).then_inc(hi_ready, 1)

        def split_hi_to(act, u):
            while next_hi[0] < min(u, UNITS):
                split_hi(act, next_hi[0])
                next_hi[0] += 1

        def products(pe, dst, terms, start=True, stop=True, **kw):
            n = len(terms)
            for i, (s_hi, s_lo, m_hi, m_lo) in enumerate(terms):
                pe.matmul(dst, s_hi, m_hi, start=start and i == 0, stop=False, **kw)
                pe.matmul(dst, s_hi, m_lo, start=False, stop=False, **kw)
                last = pe.matmul(dst, s_lo, m_hi, start=False, stop=stop and i == n - 1, **kw)
            return last

        def weight_chunks(u, first, n):
            s = u % 2
            for c in range(first, first + n):
                yield whi[s][:, c * P:(c + 1) * P], wlo[s][:, c * P:(c + 1) * P]

        def linear(pe, dst, u, m_hi, m_lo, n, first=0, chunk_ready=None, ready_base=0, signal=True):
            for c, (a, b) in enumerate(weight_chunks(u, first, n)):
                if chunk_ready is not None:
                    pe.wait_ge(chunk_ready, ready_base + c + 1)
                last = products(pe, dst, [(a, b, m_hi[:, c, :], m_lo[:, c, :])], start=c == 0, stop=c == n - 1)
            if signal:
                last.then_inc(unit_done, 1)

        def linear_by_token(pe, banks, u, j, of, s_hi, s_lo, chunk_ready=None):
            s = u % 2
            if chunk_ready is not None:
                pe.wait_ge(chunk_ready, 2 * j + 2)
            for t, b in enumerate(banks):
                terms = [(s_hi[:, 2 * j + c, t * P:(t + 1) * P], s_lo[:, 2 * j + c, t * P:(t + 1) * P],
                          whi[s][:, c * 512:(c + 1) * 512], wlo[s][:, c * 512:(c + 1) * 512]) for c in range(2)]
                last = products(pe, bank(b), terms, start=j == 0, stop=j == of - 1)
            last.then_inc(unit_done, 1)

        x_landed = [sem(f"x_landed{i}") for i in range(4)]
        vec_landed = sem("vec_landed")
        const_landed = sem("const_landed")
        constr_landed = sem("constr_landed")
        constr_ready = sem("constr_ready")

        x_updated = sem("x_updated")
        squared = sem("squared")
        summed = sem("summed")
        counts = {"x": 2, "sq": 0, "sum": 0}

        def clear_sum(dve):
            dve.memset(sumsq[:, :], 0.0).then_inc(summed, 1)
            counts["sum"] += 1

        def add_square(dve, x, k=0, i=0):
            dve.wait_ge(summed, counts["sum"] + k)
            dve.tensor_tensor(square[:, :], x, x, ALU.mult).then_inc(squared, 1)
            counts["sq"] += 1
            dve.wait_ge(squared, counts["sq"] + k)
            dve.tensor_tensor(sumsq[:, :], sumsq[:, :], square[:, :], ALU.add).then_inc(summed, 1)
            counts["sum"] += 1

        gained_hi = sem("gained_hi")
        gained = sem("gained")
        counts["gain"] = 0

        def split_gained(dve, x, gain, o, k=0):
            fixed = isinstance(k, int)
            hi, lo = ((h[:, o, :] if fixed else h[:, bass.ds(o + k, 1), :].rearrange("p a t -> p (a t)"))
                      for h in (h_hi, h_lo))
            g = col(gain, o) if fixed else vec[:, bass.ds(VEC[gain] + o + k, 1)]
            dve.tensor_scalar(hi, x, g, None, ALU.mult).then_inc(gained_hi, 1)
            counts["gain"] += 1
            dve.wait_ge(gained_hi, counts["gain"] + k)
            dve.scalar_tensor_tensor(lo, x, g, hi.bitcast(F32), ALU.mult, ALU.subtract).then_inc(gained, 1)

        class Norm:

            signals = [sem(f"norm_{s}") for s in ("mean", "std", "rstd", "f32", "hi", "ready")]
            norms, tiles = 0, 0

            def __init__(self, x, n, gain, hi, lo, total):
                self.x, self.n, self.gain, self.hi, self.lo, self.total = x, n, gain, hi, lo, total
                self.mean, self.std, self.rstd, self.f32, self.hi_made, self.ready = Norm.signals
                self.i, self.base = Norm.norms, Norm.tiles
                Norm.norms, Norm.tiles = Norm.norms + 1, Norm.tiles + n

            def tensor(self, pe):
                if self.i == 0:
                    pe.wait_ge(const_landed, 16)
                pe.wait_ge(summed, self.total)
                pe.matmul(bank(7), ones, sumsq[:, :], start=True, stop=True).then_inc(self.mean, 1)

            def factor(self, act):
                act.preload_act_table_set("natural_log_exp_and_others")
                act.wait_ge(self.mean, self.i + 1)
                act.activation(std[:, :], bank(7), ACT.Ln, scale=1.0 / (self.n * P),
                               bias=col("eps")).then_inc(self.std, 1)
                act.wait_ge(self.std, self.i + 1)
                act.activation(rstd[:, :], std[:, :], ACT.Exp, scale=-0.5).then_inc(self.rstd, 1)

            def scalar(self, act):
                self.factor(act)
                for k in range(self.n):
                    act.wait_ge(self.f32, self.base + k + 1)
                    act.activation(self.hi[:, k, :], stage32[k % 2][:, :], ACT.Copy).then_inc(self.hi_made, 1)

            def vector(self, dve):
                dve.wait_ge(self.rstd, self.i + 1)
                for k in range(self.n + 1):
                    if k < self.n:
                        if k > 1:
                            dve.wait_ge(self.ready, self.base + k - 1)
                        dve.scalar_tensor_tensor(stage32[k % 2][:, :], self.x[:, k, :], col(self.gain, k),
                                                 rstd[:, :], ALU.mult, ALU.mult).then_inc(self.f32, 1)
                    if k:
                        dve.wait_ge(self.hi_made, self.base + k)
                        dve.tensor_tensor(self.lo[:, k - 1, :], stage32[(k - 1) % 2][:, :],
                                          self.hi[:, k - 1, :].bitcast(F32), ALU.subtract).then_inc(self.ready, 1)

        class LateNorm(Norm):

            def __init__(self, x, n, gain, total, gained_base):
                Norm.__init__(self, x, 0, gain, h_hi, h_lo, total)
                self.n, self.base = n, gained_base
                self.ready = gained

        def update_x(dve, unit, o, k, b, scale, squares, gain):
            dve.wait_ge(unit_done, unit + 1 + k)
            x = xT[:, o, :] if isinstance(k, int) else xT[:, bass.ds(o + k, 1), :].rearrange("p a t -> p (a t)")
            dve.scalar_tensor_tensor(x, bank(b), scale, x, ALU.mult, ALU.add).then_inc(x_updated, 1)
            counts["x"] += 1
            if squares:
                dve.wait_ge(x_updated, counts["x"] + k)
                if gain:
                    split_gained(dve, x, gain, o, k)
                add_square(dve, x, k)

        def update_loop(dve, base, banks, scale, squares, gain=None):
            if squares:
                clear_sum(dve)
            dve.wait_ge(x_updated, counts["x"])
            c0 = dict(counts)
            with dve.Fori(0, DT // 2) as i:
                for b in range(2):
                    update_x(dve, base + b, b, i * 2, banks[b], scale, squares, gain)
            done = dict(c0)
            done["x"] += DT
            if squares:
                done["sq"] += DT
                done["sum"] += DT
            if gain:
                done["gain"] += DT
            counts.update(done)

        SUMS = {"ffn1": 9, "mix": 18, "ffn2": 27, "ple": 36, "block2": 45}
        XS = {"ffn1_0": 2, "out1": 18, "ffn2_0": 26, "ple": 42, "out2": 50}

        class FeedForward:

            signals = [sem(f"ffn_{s}") for s in ("gate", "sigmoid", "silu", "scaled", "mid", "mid_hi", "mid_ready")]

            def __init__(self, number, norm, x_base, next_gain):
                self.name, self.norm, self.x_base, self.next_gain = f"ffn{number}", norm, x_base, next_gain
                self.first = 2 * FH * (number - 1)
                self.gate, self.sig, self.silu, self.scaled, self.mid, self.mid_hi, self.ready = FeedForward.signals

            def tensor(self, pe):
                for half in range(2):
                    up, down, f0 = BASE[f"{self.name}_up{half}"], BASE[f"{self.name}_down{half}"], self.first + half * FH

                    def hidden_tile(f, k, first):
                        pe.wait_ge(lo_ready, up + 2 * f + 1 + k * 2)
                        if f0 + f > 0:
                            pe.wait_ge(self.gate, f0 + f + k)
                        linear(pe, bank(0), up, h_hi, h_lo, DT, chunk_ready=self.norm.ready if first else None,
                               ready_base=self.norm.base)
                        if first:
                            self.norm.tensor(pe)
                        pe.wait_ge(lo_ready, up + 2 * f + 2 + k * 2)
                        if f0 + f > 0:
                            pe.wait_ge(self.mid, f0 + f + k)
                        linear(pe, bank(1), up + 1, h_hi, h_lo, DT)

                    if half == 0:
                        pe.wait_ge(x_updated, self.x_base - 1)
                    hidden_tile(0, 0, half == 0)
                    with pe.Fori(0, FH - 1) as i:
                        hidden_tile(1, i, False)

                    def down_tile(b, k, first=False):
                        pe.wait_ge(lo_ready, down + b + 1 + k)
                        pe.wait_ge(x_updated, self.x_base + 8 * half + b - 1 + k)
                        linear(pe, bank(2 + b % 2), down + b, mid_hi, mid_lo, FH,
                               chunk_ready=self.ready if first else None, ready_base=f0)

                    down_tile(0, 0, True)
                    down_tile(1, 0)
                    with pe.Fori(0, DT // 2 - 1) as i:
                        for b in range(2):
                            down_tile(2 + b, i * 2)

            def scalar(self, act):
                self.norm.factor(act)
                act.preload_act_table(ACT.Sigmoid)
                for half in range(2):
                    up, f0 = BASE[f"{self.name}_up{half}"], self.first + half * FH

                    def sigmoid(f, k):
                        act.wait_ge(self.gate, f0 + f + 1 + k)
                        if f0 + f:
                            act.wait_ge(self.silu, f0 + f + k)
                        act.activation(sig[:, :], gate32[:, :], ACT.Sigmoid).then_inc(self.sig, 1)

                    split_hi_to(act, up + 2)
                    sigmoid(0, 0)
                    with act.Fori(0, FH - 1) as i:
                        split_hi(act, up + 2, i * 2)
                        split_hi(act, up + 3, i * 2)
                        sigmoid(1, i)
                    next_hi[0] = up + 2 * FH
                    split_hi_to(act, up + 2 * FH + DT)

            def vector(self, dve):
                dve.wait_ge(self.norm.rstd, self.norm.i + 1)
                for half in range(2):
                    up, f0 = BASE[f"{self.name}_up{half}"], self.first + half * FH
                    if half:
                        dve.wait_ge(unit_done, up)
                    with dve.Fori(0, FH) as i:
                        dve.wait_ge(unit_done, up + 1 + i * 2)
                        dve.tensor_tensor(gate32[:, :], bank(0), rstd[:, :], ALU.mult).then_inc(self.gate, 1)
                        dve.wait_ge(self.sig, f0 + 1 + i)
                        dve.wait_ge(self.gate, f0 + 1 + i)
                        dve.tensor_tensor(silu[:, :], sig[:, :], gate32[:, :], ALU.mult).then_inc(self.silu, 1)
                        dve.wait_ge(self.silu, f0 + 1 + i)
                        dve.tensor_tensor(silu[:, :], silu[:, :], rstd[:, :], ALU.mult).then_inc(self.scaled, 1)
                        dve.wait_ge(unit_done, up + 2 + i * 2)
                        dve.wait_ge(self.scaled, f0 + 1 + i)
                        dve.tensor_tensor(mid32[:, :], silu[:, :], bank(1), ALU.mult).then_inc(self.mid, 1)
                        hi = mid_hi[:, bass.ds(i, 1), :].rearrange("p a t -> p (a t)")
                        lo = mid_lo[:, bass.ds(i, 1), :].rearrange("p a t -> p (a t)")
                        dve.wait_ge(self.mid, f0 + 1 + i)
                        dve.tensor_copy(hi, mid32[:, :]).then_inc(self.mid_hi, 1)
                        dve.wait_ge(self.mid_hi, f0 + 1 + i)
                        dve.tensor_tensor(lo, mid32[:, :], hi.bitcast(F32), ALU.subtract).then_inc(self.ready, 1)
                        dve.wait_ge(self.ready, f0 + 1 + i)
                    update_loop(dve, BASE[f"{self.name}_down{half}"], (2, 3), 0.5, half == 1,
                                self.next_gain if half else None)

        norm_ffn1 = LateNorm(xT, DT, "ffn1_norm", SUMS["ffn1"], 0)
        ffn1 = FeedForward(1, norm_ffn1, XS["ffn1_0"], None)
        norm_mix = Norm(xT, DT, "mix_norm", h_hi, h_lo, SUMS["mix"])

        class SoftmaxAttention:

            def __init__(self, name, q, k, v, prob, probT, scale, causal, extra):
                self.q, self.k, self.v, self.prob, self.probT = q, k, v, prob, probT
                self.scale, self.causal, self.extra = scale, causal, extra
                (self.scores, self.maxed, self.neg, self.exped, self.inv, self.normed, self.turned, self.copied0,
                 self.copied1, self.summed, self.out_hi, self.out) = (
                    sem(f"{name}_{x}") for x in ("scores", "maximum", "negated", "exped", "inverse", "normed",
                                                 "transposed", "copied_even", "copied_odd", "outputs", "out_hi", "out"))

            def keys(self, t):
                return (t + 1) * P if self.causal else T

            def queries(self, s):
                return s * P if self.causal else 0

            def tensor_scores(self, pe, h):
                for t in range(TT):
                    n = self.keys(t)
                    if h:
                        pe.wait_ge(self.exped, TT * (h - 1) + t + 1)
                    (qh, ql), (kh, kl) = self.q(h), self.k(h)
                    rows = slice(t * P, (t + 1) * P)
                    last = products(pe, bank(t, n), [(qh[:, rows], ql[:, rows], kh[:, 0:n], kl[:, 0:n])],
                                    stop=not self.extra)
                    if self.extra:
                        pe.matmul(bank(t, n), sel[:, h, :], nf_hi[:, 0:n], start=False, stop=False)
                        pe.matmul(bank(t, n), sel[:, h, :], nf_lo[:, 0:n], start=False, stop=False)
                        last = pe.matmul(psum[:, 512 * t + t * P:512 * t + n], ident_r, mask_qk, start=False, stop=True)
                    last.then_inc(self.scores, 1)

            def tensor_outputs(self, pe, h):
                pe.wait_ge(self.normed, TT * (h + 1))
                for s in range(TT + 1):
                    if s < TT:
                        n = TT * h + s
                        if n >= 2:
                            pe.wait_ge((self.copied0, self.copied1)[s % 2], n // 2)
                        t0 = s if self.causal else 0
                        for t in range(t0, TT):
                            last = pe.transpose(psum[:, 512 * (4 + s % 2) + t * P:512 * (4 + s % 2) + (t + 1) * P],
                                                self.prob[h % 2][:, t, s * P:(s + 1) * P], ident)
                        last.then_inc(self.turned, 1)
                    if s:
                        r = s - 1
                        pe.wait_ge((self.copied0, self.copied1)[r % 2], 2 * h + r // 2 + 1)
                        if r == 0 and h >= 2:
                            pe.wait_ge(self.out, h - 1)
                        a = self.queries(r)
                        pe.matmul(psum[:, 512 * (6 + h % 2) + a:512 * (7 + h % 2)], self.v(h, r),
                                  self.probT[r % 2][:, a:T], start=r == 0, stop=r == TT - 1,
                                  ).then_inc(self.summed, 1)

            def tensor(self, pe, ready, next_unit):
                for semaphore, value in ready:
                    pe.wait_ge(semaphore, value)
                self.tensor_scores(pe, 0)
                for h in range(HEADS):
                    if h + 1 < HEADS:
                        self.tensor_scores(pe, h + 1)
                    else:
                        next_unit(pe, 0)
                    self.tensor_outputs(pe, h)

            def cols(self, h, what):
                a = 12 * (h % 2) + 4 * what
                return small[:, a:a + 4]

            def scalar(self, act, last_scores=None):
                for h in range(HEADS):
                    act.wait_ge(self.neg, h + 1)
                    if h >= 2:
                        act.wait_ge(self.turned, TT * (h - 1))
                    for t in range(TT):
                        n = self.keys(t)
                        act.activation(self.prob[h % 2][:, t, 0:n], bank(t, n), ACT.Exp, scale=self.scale,
                                       bias=self.cols(h, 0)[:, t:t + 1],
                                       accum_out=self.cols(h, 1)[:, t:t + 1]).then_inc(self.exped, 1)
                    if h == HEADS - 1 and last_scores is not None:
                        last_scores(act)
                    self.scalar_outputs(act, h)

            def copy_transpose(self, act, h, s):
                n = TT * h + s
                act.wait_ge(self.turned, n + 1)
                if n >= 2:
                    act.wait_ge(self.summed, n - 1)
                a = self.queries(s)
                src, dst = psum[:, 512 * (4 + s % 2) + a:512 * (5 + s % 2)], self.probT[s % 2][:, a:T]
                act.activation(dst, src, ACT.Copy).then_inc((self.copied0, self.copied1)[s % 2], 1)

            def scalar_outputs(self, act, h):
                for s in range(TT):
                    self.copy_transpose(act, h, s)
                act.wait_ge(self.summed, TT * (h + 1))
                rows = slice(HD * (h % 2), HD * (h % 2) + HD)
                src = bank(6 + h % 2)[rows, :]
                if self.extra:
                    act.activation(ya_hi[rows, h // 2, :], src, ACT.Copy).then_inc(self.out_hi, 1)
                else:
                    act.activation(y32[rows, h // 2, :], src, ACT.Copy).then_inc(self.out, 1)

            def vector_maximum(self, dve, h):
                top = self.cols(h, 0)
                if h >= 2:
                    dve.wait_ge(self.exped, TT * (h - 1))
                for t in range(TT):
                    dve.wait_ge(self.scores, TT * h + t + 1)
                    dve.tensor_reduce(top[:, t:t + 1], bank(t, self.keys(t)), AXX, ALU.max).then_inc(self.maxed, 1)
                dve.wait_ge(self.maxed, TT * (h + 1))
                dve.tensor_scalar(top, top, -self.scale, None, ALU.mult).then_inc(self.neg, 1)

            def vector(self, dve):
                self.vector_maximum(dve, 0)
                for h in range(HEADS):
                    total, inverse = self.cols(h, 1), self.cols(h, 2)
                    dve.wait_ge(self.exped, TT * (h + 1))
                    dve.reciprocal(inverse, total).then_inc(self.inv, 1)
                    dve.wait_ge(self.inv, h + 1)
                    for t in range(TT):
                        row = self.prob[h % 2][:, t, 0:self.keys(t)]
                        dve.tensor_scalar(row, row, inverse[:, t:t + 1], None, ALU.mult).then_inc(self.normed, 1)
                    if h + 1 < HEADS:
                        self.vector_maximum(dve, h + 1)
                    if h:
                        self.vector_outputs(dve, h - 1)
                self.vector_outputs(dve, HEADS - 1)

            def vector_outputs(self, dve, h):
                if self.extra:
                    rows = slice(HD * (h % 2), HD * (h % 2) + HD)
                    dve.wait_ge(self.out_hi, h + 1)
                    dve.tensor_tensor(ya_lo[rows, h // 2, :], bank(6 + h % 2)[rows, :],
                                      ya_hi[rows, h // 2, :].bitcast(F32), ALU.subtract).then_inc(self.out, 1)

        fox = SoftmaxAttention("fox", lambda h: (q_hi[:, h, :], q_lo[:, h, :]),
                               lambda h: (k_hi[:, h // 2, :], k_lo[:, h // 2, :]),
                               lambda h, s: v32[:, s, (h // 2) * P:(h // 2 + 1) * P],
                               (prob, prob_odd), probT, 1.0, True, True)

        class FoxProjections:

            def __init__(self):
                (self.sq, self.sum, self.std, self.rstd, self.f32, self.hi, self.ready, self.cleared, self.sel_landed,
                 self.sel, self.z, self.az, self.e, self.l, self.log, self.F, self.nf_hi, self.nf, self.v) = (
                    sem(f"fox_{x}") for x in ("square", "head_sum", "std", "rstd", "f32", "hi", "qk_ready", "cleared",
                                              "sel_landed", "sel", "z", "abs", "exp", "ln", "log", "F", "nf_hi",
                                              "nf", "v"))

            def tensor(self, pe, norm):
                for j in range(9):
                    if j < 8:
                        u = BASE["fox_q"] + j
                        pe.wait_ge(lo_ready, u + 1)
                        if j >= 4:
                            pe.wait_ge(self.f32, j - 3)
                        linear(pe, bank(j % 4), u, h_hi, h_lo, DT, chunk_ready=norm.ready if j == 0 else None,
                               ready_base=norm.base)
                    if j:
                        pe.wait_ge(self.sq, j)
                        if j > 2:
                            pe.wait_ge(self.std, j - 2)
                        pe.matmul(bank(4 + (j - 1) % 2), block_ones, head_sq[(j - 1) % 2][:, :], start=True,
                                  stop=True).then_inc(self.sum, 1)
                u = BASE["fox_f"]
                pe.wait_ge(lo_ready, u + 1)
                linear(pe, bank(6), u, h_hi, h_lo, DT)
                pe.wait_ge(self.std, 8)
                pe.wait_ge(self.z, 1)
                for j in range(4):
                    pe.wait_ge(lo_ready, BASE["fox_v"] + j + 1)
                    linear_by_token(pe, (4, 5, 7, 6), BASE["fox_v"] + j, j, 4, h_hi, h_lo)

            def scalar(self, act):
                act.wait_ge(self.sel_landed, 16)
                act.activation(sel[:, :, :], sel32[:, :, :], ACT.Copy).then_inc(self.sel, 1)
                act.wait_ge(constr_landed, 16)
                act.activation(constr[:, :, :], constr32[:, :, :], ACT.Copy).then_inc(constr_ready, 1)
                for j in range(9):
                    if j < 8:
                        u = BASE["fox_q"] + j
                        split_hi_to(act, u + 2)
                        act.wait_ge(unit_done, u + 1)
                        if j >= 2:
                            act.wait_ge(self.sum, j - 1)
                        act.activation(head_sq[j % 2][:, :], bank(j % 4), ACT.Square).then_inc(self.sq, 1)
                    if j:
                        i = j - 1
                        act.wait_ge(self.sum, i + 1)
                        act.activation(std[:, :], bank(4 + i % 2), ACT.Ln, scale=1.0 / HD,
                                       bias=col("eps")).then_inc(self.std, 1)
                        act.wait_ge(self.std, i + 1)
                        if i:
                            act.wait_ge(self.f32, i)
                        act.activation(rstd[:, :], std[:, :], ACT.Exp, scale=-0.5).then_inc(self.rstd, 1)
                        act.wait_ge(self.f32, i + 1)
                        src = stage32[i % 2]
                        if i < 4:
                            act.wait_ge(self.cleared, 4)
                            act.activation(q_hi[0:HD, 2 * i, :], src[0:HD, :], ACT.Copy).then_inc(self.hi, 1)
                            act.activation(q_hi[HD:P, 2 * i + 1, :], src[HD:P, :], ACT.Copy).then_inc(self.hi, 1)
                        else:
                            act.activation(k_hi[:, i - 4, :], src[:, :], ACT.Copy).then_inc(self.hi, 1)
                u = BASE["fox_f"]
                split_hi_to(act, u + 2)
                act.wait_ge(self.z, 1)
                act.activation(prob[:, 1, :], prob[:, 0, :], ACT.Abs).then_inc(self.az, 1)
                act.wait_ge(self.az, 1)
                act.activation(prob[:, 2, :], prob[:, 1, :], ACT.Exp, scale=-1.0).then_inc(self.e, 1)
                act.wait_ge(self.e, 1)
                act.activation(prob[:, 3, :], prob[:, 2, :], ACT.Ln, bias=1.0).then_inc(self.l, 1)
                split_hi_to(act, BASE["fox_v"] + 4)
                act.wait_ge(unit_done, BASE["fox_v"] + 4)
                act.wait_ge(self.sel, 1)
                for t, b in enumerate((4, 5, 7, 6)):
                    act.activation(v32[:, t, :], bank(b), ACT.Copy).then_inc(self.v, 1)
                split_hi_to(act, BASE["fox_v"] + 6)

            def vector(self, dve):
                for i, q in enumerate((q_hi, q_lo)):
                    even = q[HD:P, :, :].rearrange("p (j e) t -> p j e t", e=2)[:, :, 0, :]
                    odd = q[0:HD, :, :].rearrange("p (j e) t -> p j e t", e=2)[:, :, 1, :]
                    for half in (even, odd):
                        dve.memset(half.bitcast(F32), 0.0).then_inc(self.cleared, 1)
                dve.tensor_scalar(small[:, 31:32], col("q_norm"), HD ** -0.5, None, ALU.mult).then_inc(self.cleared, 1)
                for i in range(8):
                    dve.wait_ge(self.rstd, i + 1)
                    if i == 0:
                        dve.wait_ge(self.cleared, 5)
                    gain = small[:, 31:32] if i < 4 else col("k_norm")
                    dve.scalar_tensor_tensor(stage32[i % 2][:, :], bank(i % 4), gain, rstd[:, :],
                                             ALU.mult, ALU.mult).then_inc(self.f32, 1)
                    src = stage32[i % 2]
                    if i < 4:
                        dve.wait_ge(self.hi, 2 * i + 2)
                        for e, rows in enumerate((slice(0, HD), slice(HD, P))):
                            dve.tensor_tensor(q_lo[rows, 2 * i + e, :], src[rows, :],
                                              q_hi[rows, 2 * i + e, :].bitcast(F32), ALU.subtract).then_inc(self.ready, 1)
                        dve.wait_ge(self.ready, 2 * i + 2)
                    else:
                        dve.wait_ge(self.hi, 8 + i - 3)
                        dve.tensor_tensor(k_lo[:, i - 4, :], src[:, :], k_hi[:, i - 4, :].bitcast(F32),
                                          ALU.subtract).then_inc(self.ready, 1)
                        dve.wait_ge(self.ready, 8 + i - 3)
                dve.wait_ge(unit_done, BASE["fox_f"] + 1)
                dve.tensor_scalar(prob[:, 0, :], bank(6), col("forget_bias"), None, ALU.add).then_inc(self.z, 1)
                dve.wait_ge(self.z, 1)
                dve.wait_ge(self.l, 1)
                dve.wait_ge(constr_ready, 1)
                dve.scalar_tensor_tensor(probT[0][:, :], prob[:, 0, :], 0.0, prob[:, 3, :], ALU.min,
                                         ALU.subtract).then_inc(self.log, 1)
                dve.memset(prob[:, 1, :], 1.0).then_inc(self.log, 1)
                dve.wait_ge(self.log, 2)
                dve.tensor_tensor_scan(probT[1][:, :], prob[:, 1, :], probT[0][:, :], 0.0, ALU.mult,
                                       ALU.add).then_inc(self.F, 1)
                dve.wait_ge(self.F, 1)
                dve.tensor_scalar(nf_hi[:, :], probT[1][:, :], -1.0, None, ALU.mult).then_inc(self.nf_hi, 1)
                dve.wait_ge(self.nf_hi, 1)
                dve.scalar_tensor_tensor(nf_lo[:, :], probT[1][:, :], -1.0, nf_hi[:, :].bitcast(F32), ALU.mult,
                                         ALU.subtract).then_inc(self.nf, 1)
                dve.wait_ge(self.nf, 1)

        foxp = FoxProjections()

        class StickProjections:

            def __init__(self):
                self.hi, self.ready, self.v = (sem(f"stick_{x}") for x in ("hi", "qk_ready", "v"))

            def tensor_unit(self, pe, j):
                u = BASE["sb_q"] + j
                pe.wait_ge(lo_ready, u + 1)
                pe.wait_ge(*((fox.exped, TT * (HEADS - 1) + j + 1) if j < 4 else (self.ready, 2 * (j - 3))))
                linear(pe, bank(j % 4), u, h_hi, h_lo, DT)

            def tensor(self, pe):
                for j in range(1, 8):
                    self.tensor_unit(pe, j)
                for j in range(4):
                    pe.wait_ge(fox.out, HEADS)
                    pe.wait_ge(lo_ready, BASE["sb_v"] + j + 1)
                    linear_by_token(pe, (4, 5, 6, 7), BASE["sb_v"] + j, j, 4, h_hi, h_lo)
                    if j == 0:
                        pe.wait_ge(self.ready, 12)
                        stick.tensor_z(pe, 0)

            def scalar(self, act):
                for j in range(8):
                    u = BASE["sb_q"] + j
                    split_hi_to(act, u + 2)
                    act.wait_ge(unit_done, u + 1)
                    if j < 4:
                        act.activation(q_hi[0:HD, 2 * j, :], bank(j)[0:HD, :], ACT.Copy,
                                       scale=HD ** -0.5).then_inc(self.hi, 1)
                        act.activation(q_hi[HD:P, 2 * j + 1, :], bank(j)[HD:P, :], ACT.Copy,
                                       scale=HD ** -0.5).then_inc(self.hi, 1)
                    else:
                        act.activation(k_hi[:, j - 4, :], bank(j % 4), ACT.Copy).then_inc(self.hi, 1)
                split_hi_to(act, BASE["sb_v"] + 3)
                stick.scalar_softplus(act, 0)
                split_hi_to(act, BASE["sb_v"] + 4)
                act.wait_ge(unit_done, BASE["sb_v"] + 4)
                for t in range(TT):
                    act.activation(v32[:, t, :], bank(4 + t), ACT.Copy).then_inc(self.v, 1)
                split_hi_to(act, BASE["sb_v"] + 6)

            def vector(self, dve):
                for j in range(4):
                    dve.wait_ge(self.hi, 2 * j + 2)
                    for e, rows in enumerate((slice(0, HD), slice(HD, P))):
                        dve.scalar_tensor_tensor(q_lo[rows, 2 * j + e, :], bank(j)[rows, :], HD ** -0.5,
                                                 q_hi[rows, 2 * j + e, :].bitcast(F32), ALU.mult,
                                                 ALU.subtract).then_inc(self.ready, 1)
                for j in range(4):
                    dve.wait_ge(self.hi, 9 + j)
                    dve.tensor_tensor(k_lo[:, j, :], bank(j), k_hi[:, j, :].bitcast(F32),
                                      ALU.subtract).then_inc(self.ready, 1)

        stickp = StickProjections()

        class StickBreaking:

            def __init__(self):
                (self.z, self.az, self.e, self.l, self.sp, self.masked, self.hi, self.ready, self.sums, self.weight,
                 self.outputs, self.out_hi, self.out) = (
                    sem(f"stick_{x}") for x in ("z", "abs", "exp", "ln", "softplus", "masked", "sp_hi", "sp_ready",
                                                "sums", "weight", "outputs", "out_hi", "out"))

            def zone(self, h, s, a=0, n=None):
                o = 512 * 3 * (h % 2) + AREA[s] + a
                return psum[:, o:o + (T - s * P - a if n is None else n)]

            def whole(self, h):
                return psum[:, 512 * 3 * (h % 2):512 * 3 * (h % 2) + AREA_COLS]

            def tensor_z(self, pe, h):
                if h >= 2:
                    pe.wait_ge(self.weight, h - 1)
                for s in range(TT):
                    keys = slice(s * P, (s + 1) * P)
                    last = products(pe, self.zone(h, s), [(k_hi[:, h // 2, keys], k_lo[:, h // 2, keys],
                                                           q_hi[:, h, s * P:T], q_lo[:, h, s * P:T])],
                                    start=s != 3, stop=True, skip_group_check=True)
                last.then_inc(self.z, 1)

            def tensor_sums(self, pe, h):
                pe.wait_ge(self.ready, h + 1)
                for s in range(TT):
                    for j in range(s, TT):
                        tri = neg_tri if j == s else neg_ones
                        for sp in (sp_hi, sp_lo):
                            pe.matmul(self.zone(h, s, (j - s) * P), tri, sp[:, AREA[j]:AREA[j] + T - j * P],
                                      start=False, stop=False, skip_group_check=True)
                    last = pe.matmul(self.zone(h, s, 0, P), ident_r, mask_kq, start=False, stop=True,
                                     skip_group_check=True)
                last.then_inc(self.sums, 1)

            def tensor_outputs(self, pe, h):
                pe.wait_ge(self.weight, h + 1)
                if h >= 2:
                    pe.wait_ge(self.out, h - 1)
                for s in range(TT):
                    last = pe.matmul(psum[:, 512 * (6 + h % 2) + s * P:512 * (7 + h % 2)],
                                     v32[:, s, (h // 2) * P:(h // 2 + 1) * P],
                                     weight[h % 2][:, AREA[s]:AREA[s] + T - s * P], start=s == 0, stop=s == TT - 1)
                last.then_inc(self.outputs, 1)

            def tensor(self, pe):
                pe.wait_ge(stickp.v, TT)
                for h in range(HEADS):
                    if h + 1 < HEADS:
                        self.tensor_z(pe, h + 1)
                    self.tensor_sums(pe, h)
                    if h:
                        self.tensor_outputs(pe, h - 1)
                self.tensor_outputs(pe, HEADS - 1)

            def scalar_softplus(self, act, h):
                buf = soft[h % 2]
                act.preload_act_table_set("natural_log_exp_and_others")
                act.wait_ge(self.z, h + 1)
                if h >= 2:
                    act.wait_ge(self.ready, h - 1)
                act.activation(buf[:, :], self.whole(h), ACT.Abs).then_inc(self.az, 1)
                act.wait_ge(self.az, h + 1)
                act.activation(buf[:, :], buf[:, :], ACT.Exp, scale=-1.0).then_inc(self.e, 1)
                act.wait_ge(self.e, h + 1)
                act.activation(buf[:, :], buf[:, :], ACT.Ln, bias=1.0).then_inc(self.l, 1)

            def scalar_weight(self, act, h):
                act.wait_ge(self.sums, h + 1)
                if h >= 2:
                    act.wait_ge(self.outputs, h - 1)
                act.activation(weight[h % 2][:, :], self.whole(h), ACT.Exp).then_inc(self.weight, 1)

            def scalar_output(self, act, h):
                act.wait_ge(self.outputs, h + 1)
                rows = slice(HD * (h % 2), HD * (h % 2) + HD)
                act.activation(yb_hi[rows, h // 2, :], bank(6 + h % 2)[rows, :], ACT.Copy).then_inc(self.out_hi, 1)

            def scalar(self, act):
                for h in range(HEADS):
                    if h:
                        self.scalar_softplus(act, h)
                    if h:
                        self.scalar_weight(act, h - 1)
                    if h >= 2:
                        self.scalar_output(act, h - 2)
                self.scalar_weight(act, HEADS - 1)
                self.scalar_output(act, HEADS - 2)
                self.scalar_output(act, HEADS - 1)

            def vector_output(self, dve, h):
                dve.wait_ge(self.out_hi, h + 1)
                rows = slice(HD * (h % 2), HD * (h % 2) + HD)
                dve.tensor_tensor(yb_lo[rows, h // 2, :], bank(6 + h % 2)[rows, :],
                                  yb_hi[rows, h // 2, :].bitcast(F32), ALU.subtract).then_inc(self.out, 1)

            def vector(self, dve):
                for h in range(HEADS):
                    buf = soft[h % 2]
                    dve.wait_ge(self.l, h + 1)
                    dve.scalar_tensor_tensor(buf[:, :], self.whole(h), 0.0, buf[:, :], ALU.max,
                                             ALU.add).then_inc(self.sp, 1)
                    dve.wait_ge(self.sp, h + 1)
                    for s in range(TT):
                        diagonal = buf[:, AREA[s]:AREA[s] + P]
                        dve.tensor_tensor(diagonal, diagonal, before, ALU.mult).then_inc(self.masked, 1)
                    dve.wait_ge(self.masked, 4 * h + 4)
                    if h:
                        dve.wait_ge(self.sums, h)
                    dve.tensor_copy(sp_hi[:, :], buf[:, :]).then_inc(self.hi, 1)
                    dve.wait_ge(self.hi, h + 1)
                    dve.tensor_tensor(sp_lo[:, :], buf[:, :], sp_hi[:, :].bitcast(F32),
                                      ALU.subtract).then_inc(self.ready, 1)
                    if h >= 2:
                        self.vector_output(dve, h - 2)
                self.vector_output(dve, HEADS - 2)
                self.vector_output(dve, HEADS - 1)

        stick = StickBreaking()

        class Merge:

            signals = [sem(f"merge_{x}") for x in ("opened", "gate", "part", "sum", "hi", "ready")]

            def __init__(self, n, bias, x_base, before, squares, next_gain):
                self.next_gain = next_gain
                self.base, self.out_base = BASE[f"merge{n}"], BASE[f"out{n}"]
                self.bias, self.x_base, self.before, self.squares = bias, x_base, before, squares
                self.first = DT * (n - 1)
                self.opened, self.gate, self.part, self.sum, self.hi, self.ready = Merge.signals

            def tensor(self, pe):
                def tile(b, k, before=()):
                    u, side = self.base + 3 * b, 4 * (b % 2)
                    pe.wait_ge(self.opened, self.first // DT * (DT + 2) + b + 1 + k * 2)
                    for g in range(2):
                        pe.wait_ge(lo_ready, u + g + 1 + k * 6)
                        linear(pe, bank(side + g), u + g, h_hi, h_lo, DT)
                    pe.wait_ge(lo_ready, u + 3 + k * 6)
                    for s, v in before:
                        pe.wait_ge(s, v)
                    linear(pe, bank(side + 2), u + 2, ya_hi, ya_lo, 4, signal=False)
                    linear(pe, bank(side + 3), u + 2, yb_hi, yb_lo, 4, first=4)

                tile(0, 0, self.before)
                tile(1, 0)
                with pe.Fori(0, DT // 2 - 1) as i:
                    for b in range(2):
                        tile(2 + b, i)

                def project(b, k, first=False):
                    pe.wait_ge(lo_ready, self.out_base + b + 1 + k)
                    pe.wait_ge(x_updated, self.x_base + b - 1 + k)
                    linear(pe, bank(b % 2), self.out_base + b, merged_hi, merged_lo, DT,
                           chunk_ready=self.ready if first else None, ready_base=self.first)

                project(0, 0, True)
                project(1, 0)
                with pe.Fori(0, DT // 2 - 1) as i:
                    for b in range(2):
                        project(2 + b, i * 2)

            def scalar(self, act):
                split_hi_to(act, self.base + 2)
                with act.Fori(0, DT // 2) as i:
                    for b in range(2):
                        u = self.base + 3 * b
                        for g in range(2):
                            act.wait_ge(unit_done, u + g + 1 + i * 6)
                            act.activation(gate[b][:, g, :], bank(4 * b + g), ACT.Sigmoid,
                                           bias=gate_bias[b][:, g:g + 1]).then_inc(self.gate, 1)
                            split_hi(act, u + g + 2, i * 6)
                        split_hi(act, u + 4, i * 6)
                next_hi[0] = self.base + 26
                split_hi_to(act, self.out_base + DT)

            def open_tile(self, dve, b, o, k):
                c = VEC[self.bias] + 2 * o
                src = vec[:, c:c + 2] if isinstance(k, int) else vec[:, bass.ds(c + k * 2, 2)]
                dve.tensor_copy(gate_bias[b][:, :], src).then_inc(self.opened, 1)

            def open_first(self, dve):
                for b in range(2):
                    self.open_tile(dve, b, b, 0)

            def vector(self, dve):
                with dve.Fori(0, DT // 2) as i:
                    for b in range(2):
                        u = self.base + 3 * b
                        dve.wait_ge(unit_done, u + 3 + i * 6)
                        dve.wait_ge(self.gate, 2 * self.first + 2 * b + 2 + i * 4)
                        for g in range(2):
                            dve.tensor_tensor(gated[:, g, :], gate[b][:, g, :], bank(4 * b + 2 + g),
                                              ALU.mult).then_inc(self.part, 1)
                        dve.wait_ge(self.part, 2 * self.first + 2 * b + 2 + i * 4)
                        dve.tensor_tensor(sum32[:, :], gated[:, 0, :], gated[:, 1, :], ALU.add).then_inc(self.sum, 1)
                        dve.wait_ge(self.sum, self.first + b + 1 + i * 2)
                        hi = merged_hi[:, bass.ds(i * 2 + b, 1), :].rearrange("p a t -> p (a t)")
                        lo = merged_lo[:, bass.ds(i * 2 + b, 1), :].rearrange("p a t -> p (a t)")
                        dve.tensor_copy(hi, sum32[:, :]).then_inc(self.hi, 1)
                        dve.wait_ge(self.hi, self.first + b + 1 + i * 2)
                        dve.tensor_tensor(lo, sum32[:, :], hi.bitcast(F32), ALU.subtract).then_inc(self.ready, 1)
                        dve.wait_ge(self.ready, self.first + b + 1 + i * 2)
                        self.open_tile(dve, b, b + 2, i * 2)
                update_loop(dve, self.out_base, (0, 1), 1.0, self.squares, self.next_gain)

        merge1 = Merge(1, "no_bias", XS["out1"], [(fox.out, HEADS), (stick.out, HEADS)], True, "ffn2_norm")
        norm_ffn2 = LateNorm(xT, DT, "ffn2_norm", SUMS["ffn2"], DT)
        ffn2 = FeedForward(2, norm_ffn2, XS["ffn2_0"], "ple_norm")


        class LayerEmbedding:

            def __init__(self, norm, x_base):
                self.norm, self.x_base, self.base = norm, x_base, BASE["ple"]
                self.landed, self.hi, self.p_ready, self.gate, self.sig, self.add = (
                    sem(f"ple_{x}") for x in ("landed", "p_hi", "p_ready", "gate", "sigmoid", "add"))

            def tensor(self, pe):
                def tile(b, k, first=False):
                    pe.wait_ge(lo_ready, self.base + b + 1 + k)
                    pe.wait_ge(x_updated, self.x_base + b - 1 + k)
                    linear(pe, bank(b % 2), self.base + b, h_hi, h_lo, DT, signal=False,
                           chunk_ready=self.norm.ready if first else None, ready_base=self.norm.base)
                    if first:
                        pe.wait_ge(self.p_ready, 1)
                    linear(pe, bank(2 + b % 2), self.base + b, p_hi, p_lo, 2, first=DT)

                tile(0, 0, True)
                self.norm.tensor(pe)
                tile(1, 0)
                with pe.Fori(0, DT // 2 - 1) as i:
                    for b in range(2):
                        tile(2 + b, i * 2)

            def load(self, act):
                act.wait_ge(merge1.ready, DT)
                act.dma_start(p32[:, :, :], p_in).then_inc(self.landed, 16)

            def scalar(self, act):
                act.wait_ge(self.landed, 16)
                act.activation(p_hi[:, :, :], p32[:, :, :], ACT.Copy).then_inc(self.hi, 1)

                self.norm.factor(act)
                act.preload_act_table(ACT.Sigmoid)

                def sigmoid(b, k):
                    act.wait_ge(self.gate, b + 1 + k)
                    act.activation(ple_gate[b][:, :], ple_gate[b][:, :], ACT.Sigmoid).then_inc(self.sig, 1)

                with act.Fori(0, DT // 2 - 1) as i:
                    for b in range(2):
                        split_hi(act, self.base + 2 + b, i * 2)
                        sigmoid(b, i * 2)
                next_hi[0] = self.base + DT
                for b in range(2):
                    sigmoid(b, DT - 2)

            def vector(self, dve):
                dve.wait_ge(self.hi, 1)
                dve.tensor_tensor(p_lo[:, :, :], p32[:, :, :], p_hi[:, :, :].bitcast(F32),
                                  ALU.subtract).then_inc(self.p_ready, 1)
                dve.wait_ge(self.norm.rstd, self.norm.i + 1)
                clear_sum(dve)
                dve.wait_ge(x_updated, counts["x"])
                c0 = dict(counts)
                with dve.Fori(0, DT // 2) as i:
                    for b in range(2):
                        dve.wait_ge(unit_done, self.base + b + 1 + i * 2)
                        dve.tensor_tensor(ple_gate[b][:, :], bank(b), rstd[:, :], ALU.mult).then_inc(self.gate, 1)
                        dve.wait_ge(self.sig, b + 1 + i * 2)
                        dve.tensor_tensor(ple_add[:, :], ple_gate[b][:, :], bank(2 + b), ALU.mult).then_inc(self.add, 1)
                        dve.wait_ge(self.add, b + 1 + i * 2)
                        x = xT[:, bass.ds(i * 2 + b, 1), :].rearrange("p a t -> p (a t)")
                        dve.tensor_tensor(x, x, ple_add[:, :], ALU.add).then_inc(x_updated, 1)
                        counts["x"] += 1
                        dve.wait_ge(x_updated, counts["x"] + i * 2)
                        add_square(dve, x, i * 2)
                counts.update({"x": c0["x"] + DT, "sq": c0["sq"] + DT, "sum": c0["sum"] + DT})

        norm_ple = LateNorm(xT, DT, "ple_norm", SUMS["ple"], 2 * DT)
        ple = LayerEmbedding(norm_ple, XS["ple"])
        norm_block2 = Norm(xT, DT, "g_norm", h_hi, h_lo, SUMS["block2"])

        norm_cq = Norm(lat32, 3, "g_cq", cq_hi, cq_lo, SUMS["block2"] + 4)
        norm_ckv = Norm(ckv32, 2, "g_ckv", ckv_hi, ckv_lo, SUMS["block2"] + 7)

        class LatentProjections:

            def __init__(self):
                (self.rope_landed, self.tabs, self.lat, self.q32, self.k32, self.sq, self.sum, self.std, self.rstd,
                 self.cos, self.sin, self.rot, self.f32, self.hi, self.ready, self.v) = (
                    sem(f"latent_{x}") for x in ("rope_landed", "tabs", "latents", "q32", "k32", "square", "sum",
                                                 "std", "rstd", "cos", "sin", "rotated", "f32", "hi", "ready", "v"))

            def tensor(self, pe):
                u = BASE["mla_cq"]
                for j in range(6):
                    pe.wait_ge(lo_ready, u + j + 1)
                    linear(pe, bank(j), u + j, h_hi, h_lo, DT, chunk_ready=norm_block2.ready if j == 0 else None,
                           ready_base=norm_block2.base)
                    if j == 3:
                        norm_cq.tensor(pe)
                norm_ckv.tensor(pe)
                pe.wait_ge(norm_cq.ready, norm_cq.base + 3)
                pe.wait_ge(norm_ckv.ready, norm_ckv.base + 2)
                pe.wait_ge(self.lat, 6)
                for h in range(HEADS + 1):
                    if h < HEADS:
                        u = BASE["mla_qk"] + h
                        pe.wait_ge(lo_ready, u + 1)
                        if h >= 2:
                            pe.wait_ge(self.q32, h - 1)
                            pe.wait_ge(self.k32, h - 1)
                        b = 2 * (h % 2)
                        linear(pe, bank(b), u, cq_hi, cq_lo, 3, signal=False)
                        linear(pe, bank(b + 1), u, ckv_hi, ckv_lo, 2, first=3)
                    if h:
                        for m in (2 * h - 2, 2 * h - 1):
                            pe.wait_ge(self.sq, m + 1)
                            if m >= 2:
                                pe.wait_ge(self.std, m - 1)
                            pe.matmul(bank(4 + m % 2), ones, head_sq[m % 2][:, :], start=True,
                                      stop=True).then_inc(self.sum, 1)
                pe.wait_ge(self.q32, HEADS)
                pe.wait_ge(self.k32, HEADS)
                pe.wait_ge(lo_ready, BASE["mla_v"] + 1)
                linear_by_token(pe, (0, 1, 2, 3), BASE["mla_v"], 0, 1, ckv_hi, ckv_lo)

            def load(self, act):
                act.wait_ge(merge1.ready, DT)
                act.dma_start(rope[:, :, :], rope_in).then_inc(self.rope_landed, 16)

            def scalar(self, act):
                u = BASE["mla_cq"]
                for j in range(6):
                    split_hi_to(act, u + j + 2)
                    act.wait_ge(unit_done, u + j + 1)
                    dst = (lat32[:, j, :] if j < 3 else ckv32[:, j - 3, :]) if j < 5 else krope[:, :]
                    act.activation(dst, bank(j), ACT.Copy).then_inc(self.lat, 1)
                    if j == 3:
                        split_hi_to(act, u + 6)
                        norm_cq.scalar(act)
                norm_ckv.scalar(act)
                for m in range(2 * HEADS + 2):
                    if m >= 2:
                        i = m - 2
                        act.wait_ge(self.f32, i + 1)
                        dst = (mq_hi, mk_hi)[i % 2]
                        act.activation(dst[:, i // 2, :], head_out[i % 3][:, :], ACT.Copy).then_inc(self.hi, 1)
                    if m < 2 * HEADS:
                        h, p = m // 2, m % 2
                        u = BASE["mla_qk"] + h
                        split_hi_to(act, u + 2 + p)
                        if p == 0:
                            act.wait_ge(unit_done, u + 1)
                            if m == 0:
                                act.wait_ge(norm_cq.ready, norm_cq.base + 3)
                            else:
                                act.wait_ge(self.sin, 2 * m - 2)
                            act.activation(head32[0][:, :], bank(2 * (h % 2)), ACT.Copy).then_inc(self.q32, 1)
                        act.wait_ge(*((self.k32, h + 1) if p else (self.q32, h + 1)))
                        if m >= 2:
                            act.wait_ge(self.sum, m - 1)
                        act.activation(head_sq[p][:, :], head32[p][:, :], ACT.Square).then_inc(self.sq, 1)
                    if 1 <= m <= 2 * HEADS:
                        i = m - 1
                        act.wait_ge(self.sum, i + 1)
                        act.activation(std[:, :], bank(4 + i % 2), ACT.Ln, scale=1.0 / QKD,
                                       bias=col("eps")).then_inc(self.std, 1)
                        act.wait_ge(self.std, i + 1)
                        if i:
                            act.wait_ge(self.f32, i)
                        act.activation(rstd[:, :], std[:, :], ACT.Exp, scale=-0.5).then_inc(self.rstd, 1)
                split_hi_to(act, BASE["mla_v"] + 1)
                act.wait_ge(unit_done, BASE["mla_v"] + 1)
                act.wait_ge(self.ready, 2 * HEADS)
                for t in range(TT):
                    act.activation(mv32[:, t, :], bank(t), ACT.Copy).then_inc(self.v, 1)
                split_hi_to(act, BASE["mla_v"] + 3)

            def vector(self, dve):
                dve.wait_ge(self.rope_landed, 16)
                for i, (which, gain) in enumerate(((0, "g_qn"), (1, "g_qn"), (0, "g_kn"), (1, "g_kn"))):
                    dve.tensor_scalar(tabs[:, i, :], rope[:, which, :], col(gain), None, ALU.mult).then_inc(self.tabs, 1)
                for norm, n, x in ((norm_cq, 3, lat32), (norm_ckv, 2, ckv32)):
                    clear_sum(dve)
                    for k in range(n):
                        dve.wait_ge(self.lat, (0 if n == 3 else 3) + k + 1)
                        add_square(dve, x[:, k, :])
                    norm.vector(dve)
                dve.wait_ge(self.tabs, 4)
                dve.wait_ge(self.lat, 6)
                dve.wait_ge(norm_ckv.ready, norm_ckv.base + 2)
                for m in range(2 * HEADS + 2):
                    if m < 2 * HEADS:
                        self.rotate(dve, m)
                    if 1 <= m <= 2 * HEADS:
                        i = m - 1
                        dve.wait_ge(self.rstd, i + 1)
                        dve.wait_ge(self.rot, i + 1)
                        out32 = head_out[i % 3]
                        dve.tensor_tensor(out32[:, :], out32[:, :], rstd[:, :], ALU.mult).then_inc(self.f32, 1)
                    if m >= 2:
                        i = m - 2
                        hi, lo = ((mq_hi, mq_lo), (mk_hi, mk_lo))[i % 2]
                        dve.wait_ge(self.hi, i + 1)
                        dve.tensor_tensor(lo[:, i // 2, :], head_out[i % 3][:, :], hi[:, i // 2, :].bitcast(F32),
                                          ALU.subtract).then_inc(self.ready, 1)

            def rotate(self, dve, m):
                h, p = m // 2, m % 2
                if p == 0:
                    dve.wait_ge(unit_done, BASE["mla_qk"] + h + 1)
                    if h:
                        dve.wait_ge(self.sq, m)
                        dve.wait_ge(self.cos, m)
                        dve.wait_ge(self.sin, 2 * m)
                    dve.tensor_tensor(head32[1][:, :], bank(2 * (h % 2) + 1), krope[:, :],
                                      ALU.add).then_inc(self.k32, 1)
                out32 = head_out[m % 3]
                dve.wait_ge(*((self.k32, h + 1) if p else (self.q32, h + 1)))
                if m >= 3:
                    dve.wait_ge(self.ready, m - 2)
                dve.tensor_tensor(out32[:, :], head32[p][:, :], tabs[:, 2 * p, :], ALU.mult).then_inc(self.cos, 1)
                sw, rows = swapped[p], slice(64, P)
                if m >= 2:
                    dve.wait_ge(self.rot, m - 1)
                for a in (64, 96):
                    dve.tensor_tensor(sw[160 - a:192 - a, :], head32[p][a:a + 32, :], tabs[a:a + 32, 2 * p + 1, :],
                                      ALU.mult).then_inc(self.sin, 1)
                dve.wait_ge(self.cos, m + 1)
                dve.wait_ge(self.sin, 2 * m + 2)
                dve.tensor_tensor(out32[rows, :], out32[rows, :], sw[rows, :], ALU.add).then_inc(self.rot, 1)

        latent = LatentProjections()
        mla = SoftmaxAttention("mla", lambda h: (mq_hi[:, h, :], mq_lo[:, h, :]),
                               lambda h: (mk_hi[:, h, :], mk_lo[:, h, :]),
                               lambda h, s: mv32[:, s, (h // 2) * P:(h // 2 + 1) * P],
                               (mprob, mprob_odd), mprobT, QKD ** -0.5, False, False)

        class AttentionGate:

            def __init__(self):
                self.sig, self.silu, self.f32, self.hi, self.ready = (
                    sem(f"attention_gate_{x}") for x in ("sigmoid", "silu", "f32", "hi", "ready"))

            def tensor(self, pe, j):
                u = BASE["mla_z"] + j
                pe.wait_ge(lo_ready, u + 1)
                pe.wait_ge(mla.exped, TT * (HEADS - 1) + j + 1)
                linear(pe, bank(j), u, h_hi, h_lo, DT)

            def scalar(self, act):
                for j in range(5):
                    if j < 4:
                        act.wait_ge(unit_done, BASE["mla_z"] + j + 1)
                        act.wait_ge(*((self.silu, j - 1) if j >= 2 else (filters.ready, 7 + j)))
                        act.activation(stage32[j % 2][:, :], bank(j), ACT.Sigmoid).then_inc(self.sig, 1)
                    if j == 3:
                        split_hi_to(act, BASE["mla_z"] + 7)
                    if j:
                        act.wait_ge(self.f32, j)
                        act.activation(ya_hi[:, j - 1, :], std[:, :], ACT.Copy).then_inc(self.hi, 1)

            def vector(self, dve):
                dve.wait_ge(mla.out, HEADS)
                for j in range(4):
                    dve.wait_ge(self.sig, j + 1)
                    dve.tensor_tensor(square[:, :], stage32[j % 2][:, :], bank(j), ALU.mult).then_inc(self.silu, 1)
                    dve.wait_ge(self.silu, j + 1)
                    dve.tensor_tensor(std[:, :], square[:, :], y32[:, j, :], ALU.mult).then_inc(self.f32, 1)
                    dve.wait_ge(self.hi, j + 1)
                    dve.tensor_tensor(ya_lo[:, j, :], std[:, :], ya_hi[:, j, :].bitcast(F32),
                                      ALU.subtract).then_inc(self.ready, 1)
                    dve.wait_ge(self.ready, j + 1)

        attention_gate = AttentionGate()

        class Filters:

            TILES = [(0, 0), (0, 1), (1, 2), (1, 3), (0, 2), (0, 3), (1, 0), (1, 1)]
            EARLY = [(0, 1), (2, 3), (4,), (5, 6, 7)]
            BANKS = [6, 0, 2, 6, 0, 2, 0, 6]

            def __init__(self):
                (self.landed, self.skip_landed, self.layer, self.arg, self.turn, self.act, self.tile, self.f32,
                 self.bias, self.hi, self.ready, self.even, self.spec) = (
                    sem(f"filter_{x}") for x in ("landed", "skip_landed", "layer", "argument", "turn", "sine", "tile",
                                                 "f32", "bias", "hi", "ready", "even", "spectrum"))

            def load(self, act):
                act.wait_ge(mla.scores, TT * HEADS)
                for dst, src in ((posT[:, :], pos_in), (wf1[:, :], wf1_in), (wf2[:, :], wf2_in), (wf3[:, :], wf3_in),
                                 (decay[:, :, :], decay_in)):
                    act.dma_start(dst, src).then_inc(self.landed, 16)

            def load_skip(self, act):
                act.wait_ge(mla.summed, TT * HEADS)
                act.dma_start(hyb[:, :, :], hyb_in).then_inc(self.skip_landed, 16)

            def kf(self, o, i):
                if o and i < 5:
                    return kf_early[i][0][:, :], kf_early[i][1][:, :]
                return kf_hi[:, i, :], kf_lo[:, i, :]

            def tensor_layer(self, pe, i):
                if i == 0:
                    pe.wait_ge(self.landed, 80)
                    pe.wait_ge(mla.copied0, 2 * HEADS)
                    pe.matmul(bank(4)[0:64, :], wf1[:, :], posT[:, :], start=True, stop=True).then_inc(self.layer, 1)
                else:
                    pe.wait_ge(self.act, 1)
                    pe.matmul(bank(4)[0:64, :], wf2[:, :], hid[0][:, :], start=True, stop=True).then_inc(self.layer, 1)

            def tensor_tile(self, pe, o, i):
                n = 8 * o + i
                if n == 0:
                    pe.wait_ge(self.act, 2)
                elif n == 1:
                    pe.wait_ge(mla.copied1, 2 * HEADS)
                else:
                    pe.wait_ge(self.f32, n - 1)
                side, t = self.TILES[i]
                c = (2 * o + side) * T
                pe.matmul(bank(4 + n % 2), hid[1][:, t * P:(t + 1) * P], wf3[:, c:c + T],
                          start=True, stop=True).then_inc(self.tile, 1)

            def tensor_unit(self, pe, o, m):
                n = 4 * o + m
                u = BASE["spectra"] + n
                pe.wait_ge(lo_ready, u + 1)
                before = [i for i in range(n) if self.BANKS[i] == self.BANKS[n]]
                if before:
                    pe.wait_ge(self.spec, 2 * before[-1] + 2)
                elif n == 0:
                    pe.wait_ge(mla.out, HEADS)
                else:
                    pe.wait_ge(attention_gate.silu, self.BANKS[n] + 2)
                for odd in range(2):
                    for c, (w_hi, w_lo) in enumerate(weight_chunks(u, 4 * odd, 4)):
                        i = 4 * odd + c
                        if m == 0:
                            pe.wait_ge(self.ready, 8 * o + i + 1)
                        k_hi_, k_lo_ = self.kf(o, i)
                        last = products(pe, bank(self.BANKS[n] + odd), [(w_hi, w_lo, k_hi_, k_lo_)],
                                        start=c == 0, stop=c == 3)
                last.then_inc(unit_done, 1)

            def tensor(self, pe):
                for o in range(2):
                    for m in range(4):
                        self.tensor_unit(pe, o, m)
                        if o == 0:
                            for i in self.EARLY[m]:
                                self.tensor_tile(pe, 1, i)

            def scalar_sine(self, act, i):
                act.wait_ge(self.turn, 5 * i + 5)
                act.activation(hid[i][:, :], sumsq[0:64, :], ACT.Sin).then_inc(self.act, 1)

            def scalar_tile(self, act, o, i):
                n = 8 * o + i
                act.wait_ge(self.f32, n + 1)
                if i == 0:
                    act.wait_ge(self.bias, o + 1)
                if o and i >= 5:
                    act.wait_ge(unit_done, BASE["spectra"] + 4)
                act.activation(self.kf(o, i)[0], stage32[n % 2][:, :], ACT.Copy).then_inc(self.hi, 1)

            def scalar_unit(self, act, o, m):
                n = 4 * o + m
                u = BASE["spectra"] + n
                split_hi_to(act, u + 2)
                act.wait_ge(unit_done, u + 1)
                part, j = m // 2, m % 2
                act.activation(spec[o][:, 4 * part + j, :], bank(self.BANKS[n]), ACT.Copy).then_inc(self.even, 1)

            def scalar(self, act):
                for m in range(4):
                    self.scalar_unit(act, 0, m)
                    for i in self.EARLY[m]:
                        self.scalar_tile(act, 1, i)
                for m in range(4):
                    self.scalar_unit(act, 1, m)

            def vector_layer(self, dve, i):
                a, r = rstd[0:64, :], sumsq[0:64, :]
                c1 = 6.28125
                dve.wait_ge(self.layer, i + 1)
                dve.tensor_scalar(a, bank(4)[0:64, :], col(f"b_f{i + 1}", p=64), col(f"freq_{i + 1}", p=64), ALU.add,
                                  ALU.mult).then_inc(self.arg, 1)
                dve.wait_ge(self.arg, i + 1)

                def turn(ins):
                    ins.then_inc(self.turn, 1)
                    counts["turn"] = counts.get("turn", 0) + 1
                    dve.wait_ge(self.turn, counts["turn"])

                if i:
                    dve.wait_ge(self.act, 1)
                turn(dve.tensor_scalar(r, a, 1.0 / (2 * math.pi), BIG, ALU.mult, ALU.add))
                turn(dve.tensor_scalar(r, r, BIG, None, ALU.subtract))
                turn(dve.scalar_tensor_tensor(a, r, -c1, a, ALU.mult, ALU.add))
                turn(dve.scalar_tensor_tensor(r, r, -(2 * math.pi - c1), a, ALU.mult, ALU.add))
                turn(dve.tensor_scalar(r, r, 3.1415925, -3.1415925, ALU.min, ALU.max))

            def vector_tile(self, dve, o, i):
                n = 8 * o + i
                if n >= 2:
                    dve.wait_ge(self.ready, n - 1)
                dve.wait_ge(self.tile, n + 1)
                f32 = stage32[n % 2]
                dve.tensor_tensor(f32[:, :], bank(4 + n % 2), decay[:, self.TILES[i][1], :],
                                  ALU.mult).then_inc(self.f32, 1)
                if i == 0:
                    dve.wait_ge(self.f32, n + 1)
                    dve.wait_ge(self.skip_landed, 16)
                    dve.tensor_tensor(f32[0:1, :], f32[0:1, :], hyb[0:1, o, :], ALU.add).then_inc(self.bias, 1)
                    dve.wait_ge(self.bias, o + 1)

            def vector_tile_lo(self, dve, o, i):
                n = 8 * o + i
                hi, lo = self.kf(o, i)
                dve.wait_ge(self.hi, n + 1)
                dve.tensor_tensor(lo, stage32[n % 2][:, :], hi.bitcast(F32), ALU.subtract).then_inc(self.ready, 1)

            def vector_tiles(self, dve, o, tiles):
                for j, i in enumerate(tiles):
                    self.vector_tile(dve, o, i)
                    if j:
                        self.vector_tile_lo(dve, o, i - 1)
                self.vector_tile_lo(dve, o, tiles[-1])

            def vector_unit(self, dve, o, m):
                n = 4 * o + m
                part, j = m // 2, m % 2
                low, high, odd = spec[o][:, 4 * part + j, :], spec[o][:, 4 * part + 2 + j, :], bank(self.BANKS[n] + 1)
                dve.wait_ge(self.even, n + 1)
                a, b = (odd, low) if part else (low, odd)
                dve.tensor_tensor(high, a, b, ALU.subtract).then_inc(self.spec, 1)
                dve.wait_ge(self.spec, 2 * n + 1)
                dve.tensor_tensor(low, low, odd, ALU.add).then_inc(self.spec, 1)

            def vector(self, dve):
                for m in range(4):
                    self.vector_unit(dve, 0, m)
                    self.vector_tiles(dve, 1, self.EARLY[m])
                for m in range(4):
                    self.vector_unit(dve, 1, m)

        filters = Filters()

        def gate_and_filters_tensor(pe):
            filters.tensor_layer(pe, 0)
            attention_gate.tensor(pe, 1)
            filters.tensor_layer(pe, 1)
            attention_gate.tensor(pe, 2)
            for i in range(2):
                filters.tensor_tile(pe, 0, i)
            attention_gate.tensor(pe, 3)
            for i in range(2, 8):
                filters.tensor_tile(pe, 0, i)
            filters.tensor(pe)

        def gate_and_filters_scalar(act):
            filters.load_skip(act)
            split_hi_to(act, BASE["mla_z"] + 3)
            filters.scalar_sine(act, 0)
            split_hi_to(act, BASE["mla_z"] + 4)
            filters.scalar_sine(act, 1)
            for i in range(8):
                if i in (2, 6):
                    split_hi_to(act, BASE["mla_z"] + (5 if i == 2 else 6))
                filters.scalar_tile(act, 0, i)
            attention_gate.scalar(act)
            filters.scalar(act)

        def gate_and_filters_vector(dve):
            for i in range(2):
                filters.vector_layer(dve, i)
            filters.vector_tiles(dve, 0, range(8))
            attention_gate.vector(dve)
            filters.vector(dve)

        class HyenaInputs:

            def __init__(self):
                (self.mid, self.left, self.conv, self.turned, self.hi, self.copied, self.ready, self.sig, self.silu,
                 self.x2z) = (
                    sem(f"hyena_{x}") for x in ("middle", "left", "conv", "transposed", "v_hi", "x1", "v_ready",
                                                "sigmoid", "silu", "x2z"))

            def target(self, j):
                return conv[j % 2][:, :] if j < 8 else x2z[:, j - 8, :]

            def tensor(self, pe):
                for j in range(17):
                    if j < 16:
                        u = BASE["hy_in"] + j
                        pe.wait_ge(lo_ready, u + 1)
                        if j < 4:
                            pe.wait_ge(filters.spec, 14 if j < 2 else 12)
                        elif j < 15:
                            pe.wait_ge(self.conv, j - 3)
                        if j == 15:
                            pe.wait_ge(self.conv, 12)
                        linear(pe, bank(j % 4), u, h_hi, h_lo, DT)
                    if 1 <= j <= 8:
                        i = j - 1
                        pe.wait_ge(self.conv, i + 1)
                        if i == 0:
                            pe.wait_ge(filters.spec, 16)
                        if i >= 2:
                            pe.wait_ge(*((self.ready, i - 1) if i < 6 else (self.copied, i - 5)))
                        for t in range(TT):
                            last = pe.transpose(psum[:, 512 * (4 + i % 2) + t * P:512 * (4 + i % 2) + (t + 1) * P],
                                                conv[i % 2][:, t * P:(t + 1) * P], ident)
                        last.then_inc(self.turned, 1)

            def by_token(self, i, x):
                return x[:, :, (i % 4) * P:(i % 4 + 1) * P]

            def turned_bank(self, i):
                return bank(4 + i % 2).rearrange("p (t c) -> p t c", t=TT)

            def scalar(self, act):
                for j in range(17):
                    if j < 12:
                        split_hi_to(act, BASE["hy_in"] + j + 2)
                        act.wait_ge(unit_done, BASE["hy_in"] + j + 1)
                        if 2 <= j < 8:
                            act.wait_ge(self.turned, j - 1)
                        if j == 0:
                            act.wait_ge(filters.ready, 16)
                        act.activation(self.target(j), bank(j % 4), ACT.Identity, scale=col("w_short", 3 * j + 1),
                                       bias=col("b_short", j)).then_inc(self.mid, 1)
                    elif j < 16:
                        i = j - 12
                        split_hi_to(act, BASE["hy_in"] + j + 2)
                        act.wait_ge(unit_done, BASE["hy_in"] + j + 1)
                        if i >= 2:
                            act.wait_ge(self.silu, i - 1)
                        act.activation(stage32[i % 2][:, :], bank(j % 4), ACT.Sigmoid).then_inc(self.sig, 1)
                    if 1 <= j <= 8:
                        i = j - 1
                        act.wait_ge(self.turned, i + 1)
                        dst = self.by_token(i, v_hi if i < 4 else x1tok)
                        act.activation(dst, self.turned_bank(i), ACT.Copy).then_inc(self.hi if i < 4 else self.copied, 1)

            def vector(self, dve):
                for j in range(17):
                    if j < 12:
                        dst, b = self.target(j), bank(j % 4)
                        dve.wait_ge(self.mid, j + 1)
                        dve.scalar_tensor_tensor(dst[:, 1:T], b[:, 0:T - 1], col("w_short", 3 * j), dst[:, 1:T],
                                                 ALU.mult, ALU.add).then_inc(self.left, 1)
                        dve.wait_ge(self.left, j + 1)
                        dve.scalar_tensor_tensor(dst[:, 0:T - 1], b[:, 1:T], col("w_short", 3 * j + 2), dst[:, 0:T - 1],
                                                 ALU.mult, ALU.add).then_inc(self.conv, 1)
                    elif j < 16:
                        i = j - 12
                        if i == 0:
                            dve.wait_ge(self.conv, 12)
                        else:
                            dve.wait_ge(self.x2z, i)
                        dve.wait_ge(self.sig, i + 1)
                        dve.tensor_tensor(square[:, :], stage32[i % 2][:, :], bank(j % 4), ALU.mult).then_inc(self.silu, 1)
                        dve.wait_ge(self.silu, i + 1)
                        dve.tensor_tensor(x2z[:, i, :], x2z[:, i, :], square[:, :], ALU.mult).then_inc(self.x2z, 1)
                    if 1 <= j <= 4:
                        i = j - 1
                        dve.wait_ge(self.hi, i + 1)
                        dve.tensor_tensor(self.by_token(i, v_lo), self.turned_bank(i),
                                          self.by_token(i, v_hi).bitcast(F32), ALU.subtract).then_inc(self.ready, 1)

        hyena_in = HyenaInputs()

        class LongConvolution:

            signals = [sem(f"long_{x}") for x in ("products", "f32", "hi", "ready", "back", "gated", "gated_hi", "out")]

            def __init__(self, o):
                self.o = o
                self.prod, self.f32, self.hi, self.ready, self.back, self.out32, self.out_hi, self.out = LongConvolution.signals

            def tensor(self, pe, before):
                for s, v in before:
                    pe.wait_ge(s, v)
                for j in range(4):
                    u = BASE[f"fwd{self.o}"] + j
                    pe.wait_ge(lo_ready, u + 1)
                    if j >= 2:
                        pe.wait_ge(self.prod, 16 * self.o + 4 * (j - 1))
                    b = 2 * (j % 2)
                    linear(pe, bank(b), u, v_hi, v_lo, 4, signal=False,
                           chunk_ready=self.out if self.o and j == 0 else None)
                    linear(pe, bank(b + 1), u, v_hi, v_lo, 4, first=4)
                for j in range(4):
                    u = BASE[f"inv{self.o}"] + j
                    s = u % 2
                    pe.wait_ge(lo_ready, u + 1)
                    pe.wait_ge(self.ready, 8 * self.o + 2 * j + 2)
                    if j == 0 and self.o:
                        pe.wait_ge(self.out32, 4)
                    for t in range(TT):
                        terms = []
                        for c in range(2):
                            y, cols = 4 * c + j, slice(t * P, (t + 1) * P)
                            if self.o == 0:
                                terms.append((whi[s][:, c * T + t * P:c * T + (t + 1) * P],
                                              wlo[s][:, c * T + t * P:c * T + (t + 1) * P], Y_hi[:, y, :], Y_lo[:, y, :]))
                            else:
                                terms.append((Y_hi[:, y, cols], Y_lo[:, y, cols],
                                              whi[s][:, c * T:(c + 1) * T], wlo[s][:, c * T:(c + 1) * T]))
                        last = products(pe, bank(4 + t), terms, start=j == 0, stop=j == 3)
                        if j == 3 and t < 3:
                            last.then_inc(self.back, 1)
                    last.then_inc(unit_done, 1)

            def scalar(self, act):
                for j in range(4):
                    split_hi_to(act, BASE[f"fwd{self.o}"] + j + 2)
                    for i in range(2):
                        act.wait_ge(self.f32, 8 * self.o + 2 * j + i + 1)
                        act.activation(Y_hi[:, 4 * i + j, :], stage32[i][:, :], ACT.Copy).then_inc(self.hi, 1)
                split_hi_to(act, BASE[f"inv{self.o}"] + 6)
                for j in range(4):
                    act.wait_ge(self.out32, 4 * self.o + j + 1)
                    act.activation(yb_hi[:, j, :], stage32[j % 2][:, :], ACT.Copy).then_inc(self.out_hi, 1)

            def vector(self, dve):
                for j in range(4):
                    dve.wait_ge(unit_done, BASE[f"fwd{self.o}"] + j + 1)
                    k_re, k_im = spec[self.o][:, j, :], spec[self.o][:, 4 + j, :]
                    u_re, u_im = bank(2 * (j % 2)), bank(2 * (j % 2) + 1)
                    if j:
                        dve.wait_ge(self.ready, 8 * self.o + 2 * j)
                    for i, (a, b) in enumerate(((k_re, u_re), (k_im, u_im), (k_re, u_im), (k_im, u_re))):
                        dve.tensor_tensor(prod[i][:, :], a, b, ALU.mult).then_inc(self.prod, 1)
                    dve.wait_ge(self.prod, 16 * self.o + 4 * j + 4)
                    for i, op in enumerate((ALU.subtract, ALU.add)):
                        dve.tensor_tensor(stage32[i][:, :], prod[2 * i][:, :], prod[2 * i + 1][:, :],
                                          op).then_inc(self.f32, 1)
                    for i in range(2):
                        dve.wait_ge(self.hi, 8 * self.o + 2 * j + i + 1)
                        dve.tensor_tensor(Y_lo[:, 4 * i + j, :], stage32[i][:, :],
                                          Y_hi[:, 4 * i + j, :].bitcast(F32), ALU.subtract).then_inc(self.ready, 1)
                dve.wait_ge(self.ready, 8 * self.o + 8)
                for j in range(5):
                    if j < 4:
                        dve.wait_ge(*((self.back, 3 * self.o + j + 1) if j < 3 else (unit_done, BASE[f"inv{self.o}"] + 4)))
                        if j >= 2:
                            dve.wait_ge(self.out, 4 * self.o + j - 1)
                        gate_tile = (x1tok, x2z)[self.o][:, j, :]
                        dve.tensor_tensor(stage32[j % 2][:, :], gate_tile, bank(4 + j), ALU.mult).then_inc(self.out32, 1)
                    if j:
                        dve.wait_ge(self.out_hi, 4 * self.o + j)
                        dve.tensor_tensor(yb_lo[:, j - 1, :], stage32[(j - 1) % 2][:, :],
                                          yb_hi[:, j - 1, :].bitcast(F32), ALU.subtract).then_inc(self.out, 1)
                dve.wait_ge(self.out, 4 * self.o + 4)

        long0, long1 = LongConvolution(0), LongConvolution(1)
        merge2 = Merge(2, "b_gate", XS["out2"], [(attention_gate.ready, 4), (long1.out, 8)], False, None)

        block = ctx.enter_context(nc.Block())
        stored = sem("stored")

        @block.sync
        def _(sp):
            load_unit(sp, 0, 0, "k", 0)
            for i in range(4):
                sp.dma_start(xT[:, 2 * i:2 * i + 2, :], x_in[:, 2 * i:2 * i + 2, :]).then_inc(x_landed[i], 16)
            load_unit(sp, 1, 0, "k", 1)
            stream_loads(sp)
            sp.wait_ge(x_updated, XS["out2"] + DT)
            sp.dma_start(out, xT[:, :, :]).then_inc(stored, 16)
            sp.wait_ge(stored, 16)

        @block.gpsimd
        def _(pool):
            stream_lo(pool)

        @block.scalar
        def _(act):
            act.dma_start(vec[:, :], vec_in).then_inc(vec_landed, 16)
            act.dma_start(constf[:, :, :], constf_in).then_inc(const_landed, 16)
            split_hi_to(act, 2)
            act.wait_ge(vec_landed, 16)
            ffn1.scalar(act)
            act.dma_start(sel32[:, :, :], sel_in).then_inc(foxp.sel_landed, 16)
            act.dma_start(constr32[:, :, :], constr_in).then_inc(constr_landed, 16)
            split_hi_to(act, BASE["fox_q"] + 2)
            norm_mix.scalar(act)
            foxp.scalar(act)
            fox.scalar(act)
            stickp.scalar(act)
            stick.scalar(act)
            merge1.scalar(act)
            split_hi_to(act, BASE["ffn2_up0"] + 2)
            ple.load(act)
            ffn2.scalar(act)
            split_hi_to(act, BASE["ple"] + 2)
            ple.scalar(act)
            latent.load(act)
            split_hi_to(act, BASE["mla_cq"] + 2)
            norm_block2.scalar(act)
            latent.scalar(act)
            mla.scalar(act, filters.load)
            gate_and_filters_scalar(act)
            hyena_in.scalar(act)
            long0.scalar(act)
            long1.scalar(act)
            merge2.scalar(act)

        @block.vector
        def _(dve):
            dve.memset(small[:, :], 0.0).then_inc(x_updated, 2)
            clear_sum(dve)
            dve.wait_ge(vec_landed, 16)
            for k in range(DT):
                if k % 2 == 0:
                    dve.wait_ge(x_landed[k // 2], 16)
                split_gained(dve, xT[:, k, :], "ffn1_norm", k)
                add_square(dve, xT[:, k, :])
            ffn1.vector(dve)
            norm_mix.vector(dve)
            foxp.vector(dve)
            fox.vector(dve)
            stickp.vector(dve)
            merge1.open_first(dve)
            stick.vector(dve)
            merge1.vector(dve)
            ffn2.vector(dve)
            ple.vector(dve)
            norm_block2.vector(dve)
            latent.vector(dve)
            mla.vector(dve)
            gate_and_filters_vector(dve)
            hyena_in.vector(dve)
            long0.vector(dve)
            merge2.open_first(dve)
            long1.vector(dve)
            merge2.vector(dve)

        @block.tensor
        def _(pe):
            ffn1.tensor(pe)
            norm_mix.tensor(pe)
            foxp.tensor(pe, norm_mix)
            fox.tensor(pe, [(constr_ready, 1), (foxp.sel, 1), (foxp.ready, 12), (foxp.nf, 1), (foxp.v, TT)],
                       stickp.tensor_unit)
            stickp.tensor(pe)
            stick.tensor(pe)
            merge1.tensor(pe)
            ffn2.tensor(pe)
            ple.tensor(pe)
            norm_block2.tensor(pe)
            latent.tensor(pe)
            mla.tensor(pe, [(latent.ready, 2 * HEADS), (latent.v, TT)], attention_gate.tensor)
            gate_and_filters_tensor(pe)
            hyena_in.tensor(pe)
            long0.tensor(pe, [(hyena_in.ready, 4), (hyena_in.silu, 4)])
            long1.tensor(pe, [])
            merge2.tensor(pe)


def _feature_units(w):
    kk, n = w.shape
    return w.reshape(kk // P, P, n // P, P).transpose(2, 1, 0, 3).reshape(n // P, P, kk)


def _token_units(w):
    kk, n = w.shape
    return w.reshape(kk // 256, 2, P, n).transpose(0, 2, 1, 3).reshape(kk // 256, P, 2 * n)


def _wide(u, n=1024):
    out = np.zeros((u.shape[0], P, n), np.float32)
    out[:, :, :u.shape[2]] = u
    return out


def _columns(v):
    return np.ascontiguousarray(v.reshape(-1, P).T)


def _rope_rows(a, axis=0):
    a = np.moveaxis(a, axis, 0)
    out = np.zeros((P,) + a.shape[1:], np.float32)
    out[0:64] = a[0:64]
    out[64:80] = a[64:80]
    out[96:112] = a[80:96]
    return np.moveaxis(out, 0, axis)


def _constants():
    i = np.arange(P)
    eye = np.eye(P, dtype=np.float32)
    blocks = (i[:, None] // HD == i[None, :] // HD).astype(np.float32)
    before = (i[:, None] < i[None, :]).astype(np.float32)
    constf = np.stack([eye, blocks, np.ones((P, P), np.float32), before], 1)
    tri = -(i[:, None] >= i[None, :]).astype(np.float32)
    mask_qk = np.where(i[None, :] > i[:, None], np.float32(NEG), np.float32(0))
    mask_kq = np.where(i[:, None] >= i[None, :], np.float32(NEG), np.float32(0))
    constr = np.stack([eye, tri, -np.ones((P, P), np.float32), mask_qk, mask_kq], 1)
    sel = np.zeros((P, HEADS, P), np.float32)
    for h in range(HEADS):
        sel[h, h, :] = 1
    pos = np.arange(T, dtype=np.float32)
    inv = (np.float32(ROPE_THETA) ** (-np.arange(0, ROPE, 2, dtype=np.float32) / np.float32(ROPE))).astype(np.float32)
    ang = (pos[:, None] * inv[None, :]).astype(np.float32)
    c, s = np.cos(ang).T, np.sin(ang).T
    rope = np.zeros((P, 2, T), np.float32)
    rope[0:64, 0] = 1
    rope[64:80, 0], rope[96:112, 0] = c, c
    rope[64:80, 1], rope[96:112, 1] = s, -s
    t = np.linspace(0.0, 1.0, T, dtype=np.float32)
    lo, hi = math.log(1e-2) / 1.5, math.log(1e-2) / 0.3
    deltas = np.abs(np.linspace(lo, hi, T, dtype=np.float32))
    parity = np.concatenate([np.arange(0, T, 2), np.arange(1, T, 2)])
    decay = np.exp(-t[:, None] * deltas).astype(np.float32)[parity].reshape(TT, P, T).transpose(1, 0, 2)
    bands = 16
    f = np.linspace(1e-4, bands - 1, bands, dtype=np.float32)
    a2 = (np.float32(2.0 * np.pi / T) * pos[:, None] * f[None, :]).astype(np.float32)
    posT = np.concatenate([t[:, None], np.cos(a2), -np.sin(a2)], -1).T.astype(np.float32)[:, parity]
    n = np.arange(T, dtype=np.float64)
    f = np.concatenate([np.arange(T // 2), T - 1 - np.arange(T // 2)])
    w = np.pi * (2 * f + 1) / (2 * T)
    th, th1 = n[:, None] * w, (n[:, None] + 1) * w
    fwd = np.concatenate([np.cos(th), -np.sin(th)], 1).astype(np.float32)
    neg = np.concatenate([np.cos(th1), np.sin(th1)], 1).astype(np.float32)
    inv_ = (np.concatenate([np.cos(th.T), -np.sin(th.T)], 0) / T).astype(np.float32)
    taps = np.concatenate([fwd[parity], neg[parity]], 0).reshape(8, P, 2 * T)
    lower = np.concatenate([np.arange(T // 2), T + np.arange(T // 2)])
    slots = [0, 1, 6, 7, 2, 3, 4, 5]
    spectra = _feature_units(taps[slots].reshape(2 * T, 2 * T)[:, lower])
    fu = _feature_units(fwd)
    fwd_units = np.concatenate([fu[0:4], fu[4:8]], 2)
    inv_units = np.concatenate([inv_[:T].reshape(4, P, T), inv_[T:].reshape(4, P, T)], 2)
    return constf, constr, sel, rope, decay, posT, spectra, fwd_units, inv_units


def kernel(**inputs):
    import concourse.bacc as _bacc
    from concourse.bass_utils import run_bass_kernel_spmd as _run

    g = {k: np.ascontiguousarray(v) for k, v in inputs.items()}
    constf, constr, sel, rope, decay, posT, spectra, fwd_units, inv_units = _constants()

    def cols(w, a, n):
        return w[:, a:a + n]

    ks, ds = [], []
    for n in ("1", "2"):
        up = np.stack([_feature_units(g[f"ffn{n}_w_gate"][0]), _feature_units(g[f"ffn{n}_w_up"][0])], 1)
        down = g[f"ffn{n}_w_down"][0]
        halves = []
        for half in range(2):
            halves.append(up[half * FH:(half + 1) * FH].reshape(2 * FH, P, D))
            ds.append(_feature_units(down[half * FH * P:(half + 1) * FH * P]))
        ks.append(halves)
    w1 = g["w_in"][0]
    fq, fk, fv, fl, sq, sk, sv, gf, gs = [w1[:, a:b] for a, b in zip(
        [0, 512, 1024, 1536, 1544, 2056, 2568, 3080, 4104], [512, 1024, 1536, 1544, 2056, 2568, 3080, 4104, 5128])]
    flp = np.zeros((D, P), np.float32)
    flp[:, 0:HEADS] = fl

    def merge_units(ga, gb, ba, bb):
        both = np.concatenate([_feature_units(ba), _feature_units(bb)], 2)
        return np.stack([_feature_units(ga), _feature_units(gb), both], 1).reshape(3 * DT, P, D)

    w2 = g["w_in_2"][0]
    edges = np.cumsum([0, 1536, 512, 384, 256, 32, 512, 1024, 1024])
    hy, zh, cq, ckv, kr, za, gh, ga = [w2[:, a:b] for a, b in zip(edges[:-1], edges[1:])]
    krp = np.zeros((D, P), np.float32)
    krp[:, 64:80], krp[:, 96:112] = kr[:, 0:16], kr[:, 16:32]
    uq = _rope_rows(g["w_uq_2"][0].reshape(384, HEADS, QKD), 2)
    ukv = g["w_ukv_2"][0].reshape(256, HEADS, P)
    uk = np.zeros((256, HEADS, P), np.float32)
    uk[:, :, 0:64] = ukv[:, :, 0:64]
    qk = np.concatenate([_feature_units(uq.reshape(384, D)), _feature_units(uk.reshape(256, D))], 2)
    uv = np.ascontiguousarray(ukv[:, :, 64:128]).reshape(256, 512)
    wk = np.concatenate([
        ks[0][0], ks[0][1],
        _feature_units(fq), _feature_units(fk), _feature_units(flp), _token_units(fv),
        _feature_units(sq), _feature_units(sk), _token_units(sv),
        merge_units(gf, gs, g["w_branch_fox"][0], g["w_branch_sb"][0]), _feature_units(g["w_out"][0]),
        ks[1][0], ks[1][1],
        _feature_units(cq), _feature_units(ckv), _feature_units(krp), _wide(qk), _token_units(uv), _feature_units(za),
        spectra, spectra, _feature_units(hy), _feature_units(zh),
        fwd_units, inv_units, fwd_units, inv_units,
        merge_units(ga, gh, g["w_attn_out_2"][0], g["w_hy_out_2"][0]), _feature_units(g["w_out_2"][0]),
    ], 0)
    assert wk.shape[0] == _at["k"]
    wd = np.concatenate(ds, 0)
    wp = np.concatenate([_feature_units(g["w_ple_gate"][0]), _feature_units(g["w_ple_proj"][0])], 2)

    vec = np.zeros((P, NVEC), np.float32)

    def put(name, v):
        vec[:v.shape[0], VEC[name]:VEC[name] + v.shape[1]] = v

    for name in ("ffn1_norm", "mix_norm", "ffn2_norm", "ple_norm"):
        put(name, _columns(g[name][0]))
    put("g_norm", _columns(g["g_norm_2"][0]))
    for name in ("q_norm", "k_norm"):
        put(name, np.concatenate([g[name][0], g[name][0]])[:, None])
    put("forget_bias", g["forget_bias"][0][:, None])
    bg = g["b_gate_2"][0]
    put("b_gate", np.stack([_columns(bg[D:]), _columns(bg[:D])], 2).reshape(P, 2 * DT))
    put("w_short", np.stack([_columns(g["w_short_2"][0][j]) for j in range(3)], 2).reshape(P, 36))
    put("b_short", _columns(g["b_short_2"][0]))
    put("g_cq", _columns(g["g_cq_2"][0]))
    put("g_ckv", _columns(g["g_ckv_2"][0]))
    for name in ("g_qn", "g_kn"):
        put(name, _rope_rows(g[name + "_2"][0])[:, None])
    for name in ("b_f1", "freq_1", "b_f2", "freq_2"):
        put(name, g[name + "_2"][0][:, None])
    vec[:, VEC["eps"]] = EPS

    arrays = {
        "wk": wk, "wd": wd, "wp": wp,
        "x": np.ascontiguousarray(g["x"][0].T).reshape(DT, P, T).transpose(1, 0, 2),
        "p": np.ascontiguousarray(g["p"][0, 0].T).reshape(2, P, T).transpose(1, 0, 2),
        "vec": vec, "constf": constf, "constr": constr, "sel": sel, "rope": rope, "decay": decay, "pos": posT,
        "wf1": g["w_f1_2"][0], "wf2": g["w_f2_2"][0], "wf3": g["w_f3_2"][0], "hyb": g["hy_bias_2"],
    }
    arrays = {k: np.ascontiguousarray(v) for k, v in arrays.items()}
    nc = _bacc.Bacc("TRN2", target_bir_lowering=False, num_devices=1)
    args = [nc.dram_tensor(f"{k}_dram", v.shape, F32, kind="ExternalInput").ap() for k, v in arrays.items()]
    args.append(nc.dram_tensor("out_dram", (P, DT, T), F32, kind="ExternalOutput").ap())
    build(nc, *args)
    r = _run(nc, [{f"{k}_dram": v for k, v in arrays.items()}], core_ids=[0])
    got = r.results[0]["out_dram"]
    return np.ascontiguousarray(got.transpose(1, 0, 2).reshape(D, T).T).reshape(1, T, D)
```

```python
from contextlib import ExitStack
import math

import numpy as np

import concourse.bass as bass
from concourse import mybir

F32 = mybir.dt.float32
F32R = mybir.dt.float32r
ACT = mybir.ActivationFunctionType
ALU = mybir.AluOpType
AXX = mybir.AxisListType.X

P = 128
D = 1024
T = 512
DT = D // P
TT = T // P
DFF = 2816
FH = DFF // P // 2
HEADS = 8
HD = 64
EPS = 1e-6
NEG = -1.0e30
BIG = float(1.5 * 2 ** 23)
ROPE_THETA = 10000.0
ROPE = 32
QKD = 96

WIDTH = {"k": 1024, "d": FH * P, "p": 10 * P}
SEGMENTS = [
    ("ffn1_up0", 22, "k"), ("ffn1_down0", 8, "d"), ("ffn1_up1", 22, "k"), ("ffn1_down1", 8, "d"),
    ("fox_q", 4, "k"), ("fox_k", 4, "k"), ("fox_f", 1, "k"), ("fox_v", 4, "k"),
    ("sb_q", 4, "k"), ("sb_k", 4, "k"), ("sb_v", 4, "k"), ("merge1", 24, "k"), ("out1", 8, "k"),
    ("ffn2_up0", 22, "k"), ("ffn2_down0", 8, "d"), ("ffn2_up1", 22, "k"), ("ffn2_down1", 8, "d"),
    ("ple", 8, "p"),
    ("mla_cq", 3, "k"), ("mla_ckv", 2, "k"), ("mla_kr", 1, "k"), ("mla_qk", 8, "k"), ("mla_v", 1, "k"),
    ("mla_z", 4, "k"),
    ("spectra", 8, "k"), ("hy_in", 8, "k"), ("long0", 8, "k"), ("long1", 8, "k"),
    ("merge2", 24, "k"), ("out2", 8, "k"),
]
BASE, RUNS = {}, []
_u = 0
_at = {"k": 0, "d": 0, "p": 0}
for _name, _n, _c in SEGMENTS:
    BASE[_name] = _u
    if RUNS and RUNS[-1][1] == _c:
        RUNS[-1][3] += _n
    else:
        RUNS.append([_u, _c, _at[_c], _n])
    _u += _n
    _at[_c] += _n
UNITS = _u

VEC = {}
_v = 0
for _name, _n in [("ffn1_norm", 8), ("mix_norm", 8), ("ffn2_norm", 8), ("ple_norm", 8), ("g_norm", 8),
                  ("q_norm", 1), ("k_norm", 1), ("forget_bias", 1), ("no_bias", 18), ("b_gate", 18),
                  ("w_short", 36), ("b_short", 12), ("g_cq", 3), ("g_ckv", 2),
                  ("g_qn", 1), ("g_kn", 1),
                  ("b_f1", 1), ("freq_1", 1), ("b_f2", 1), ("freq_2", 1), ("eps", 1)]:
    VEC[_name] = _v
    _v += _n
NVEC = _v



AREA = {0: 0, 1: 512, 3: 896, 2: 1024}
AREA_COLS = 1280


def build(nc, wk, wd, wp, x_in, p_in, vec_in, constf_in, constr_in, sel_in, rope_in, decay_in, pos_in,
          wf1_in, wf2_in, wf3_in, hyb_in, out):
    ctx = ExitStack()

    def sem(name):
        return ctx.enter_context(nc.semaphore(name))

    with ctx:
        def keep(name, shape, dt=F32):
            return ctx.enter_context(nc.sbuf_tensor(name, shape, dt))

        xT = keep("xT", [P, DT, T])
        h_hi = keep("h_hi", [P, DT, T], F32R)
        h_lo = keep("h_lo", [P, DT, T], F32R)
        raw = [keep(f"raw{s}", [P, FH * P]) for s in range(2)]
        whi = [keep(f"whi{s}", [P, FH * P], F32R) for s in range(2)]
        wlo = [keep(f"wlo{s}", [P, FH * P], F32R) for s in range(2)]
        vec = keep("vec", [P, NVEC])
        constf = keep("constf", [P, 4, P])
        constr = keep("constr", [P, 5, P], F32R)
        zsilu = nc.alloc_sbuf_tensor_at("zsilu", [P, T], F32, offset=nc.sbuf_base - 5 * P * 4)[:, :]
        scratch = keep("scratch", [P, 6 * T])
        sumsq, square, std, rstd, *stage32 = (scratch[:, i * T:(i + 1) * T] for i in range(6))
        small = keep("small", [P, 32])
        psum = ctx.enter_context(nc.psum_tensor("psum", [P, 8 * 512], F32))
        ident, block_ones, ones, before = (constf[:, i, :] for i in range(4))
        ident_r, neg_tri, neg_ones, mask_qk, mask_kq = (constr[:, i, :] for i in range(5))
        head_sq = [square, sumsq]
        first_square = [square, std]

        arena = ctx.enter_context(nc.sbuf_tensor("arena_end", [P, 109 * 256], F32))
        arena0 = nc.sbuf_base - 109 * 1024

        def at(kib, name, shape, dt=F32):
            return nc.alloc_sbuf_tensor_at(name, shape, dt, offset=arena0 + int(kib * 1024))

        mid_hi = at(0, "mid_hi", [P, FH, T], F32R)
        mid_lo = at(22, "mid_lo", [P, FH, T], F32R)
        sig = at(44, "sig", [P, T])
        silu = at(46, "silu", [P, T])
        mid32 = at(48, "mid32", [P, T])
        gate32 = at(50, "gate32", [P, T])
        constr32 = at(96, "constr32", [P, 5, P])
        ya_hi = at(0, "ya_hi", [P, 4, T], F32R)
        ya_lo = at(8, "ya_lo", [P, 4, T], F32R)
        yb_hi = at(16, "yb_hi", [P, 4, T], F32R)
        yb_lo = at(24, "yb_lo", [P, 4, T], F32R)
        q_hi = at(32, "q_hi", [P, HEADS, T], F32R)
        q_lo = at(48, "q_lo", [P, HEADS, T], F32R)
        k_hi = at(64, "k_hi", [P, 4, T], F32R)
        k_lo = at(72, "k_lo", [P, 4, T], F32R)
        v32 = at(80, "v32", [P, TT, T])
        prob = at(88, "prob", [P, TT, T])
        prob_odd = at(16, "prob_odd", [P, TT, T])
        probT = [at(96 + 2 * i, f"probT{i}", [P, T]) for i in range(2)]
        nf_hi = at(100, "nf_hi", [P, T], F32R)
        nf_lo = at(102, "nf_lo", [P, T], F32R)
        sel = at(104, "sel", [P, HEADS, P], F32R)
        sel32 = at(80, "sel32", [P, HEADS, P])
        soft = [at(88, "soft", [P, AREA_COLS]), scratch[:, 0:AREA_COLS]]
        sp_hi = at(93, "sp_hi", [P, AREA_COLS], F32R)
        sp_lo = at(98, "sp_lo", [P, AREA_COLS], F32R)
        weight = [at(103, "weight", [P, AREA_COLS]), scratch[:, 3 * T:3 * T + AREA_COLS]]
        merged_hi = at(32, "merged_hi", [P, DT, T], F32R)
        merged_lo = at(48, "merged_lo", [P, DT, T], F32R)
        gate = [at(64 + 4 * i, f"gate{i}", [P, 2, T]) for i in range(2)]
        gated = at(72, "gated", [P, 2, T])
        sum32 = at(76, "sum32", [P, T])
        gate_bias = [small[:, 24 + 2 * i:26 + 2 * i] for i in range(2)]
        p32 = at(64, "p32", [P, 2, T])
        p_hi = at(68, "p_hi", [P, 2, T], F32R)
        p_lo = at(72, "p_lo", [P, 2, T], F32R)
        ple_gate = [at(76 + 2 * i, f"ple_gate{i}", [P, T]) for i in range(2)]
        ple_add = at(80, "ple_add", [P, T])
        mq_hi = at(32, "mq_hi", [P, HEADS, T], F32R)
        mq_lo = at(48, "mq_lo", [P, HEADS, T], F32R)
        mk_hi = at(64, "mk_hi", [P, HEADS, T], F32R)
        mk_lo = at(80, "mk_lo", [P, HEADS, T], F32R)
        cq_hi = at(0, "cq_hi", [P, 3, T], F32R)
        cq_lo = at(6, "cq_lo", [P, 3, T], F32R)
        ckv_hi = at(12, "ckv_hi", [P, 2, T], F32R)
        ckv_lo = at(16, "ckv_lo", [P, 2, T], F32R)
        tabs = at(20, "tabs", [P, 4, T])
        krope = at(28, "krope", [P, T])
        lat32 = at(96, "lat32", [P, 3, T])
        ckv32 = at(64, "ckv32", [P, 2, T])
        head32 = [at(96 + 2 * i, f"head32_{i}", [P, T]) for i in range(2)]
        swapped = [at(100 + 6 * i, f"swapped{i}", [P, T]) for i in range(2)]
        rope = at(102, "rope", [P, 2, T])
        head_out = [*stage32, at(102, "head_out2", [P, T])]
        mv32 = at(96, "mv32", [P, TT, T])
        mprobT = [at(104 + 2 * i, f"mprobT{i}", [P, T]) for i in range(2)]
        mprob = at(16, "mprob", [P, TT, T])
        mprob_odd = at(0, "mprob_odd", [P, TT, T])
        y32 = at(24, "y32", [P, 4, T])
        spec = [at(48, "spec0", [P, 8, T]), at(32, "spec1", [P, 8, T])]
        Y_lo = at(48, "Y_lo", [P, 8, T], F32R)
        Y_hi = at(64, "Y_hi", [P, 8, T], F32R)
        kf_hi = at(64, "kf_hi", [P, 8, T], F32R)
        kf_lo = at(80, "kf_lo", [P, 8, T], F32R)
        kf_early = [[at(16 + 2 * i if i < 7 else 82 + 2 * i, f"kf_early{i}", [P, T], F32R) for i in (a, a + 1)]
                    for a in (0, 2, 4, 6, 8)]
        wf3 = at(32, "wf3", [64, 4 * T])
        decay = at(40, "decay", [P, TT, T])
        hid = [at(48, "hid0", [64, T]), at(102, "hid1", [64, T])]
        posT = at(50, "posT", [33, T])
        wf1 = at(52, "wf1", [33, 64])
        wf2 = at(53, "wf2", [64, 64])
        hyb = at(104, "hyb", [1, 2, T])
        v_hi, v_lo = yb_hi, yb_lo
        x1tok = at(80, "x1tok", [P, TT, T])
        x2z = at(88, "x2z", [P, TT, T])
        conv = [at(96 + 2 * i, f"conv{i}", [P, T]) for i in range(2)]
        prod = [at(100 + 2 * i, f"prod{i}", [P, T]) for i in range(4)]

        def bank(b, n=512):
            return psum[:, 512 * b:512 * b + n]

        def col(name, i=0, p=P):
            return vec[0:p, VEC[name] + i:VEC[name] + i + 1]

        landed = [sem(f"landed{s}") for s in range(2)]
        hi_ready = sem("hi_ready")
        lo_ready = sem("lo_ready")
        unit_done = sem("unit_done")

        def runs():
            yield from RUNS

        def load_unit(sp, u, k, c, a):
            if not (isinstance(k, int) and u < 2):
                sp.wait_ge(lo_ready, u + k - 1)
            src = {"k": wk, "d": wd, "p": wp}[c]
            w = WIDTH[c]
            row = src[a + k] if isinstance(k, int) else src[bass.ds(a + k, 1)].rearrange("a p n -> (a p) n")
            sp.dma_start(raw[u % 2][:, 0:w], row).then_inc(landed[u % 2], 16)

        def stream_loads(sp):
            for u, c, a, n in runs():
                head = 2 if u < 2 else 0
                with sp.Fori(0, (n - head) // 2) as i:
                    for b in range(2):
                        load_unit(sp, u + head + b, i * 2, c, a + head + b)
                if (n - head) % 2:
                    load_unit(sp, u + n - 1, 0, c, a + n - 1)

        def split_lo(pool, u, k, w):
            pool.wait_ge(hi_ready, u + 1 + k)
            s = u % 2
            pool.tensor_tensor(wlo[s][:, 0:w], raw[s][:, 0:w], whi[s][:, 0:w].bitcast(F32),
                               ALU.subtract).then_inc(lo_ready, 1)

        def stream_lo(pool, first, last):
            for u0, c, a, n in runs():
                u, n = max(u0, first), min(u0 + n, last) - max(u0, first)
                if n > 1:
                    with pool.Fori(0, n // 2) as i:
                        for b in range(2):
                            split_lo(pool, u + b, i * 2, WIDTH[c])
                if n > 0 and n % 2:
                    split_lo(pool, u + n - 1, 0, WIDTH[c])

        class_of = [c for _, n, c in SEGMENTS for _ in range(n)]
        next_hi = [0]

        def split_hi(act, u, k=0):
            s, w = u % 2, WIDTH[class_of[u]]
            act.wait_ge(landed[s], 16 * (u // 2 + 1) + k * 8)
            if not (isinstance(k, int) and u < 2):
                act.wait_ge(unit_done, u - 1 + k)
            act.activation(whi[s][:, 0:w], raw[s][:, 0:w], ACT.Copy).then_inc(hi_ready, 1)

        def split_hi_to(act, u):
            while next_hi[0] < min(u, UNITS):
                split_hi(act, next_hi[0])
                next_hi[0] += 1

        def products(pe, dst, terms, start=True, stop=True, **kw):
            n = len(terms)
            for i, (s_hi, s_lo, m_hi, m_lo) in enumerate(terms):
                pe.matmul(dst, s_hi, m_hi, start=start and i == 0, stop=False, **kw)
                pe.matmul(dst, s_hi, m_lo, start=False, stop=False, **kw)
                last = pe.matmul(dst, s_lo, m_hi, start=False, stop=stop and i == n - 1, **kw)
            return last

        def weight_chunks(u, first, n):
            s = u % 2
            for c in range(first, first + n):
                yield whi[s][:, c * P:(c + 1) * P], wlo[s][:, c * P:(c + 1) * P]

        def linear(pe, dst, u, m_hi, m_lo, n, first=0, chunk_ready=None, ready_base=0, signal=True):
            for c, (a, b) in enumerate(weight_chunks(u, first, n)):
                if chunk_ready is not None:
                    pe.wait_ge(chunk_ready, ready_base + c + 1)
                last = products(pe, dst, [(a, b, m_hi[:, c, :], m_lo[:, c, :])], start=c == 0, stop=c == n - 1)
            if signal:
                last.then_inc(unit_done, 1)

        def linear_by_token(pe, banks, u, j, of, s_hi, s_lo, chunk_ready=None):
            s = u % 2
            if chunk_ready is not None:
                pe.wait_ge(chunk_ready, 2 * j + 2)
            for t, b in enumerate(banks):
                terms = [(s_hi[:, 2 * j + c, t * P:(t + 1) * P], s_lo[:, 2 * j + c, t * P:(t + 1) * P],
                          whi[s][:, c * 512:(c + 1) * 512], wlo[s][:, c * 512:(c + 1) * 512]) for c in range(2)]
                last = products(pe, bank(b), terms, start=j == 0, stop=j == of - 1)
            last.then_inc(unit_done, 1)

        x_landed = [sem(f"x_landed{i}") for i in range(4)]
        vec_landed = sem("vec_landed")
        const_landed = sem("const_landed")
        constr_landed = sem("constr_landed")
        constr_ready = sem("constr_ready")

        x_updated = sem("x_updated")
        squared = sem("squared")
        summed = sem("summed")
        counts = {"x": 2, "sq": 0, "sum": 0}

        def clear_sum(dve):
            dve.memset(sumsq[:, :], 0.0).then_inc(summed, 1)
            counts["sum"] += 1

        def add_square(dve, x, k=0, i=0):
            dve.wait_ge(summed, counts["sum"] + k)
            dve.tensor_tensor(square[:, :], x, x, ALU.mult).then_inc(squared, 1)
            counts["sq"] += 1
            dve.wait_ge(squared, counts["sq"] + k)
            dve.tensor_tensor(sumsq[:, :], sumsq[:, :], square[:, :], ALU.add).then_inc(summed, 1)
            counts["sum"] += 1

        gained_hi = sem("gained_hi")
        gained = sem("gained")
        counts["gain"] = 0

        def split_gained(dve, x, gain, o, k=0):
            fixed = isinstance(k, int)
            hi, lo = ((h[:, o, :] if fixed else h[:, bass.ds(o + k, 1), :].rearrange("p a t -> p (a t)"))
                      for h in (h_hi, h_lo))
            g = col(gain, o) if fixed else vec[:, bass.ds(VEC[gain] + o + k, 1)]
            dve.tensor_scalar(hi, x, g, None, ALU.mult).then_inc(gained_hi, 1)
            counts["gain"] += 1
            dve.wait_ge(gained_hi, counts["gain"] + k)
            dve.scalar_tensor_tensor(lo, x, g, hi.bitcast(F32), ALU.mult, ALU.subtract).then_inc(gained, 1)

        class Norm:

            signals = [sem(f"norm_{s}") for s in ("mean", "std", "rstd", "f32", "hi", "ready")]
            norms, tiles = 0, 0

            def __init__(self, x, n, gain, hi, lo, total):
                self.x, self.n, self.gain, self.hi, self.lo, self.total = x, n, gain, hi, lo, total
                self.mean, self.std, self.rstd, self.f32, self.hi_made, self.ready = Norm.signals
                self.i, self.base = Norm.norms, Norm.tiles
                Norm.norms, Norm.tiles = Norm.norms + 1, Norm.tiles + n

            def tensor(self, pe):
                if self.i == 0:
                    pe.wait_ge(const_landed, 16)
                pe.wait_ge(summed, self.total)
                pe.matmul(bank(7), ones, sumsq[:, :], start=True, stop=True).then_inc(self.mean, 1)

            def factor(self, act):
                act.preload_act_table_set("natural_log_exp_and_others")
                act.wait_ge(self.mean, self.i + 1)
                act.activation(std[:, :], bank(7), ACT.Ln, scale=1.0 / (self.n * P),
                               bias=col("eps")).then_inc(self.std, 1)
                act.wait_ge(self.std, self.i + 1)
                act.activation(rstd[:, :], std[:, :], ACT.Exp, scale=-0.5).then_inc(self.rstd, 1)

            def scalar(self, act):
                self.factor(act)
                for k in range(self.n):
                    act.wait_ge(self.f32, self.base + k + 1)
                    act.activation(self.hi[:, k, :], stage32[k % 2][:, :], ACT.Copy).then_inc(self.hi_made, 1)

            def vector(self, dve):
                dve.wait_ge(self.rstd, self.i + 1)
                for k in range(self.n + 1):
                    if k < self.n:
                        if k > 1:
                            dve.wait_ge(self.ready, self.base + k - 1)
                        dve.scalar_tensor_tensor(stage32[k % 2][:, :], self.x[:, k, :], col(self.gain, k),
                                                 rstd[:, :], ALU.mult, ALU.mult).then_inc(self.f32, 1)
                    if k:
                        dve.wait_ge(self.hi_made, self.base + k)
                        dve.tensor_tensor(self.lo[:, k - 1, :], stage32[(k - 1) % 2][:, :],
                                          self.hi[:, k - 1, :].bitcast(F32), ALU.subtract).then_inc(self.ready, 1)

        class LateNorm(Norm):

            def __init__(self, x, n, gain, total, gained_base):
                Norm.__init__(self, x, 0, gain, h_hi, h_lo, total)
                self.n, self.base = n, gained_base
                self.ready = gained

        def update_x(dve, unit, o, k, b, scale, squares, gain):
            dve.wait_ge(unit_done, unit + 1 + k)
            x = xT[:, o, :] if isinstance(k, int) else xT[:, bass.ds(o + k, 1), :].rearrange("p a t -> p (a t)")
            dve.scalar_tensor_tensor(x, bank(b), scale, x, ALU.mult, ALU.add).then_inc(x_updated, 1)
            counts["x"] += 1
            if squares:
                dve.wait_ge(x_updated, counts["x"] + k)
                if gain:
                    split_gained(dve, x, gain, o, k)
                add_square(dve, x, k)

        def update_loop(dve, base, banks, scale, squares, gain=None):
            if squares:
                clear_sum(dve)
            dve.wait_ge(x_updated, counts["x"])
            c0 = dict(counts)
            with dve.Fori(0, DT // 2) as i:
                for b in range(2):
                    update_x(dve, base + b, b, i * 2, banks[b], scale, squares, gain)
            done = dict(c0)
            done["x"] += DT
            if squares:
                done["sq"] += DT
                done["sum"] += DT
            if gain:
                done["gain"] += DT
            counts.update(done)

        SUMS = {"ffn1": 9, "mix": 18, "ffn2": 27, "ple": 36, "block2": 45}
        XS = {"ffn1_0": 2, "out1": 18, "ffn2_0": 26, "ple": 42, "out2": 50}

        class FeedForward:

            signals = [sem(f"ffn_{s}") for s in ("gate", "sigmoid", "silu", "scaled", "mid", "mid_hi", "mid_ready")]

            def __init__(self, number, norm, x_base, next_gain):
                self.name, self.norm, self.x_base, self.next_gain = f"ffn{number}", norm, x_base, next_gain
                self.first = 2 * FH * (number - 1)
                self.gate, self.sig, self.silu, self.scaled, self.mid, self.mid_hi, self.ready = FeedForward.signals

            def tensor(self, pe):
                for half in range(2):
                    up, down, f0 = BASE[f"{self.name}_up{half}"], BASE[f"{self.name}_down{half}"], self.first + half * FH

                    def hidden_tile(f, k, first):
                        pe.wait_ge(lo_ready, up + 2 * f + 1 + k * 2)
                        if f0 + f > 0:
                            pe.wait_ge(self.gate, f0 + f + k)
                        linear(pe, bank(0), up, h_hi, h_lo, DT, chunk_ready=self.norm.ready if first else None,
                               ready_base=self.norm.base)
                        if first:
                            self.norm.tensor(pe)
                        pe.wait_ge(lo_ready, up + 2 * f + 2 + k * 2)
                        if f0 + f > 0:
                            pe.wait_ge(self.mid, f0 + f + k)
                        linear(pe, bank(1), up + 1, h_hi, h_lo, DT)

                    if half == 0:
                        pe.wait_ge(x_updated, self.x_base - 1)
                    hidden_tile(0, 0, half == 0)
                    with pe.Fori(0, FH - 1) as i:
                        hidden_tile(1, i, False)

                    def down_tile(b, k, first=False):
                        pe.wait_ge(lo_ready, down + b + 1 + k)
                        pe.wait_ge(x_updated, self.x_base + 8 * half + b - 1 + k)
                        linear(pe, bank(2 + b % 2), down + b, mid_hi, mid_lo, FH,
                               chunk_ready=self.ready if first else None, ready_base=f0)

                    down_tile(0, 0, True)
                    down_tile(1, 0)
                    with pe.Fori(0, DT // 2 - 1) as i:
                        for b in range(2):
                            down_tile(2 + b, i * 2)

            def scalar(self, act):
                self.norm.factor(act)
                act.preload_act_table(ACT.Sigmoid)
                for half in range(2):
                    up, f0 = BASE[f"{self.name}_up{half}"], self.first + half * FH

                    def sigmoid(f, k):
                        act.wait_ge(self.gate, f0 + f + 1 + k)
                        if f0 + f:
                            act.wait_ge(self.silu, f0 + f + k)
                        act.activation(sig[:, :], gate32[:, :], ACT.Sigmoid).then_inc(self.sig, 1)

                    split_hi_to(act, up + 2)
                    sigmoid(0, 0)
                    with act.Fori(0, FH - 1) as i:
                        split_hi(act, up + 2, i * 2)
                        split_hi(act, up + 3, i * 2)
                        sigmoid(1, i)
                    next_hi[0] = up + 2 * FH
                    split_hi_to(act, up + 2 * FH + DT)

            def vector(self, dve):
                dve.wait_ge(self.norm.rstd, self.norm.i + 1)
                for half in range(2):
                    up, f0 = BASE[f"{self.name}_up{half}"], self.first + half * FH
                    if half:
                        dve.wait_ge(unit_done, up)
                    with dve.Fori(0, FH) as i:
                        dve.wait_ge(unit_done, up + 1 + i * 2)
                        dve.tensor_tensor(gate32[:, :], bank(0), rstd[:, :], ALU.mult).then_inc(self.gate, 1)
                        dve.wait_ge(self.sig, f0 + 1 + i)
                        dve.wait_ge(self.gate, f0 + 1 + i)
                        dve.tensor_tensor(silu[:, :], sig[:, :], gate32[:, :], ALU.mult).then_inc(self.silu, 1)
                        dve.wait_ge(self.silu, f0 + 1 + i)
                        dve.tensor_tensor(silu[:, :], silu[:, :], rstd[:, :], ALU.mult).then_inc(self.scaled, 1)
                        dve.wait_ge(unit_done, up + 2 + i * 2)
                        dve.wait_ge(self.scaled, f0 + 1 + i)
                        dve.tensor_tensor(mid32[:, :], silu[:, :], bank(1), ALU.mult).then_inc(self.mid, 1)
                        hi = mid_hi[:, bass.ds(i, 1), :].rearrange("p a t -> p (a t)")
                        lo = mid_lo[:, bass.ds(i, 1), :].rearrange("p a t -> p (a t)")
                        dve.wait_ge(self.mid, f0 + 1 + i)
                        dve.tensor_copy(hi, mid32[:, :]).then_inc(self.mid_hi, 1)
                        dve.wait_ge(self.mid_hi, f0 + 1 + i)
                        dve.tensor_tensor(lo, mid32[:, :], hi.bitcast(F32), ALU.subtract).then_inc(self.ready, 1)
                        dve.wait_ge(self.ready, f0 + 1 + i)
                    update_loop(dve, BASE[f"{self.name}_down{half}"], (2, 3), 0.5, half == 1,
                                self.next_gain if half else None)

        norm_ffn1 = LateNorm(xT, DT, "ffn1_norm", SUMS["ffn1"], 0)
        ffn1 = FeedForward(1, norm_ffn1, XS["ffn1_0"], None)
        norm_mix = Norm(xT, DT, "mix_norm", h_hi, h_lo, SUMS["mix"])

        class SoftmaxAttention:

            def __init__(self, name, q, k, v, prob, probT, scale, causal, extra):
                self.q, self.k, self.v, self.prob, self.probT = q, k, v, prob, probT
                self.scale, self.causal, self.extra = scale, causal, extra
                (self.scores, self.maxed, self.neg, self.exped, self.inv, self.normed, self.turned, self.copied0,
                 self.copied1, self.summed, self.out_hi, self.out) = (
                    sem(f"{name}_{x}") for x in ("scores", "maximum", "negated", "exped", "inverse", "normed",
                                                 "transposed", "copied_even", "copied_odd", "outputs", "out_hi", "out"))

            def keys(self, t):
                return (t + 1) * P if self.causal else T

            def queries(self, s):
                return s * P if self.causal else 0

            def tensor_scores(self, pe, h):
                for t in range(TT):
                    n = self.keys(t)
                    if h:
                        pe.wait_ge(self.exped, TT * (h - 1) + t + 1)
                    (qh, ql), (kh, kl) = self.q(h), self.k(h)
                    rows = slice(t * P, (t + 1) * P)
                    last = products(pe, bank(t, n), [(qh[:, rows], ql[:, rows], kh[:, 0:n], kl[:, 0:n])],
                                    stop=not self.extra)
                    if self.extra:
                        pe.matmul(bank(t, n), sel[:, h, :], nf_hi[:, 0:n], start=False, stop=False)
                        pe.matmul(bank(t, n), sel[:, h, :], nf_lo[:, 0:n], start=False, stop=False)
                        last = pe.matmul(psum[:, 512 * t + t * P:512 * t + n], ident_r, mask_qk, start=False, stop=True)
                    last.then_inc(self.scores, 1)

            def tensor_outputs(self, pe, h):
                pe.wait_ge(self.normed, TT * (h + 1))
                for s in range(TT + 1):
                    if s < TT:
                        n = TT * h + s
                        if n >= 2:
                            pe.wait_ge((self.copied0, self.copied1)[s % 2], n // 2)
                        t0 = s if self.causal else 0
                        for t in range(t0, TT):
                            last = pe.transpose(psum[:, 512 * (4 + s % 2) + t * P:512 * (4 + s % 2) + (t + 1) * P],
                                                self.prob[h % 2][:, t, s * P:(s + 1) * P], ident)
                        last.then_inc(self.turned, 1)
                    if s:
                        r = s - 1
                        pe.wait_ge((self.copied0, self.copied1)[r % 2], 2 * h + r // 2 + 1)
                        if r == 0 and h >= 2:
                            pe.wait_ge(self.out, h - 1)
                        a = self.queries(r)
                        pe.matmul(psum[:, 512 * (6 + h % 2) + a:512 * (7 + h % 2)], self.v(h, r),
                                  self.probT[r % 2][:, a:T], start=r == 0, stop=r == TT - 1,
                                  ).then_inc(self.summed, 1)

            def tensor(self, pe, ready, next_unit):
                for semaphore, value in ready:
                    pe.wait_ge(semaphore, value)
                self.tensor_scores(pe, 0)
                for h in range(HEADS):
                    if h + 1 < HEADS:
                        self.tensor_scores(pe, h + 1)
                    else:
                        next_unit(pe, 0)
                    self.tensor_outputs(pe, h)

            def cols(self, h, what):
                a = 12 * (h % 2) + 4 * what
                return small[:, a:a + 4]

            def scalar_exp(self, act, h, t, last_scores):
                if t == 0:
                    act.wait_ge(self.neg, h + 1)
                    if h >= 2:
                        act.wait_ge(self.turned, TT * (h - 1))
                n = self.keys(t)
                act.activation(self.prob[h % 2][:, t, 0:n], bank(t, n), ACT.Exp, scale=self.scale,
                               bias=self.cols(h, 0)[:, t:t + 1],
                               accum_out=self.cols(h, 1)[:, t:t + 1]).then_inc(self.exped, 1)
                if h == HEADS - 1 and t == TT - 1 and last_scores is not None:
                    last_scores(act)

            def scalar(self, act, last_scores=None):
                for t in range(TT):
                    self.scalar_exp(act, 0, t, last_scores)
                for h in range(HEADS):
                    self.scalar_outputs(act, h, last_scores)

            def copy_transpose(self, act, h, s):
                n = TT * h + s
                act.wait_ge(self.turned, n + 1)
                if n >= 2:
                    act.wait_ge(self.summed, n - 1)
                a = self.queries(s)
                src, dst = psum[:, 512 * (4 + s % 2) + a:512 * (5 + s % 2)], self.probT[s % 2][:, a:T]
                act.activation(dst, src, ACT.Copy).then_inc((self.copied0, self.copied1)[s % 2], 1)

            def scalar_outputs(self, act, h, last_scores):
                for s in range(TT):
                    self.copy_transpose(act, h, s)
                    if s and h + 1 < HEADS:
                        self.scalar_exp(act, h + 1, s - 1, last_scores)
                if h + 1 < HEADS:
                    self.scalar_exp(act, h + 1, TT - 1, last_scores)
                act.wait_ge(self.summed, TT * (h + 1))
                rows = slice(HD * (h % 2), HD * (h % 2) + HD)
                src = bank(6 + h % 2)[rows, :]
                if self.extra:
                    act.activation(ya_hi[rows, h // 2, :], src, ACT.Copy).then_inc(self.out_hi, 1)
                else:
                    act.activation(y32[rows, h // 2, :], src, ACT.Copy).then_inc(self.out, 1)

            def vector_maximum(self, dve, h):
                top = self.cols(h, 0)
                if h >= 2:
                    dve.wait_ge(self.exped, TT * (h - 1))
                for t in range(TT):
                    dve.wait_ge(self.scores, TT * h + t + 1)
                    dve.tensor_reduce(top[:, t:t + 1], bank(t, self.keys(t)), AXX, ALU.max).then_inc(self.maxed, 1)
                dve.wait_ge(self.maxed, TT * (h + 1))
                dve.tensor_scalar(top, top, -self.scale, None, ALU.mult).then_inc(self.neg, 1)

            def vector(self, dve):
                self.vector_maximum(dve, 0)
                for h in range(HEADS):
                    total, inverse = self.cols(h, 1), self.cols(h, 2)
                    dve.wait_ge(self.exped, TT * (h + 1))
                    dve.reciprocal(inverse, total).then_inc(self.inv, 1)
                    dve.wait_ge(self.inv, h + 1)
                    for t in range(TT):
                        row = self.prob[h % 2][:, t, 0:self.keys(t)]
                        dve.tensor_scalar(row, row, inverse[:, t:t + 1], None, ALU.mult).then_inc(self.normed, 1)
                    if h + 1 < HEADS:
                        self.vector_maximum(dve, h + 1)
                    if h:
                        self.vector_outputs(dve, h - 1)
                self.vector_outputs(dve, HEADS - 1)

            def vector_outputs(self, dve, h):
                if self.extra:
                    rows = slice(HD * (h % 2), HD * (h % 2) + HD)
                    dve.wait_ge(self.out_hi, h + 1)
                    dve.tensor_tensor(ya_lo[rows, h // 2, :], bank(6 + h % 2)[rows, :],
                                      ya_hi[rows, h // 2, :].bitcast(F32), ALU.subtract).then_inc(self.out, 1)

        fox = SoftmaxAttention("fox", lambda h: (q_hi[:, h, :], q_lo[:, h, :]),
                               lambda h: (k_hi[:, h // 2, :], k_lo[:, h // 2, :]),
                               lambda h, s: v32[:, s, (h // 2) * P:(h // 2 + 1) * P],
                               (prob, prob_odd), probT, 1.0, True, True)

        class FoxProjections:

            def __init__(self):
                (self.sq, self.sum, self.std, self.rstd, self.f32, self.hi, self.ready, self.cleared, self.sel_landed,
                 self.sel, self.forget, self.softplus, self.v) = (
                    sem(f"fox_{x}") for x in ("square", "head_sum", "std", "rstd", "f32", "hi", "qk_ready", "cleared",
                                              "sel_landed", "sel", "forget", "softplus", "v"))

            def tensor(self, pe, norm):
                for j in range(9):
                    if j < 8:
                        u = BASE["fox_q"] + j
                        pe.wait_ge(lo_ready, u + 1)
                        if j >= 4:
                            pe.wait_ge(self.f32, j - 3)
                        linear(pe, bank(j % 4), u, h_hi, h_lo, DT, chunk_ready=norm.ready if j == 0 else None,
                               ready_base=norm.base)
                    if j:
                        pe.wait_ge(self.sq, j)
                        if j > 2:
                            pe.wait_ge(self.std, j - 2)
                        pe.matmul(bank(4 + (j - 1) % 2), block_ones, head_sq[(j - 1) % 2][:, :], start=True,
                                  stop=True).then_inc(self.sum, 1)
                u = BASE["fox_f"]
                pe.wait_ge(lo_ready, u + 1)
                linear(pe, bank(6), u, h_hi, h_lo, DT)
                pe.wait_ge(self.std, 8)
                pe.wait_ge(self.forget, 1)
                for j in range(4):
                    pe.wait_ge(lo_ready, BASE["fox_v"] + j + 1)
                    linear_by_token(pe, (4, 5, 7, 6), BASE["fox_v"] + j, j, 4, h_hi, h_lo)

            def scalar(self, act):
                act.wait_ge(self.sel_landed, 16)
                act.activation(sel[:, :, :], sel32[:, :, :], ACT.Copy).then_inc(self.sel, 1)
                act.wait_ge(constr_landed, 16)
                act.activation(constr[:, :, :], constr32[:, :, :], ACT.Copy).then_inc(constr_ready, 1)
                for j in range(9):
                    if j < 8:
                        u = BASE["fox_q"] + j
                        split_hi_to(act, u + 2)
                        act.wait_ge(unit_done, u + 1)
                        if j >= 2:
                            act.wait_ge(self.sum, j - 1)
                        act.activation(head_sq[j % 2][:, :], bank(j % 4), ACT.Square).then_inc(self.sq, 1)
                        split_hi_to(act, u + 3)
                    if j:
                        i = j - 1
                        act.wait_ge(self.sum, i + 1)
                        act.activation(std[:, :], bank(4 + i % 2), ACT.Ln, scale=1.0 / HD,
                                       bias=col("eps")).then_inc(self.std, 1)
                        act.wait_ge(self.std, i + 1)
                        if i:
                            act.wait_ge(self.f32, i)
                        act.activation(rstd[:, :], std[:, :], ACT.Exp, scale=-0.5).then_inc(self.rstd, 1)
                        act.wait_ge(self.f32, i + 1)
                        src = stage32[i % 2]
                        if i < 4:
                            act.wait_ge(self.cleared, 4)
                            act.activation(q_hi[0:HD, 2 * i, :], src[0:HD, :], ACT.Copy).then_inc(self.hi, 1)
                            act.activation(q_hi[HD:P, 2 * i + 1, :], src[HD:P, :], ACT.Copy).then_inc(self.hi, 1)
                        else:
                            act.activation(k_hi[:, i - 4, :], src[:, :], ACT.Copy).then_inc(self.hi, 1)
                u = BASE["fox_f"]
                split_hi_to(act, u + 2)
                act.wait_ge(self.forget, 1)
                act.activation(prob[:, 1, :], prob[:, 0, :], ACT.Abs).then_inc(self.softplus, 1)
                act.wait_ge(self.softplus, 1)
                act.activation(prob[:, 2, :], prob[:, 1, :], ACT.Exp, scale=-1.0).then_inc(self.softplus, 1)
                act.wait_ge(self.softplus, 2)
                act.activation(prob[:, 3, :], prob[:, 2, :], ACT.Ln, bias=1.0).then_inc(self.softplus, 1)
                split_hi_to(act, BASE["fox_v"] + 4)
                act.wait_ge(unit_done, BASE["fox_v"] + 4)
                act.wait_ge(self.sel, 1)
                for t, b in enumerate((4, 5, 7, 6)):
                    act.activation(v32[:, t, :], bank(b), ACT.Copy).then_inc(self.v, 1)
                split_hi_to(act, BASE["fox_v"] + 6)

            def vector(self, dve):
                for i, q in enumerate((q_hi, q_lo)):
                    even = q[HD:P, :, :].rearrange("p (j e) t -> p j e t", e=2)[:, :, 0, :]
                    odd = q[0:HD, :, :].rearrange("p (j e) t -> p j e t", e=2)[:, :, 1, :]
                    for half in (even, odd):
                        dve.memset(half.bitcast(F32), 0.0).then_inc(self.cleared, 1)
                dve.tensor_scalar(small[:, 31:32], col("q_norm"), HD ** -0.5, None, ALU.mult).then_inc(self.cleared, 1)
                for i in range(8):
                    dve.wait_ge(self.rstd, i + 1)
                    if i == 0:
                        dve.wait_ge(self.cleared, 5)
                    gain = small[:, 31:32] if i < 4 else col("k_norm")
                    dve.scalar_tensor_tensor(stage32[i % 2][:, :], bank(i % 4), gain, rstd[:, :],
                                             ALU.mult, ALU.mult).then_inc(self.f32, 1)
                    src = stage32[i % 2]
                    if i < 4:
                        dve.wait_ge(self.hi, 2 * i + 2)
                        for e, rows in enumerate((slice(0, HD), slice(HD, P))):
                            dve.tensor_tensor(q_lo[rows, 2 * i + e, :], src[rows, :],
                                              q_hi[rows, 2 * i + e, :].bitcast(F32), ALU.subtract).then_inc(self.ready, 1)
                        dve.wait_ge(self.ready, 2 * i + 2)
                    else:
                        dve.wait_ge(self.hi, 8 + i - 3)
                        dve.tensor_tensor(k_lo[:, i - 4, :], src[:, :], k_hi[:, i - 4, :].bitcast(F32),
                                          ALU.subtract).then_inc(self.ready, 1)
                        dve.wait_ge(self.ready, 8 + i - 3)
                dve.wait_ge(unit_done, BASE["fox_f"] + 1)
                dve.tensor_scalar(prob[:, 0, :], bank(6), col("forget_bias"), None, ALU.add).then_inc(self.forget, 1)
                dve.wait_ge(self.forget, 1)
                dve.wait_ge(self.softplus, 3)
                dve.wait_ge(constr_ready, 1)
                dve.scalar_tensor_tensor(probT[0][:, :], prob[:, 0, :], 0.0, prob[:, 3, :], ALU.min,
                                         ALU.subtract).then_inc(self.forget, 1)
                dve.memset(prob[:, 1, :], 1.0).then_inc(self.forget, 1)
                dve.wait_ge(self.forget, 3)
                dve.tensor_tensor_scan(probT[1][:, :], prob[:, 1, :], probT[0][:, :], 0.0, ALU.mult,
                                       ALU.add).then_inc(self.forget, 1)
                dve.wait_ge(self.forget, 4)
                dve.tensor_scalar(nf_hi[:, :], probT[1][:, :], -1.0, None, ALU.mult).then_inc(self.forget, 1)
                dve.wait_ge(self.forget, 5)
                dve.scalar_tensor_tensor(nf_lo[:, :], probT[1][:, :], -1.0, nf_hi[:, :].bitcast(F32), ALU.mult,
                                         ALU.subtract).then_inc(self.forget, 1)
                dve.wait_ge(self.forget, 6)

        foxp = FoxProjections()

        class StickProjections:

            def __init__(self):
                self.hi, self.ready, self.v = (sem(f"stick_{x}") for x in ("hi", "qk_ready", "v"))

            def tensor_unit(self, pe, j):
                u = BASE["sb_q"] + j
                pe.wait_ge(lo_ready, u + 1)
                pe.wait_ge(*((fox.exped, TT * (HEADS - 1) + j + 1) if j < 4 else (self.ready, 2 * (j - 3))))
                linear(pe, bank(j % 4), u, h_hi, h_lo, DT)

            def tensor(self, pe):
                for j in range(1, 8):
                    self.tensor_unit(pe, j)
                for j in range(4):
                    pe.wait_ge(fox.out, HEADS)
                    pe.wait_ge(lo_ready, BASE["sb_v"] + j + 1)
                    linear_by_token(pe, (4, 5, 6, 7), BASE["sb_v"] + j, j, 4, h_hi, h_lo)
                    if j == 0:
                        pe.wait_ge(self.ready, 12)
                        stick.tensor_z(pe, 0)

            def scalar(self, act):
                for j in range(8):
                    u = BASE["sb_q"] + j
                    split_hi_to(act, u + 2)
                    act.wait_ge(unit_done, u + 1)
                    if j < 4:
                        act.activation(q_hi[0:HD, 2 * j, :], bank(j)[0:HD, :], ACT.Copy,
                                       scale=HD ** -0.5).then_inc(self.hi, 1)
                        act.activation(q_hi[HD:P, 2 * j + 1, :], bank(j)[HD:P, :], ACT.Copy,
                                       scale=HD ** -0.5).then_inc(self.hi, 1)
                    else:
                        act.activation(k_hi[:, j - 4, :], bank(j % 4), ACT.Copy).then_inc(self.hi, 1)
                split_hi_to(act, BASE["sb_v"] + 3)
                stick.scalar_softplus(act, 0)
                split_hi_to(act, BASE["sb_v"] + 4)
                act.wait_ge(unit_done, BASE["sb_v"] + 4)
                for t in range(TT):
                    act.activation(v32[:, t, :], bank(4 + t), ACT.Copy).then_inc(self.v, 1)
                split_hi_to(act, BASE["sb_v"] + 6)

            def vector(self, dve):
                for j in range(4):
                    dve.wait_ge(self.hi, 2 * j + 2)
                    for e, rows in enumerate((slice(0, HD), slice(HD, P))):
                        dve.scalar_tensor_tensor(q_lo[rows, 2 * j + e, :], bank(j)[rows, :], HD ** -0.5,
                                                 q_hi[rows, 2 * j + e, :].bitcast(F32), ALU.mult,
                                                 ALU.subtract).then_inc(self.ready, 1)
                for j in range(4):
                    dve.wait_ge(self.hi, 9 + j)
                    dve.tensor_tensor(k_lo[:, j, :], bank(j), k_hi[:, j, :].bitcast(F32),
                                      ALU.subtract).then_inc(self.ready, 1)

        stickp = StickProjections()

        class StickBreaking:

            def __init__(self):
                (self.z, self.az, self.e, self.l, self.sp, self.masked, self.hi, self.ready, self.sums, self.weight,
                 self.outputs, self.out_hi, self.out) = (
                    sem(f"stick_{x}") for x in ("z", "abs", "exp", "ln", "softplus", "masked", "sp_hi", "sp_ready",
                                                "sums", "weight", "outputs", "out_hi", "out"))

            def zone(self, h, s, a=0, n=None):
                o = 512 * 3 * (h % 2) + AREA[s] + a
                return psum[:, o:o + (T - s * P - a if n is None else n)]

            def whole(self, h):
                return psum[:, 512 * 3 * (h % 2):512 * 3 * (h % 2) + AREA_COLS]

            def tensor_z(self, pe, h):
                if h >= 2:
                    pe.wait_ge(self.weight, h - 1)
                for s in range(TT):
                    keys = slice(s * P, (s + 1) * P)
                    last = products(pe, self.zone(h, s), [(k_hi[:, h // 2, keys], k_lo[:, h // 2, keys],
                                                           q_hi[:, h, s * P:T], q_lo[:, h, s * P:T])],
                                    start=s != 3, stop=True, skip_group_check=True)
                last.then_inc(self.z, 1)

            def tensor_sums(self, pe, h):
                pe.wait_ge(self.ready, h + 1)
                for s in range(TT):
                    for j in range(s, TT):
                        tri = neg_tri if j == s else neg_ones
                        for sp in (sp_hi, sp_lo):
                            pe.matmul(self.zone(h, s, (j - s) * P), tri, sp[:, AREA[j]:AREA[j] + T - j * P],
                                      start=False, stop=False, skip_group_check=True)
                    last = pe.matmul(self.zone(h, s, 0, P), ident_r, mask_kq, start=False, stop=True,
                                     skip_group_check=True)
                last.then_inc(self.sums, 1)

            def tensor_outputs(self, pe, h):
                pe.wait_ge(self.weight, h + 1)
                if h >= 2:
                    pe.wait_ge(self.out, h - 1)
                for s in range(TT):
                    last = pe.matmul(psum[:, 512 * (6 + h % 2) + s * P:512 * (7 + h % 2)],
                                     v32[:, s, (h // 2) * P:(h // 2 + 1) * P],
                                     weight[h % 2][:, AREA[s]:AREA[s] + T - s * P], start=s == 0, stop=s == TT - 1)
                last.then_inc(self.outputs, 1)

            def tensor(self, pe):
                pe.wait_ge(stickp.v, TT)
                for h in range(HEADS):
                    if h + 1 < HEADS:
                        self.tensor_z(pe, h + 1)
                    self.tensor_sums(pe, h)
                    if h:
                        self.tensor_outputs(pe, h - 1)
                self.tensor_outputs(pe, HEADS - 1)

            def scalar_softplus(self, act, h):
                buf = soft[h % 2]
                if h == 0:
                    act.preload_act_table_set("natural_log_exp_and_others")
                act.wait_ge(self.z, h + 1)
                if h >= 2:
                    act.wait_ge(self.ready, h - 1)
                act.activation(buf[:, :], self.whole(h), ACT.Abs).then_inc(self.az, 1)
                act.wait_ge(self.az, h + 1)
                act.activation(buf[:, :], buf[:, :], ACT.Exp, scale=-1.0).then_inc(self.e, 1)
                act.wait_ge(self.e, h + 1)
                act.activation(buf[:, :], buf[:, :], ACT.Ln, bias=1.0).then_inc(self.l, 1)

            def scalar_weight(self, act, h):
                act.wait_ge(self.sums, h + 1)
                if h >= 2:
                    act.wait_ge(self.outputs, h - 1)
                act.activation(weight[h % 2][:, :], self.whole(h), ACT.Exp).then_inc(self.weight, 1)

            def scalar_output(self, act, h):
                act.wait_ge(self.outputs, h + 1)
                rows = slice(HD * (h % 2), HD * (h % 2) + HD)
                act.activation(yb_hi[rows, h // 2, :], bank(6 + h % 2)[rows, :], ACT.Copy).then_inc(self.out_hi, 1)

            def scalar(self, act):
                for h in range(HEADS):
                    if h:
                        self.scalar_softplus(act, h)
                    if h:
                        self.scalar_weight(act, h - 1)
                    if h >= 2:
                        self.scalar_output(act, h - 2)
                self.scalar_weight(act, HEADS - 1)
                self.scalar_output(act, HEADS - 2)
                self.scalar_output(act, HEADS - 1)

            def vector_output(self, dve, h):
                dve.wait_ge(self.out_hi, h + 1)
                rows = slice(HD * (h % 2), HD * (h % 2) + HD)
                dve.tensor_tensor(yb_lo[rows, h // 2, :], bank(6 + h % 2)[rows, :],
                                  yb_hi[rows, h // 2, :].bitcast(F32), ALU.subtract).then_inc(self.out, 1)

            def vector(self, dve):
                for h in range(HEADS):
                    buf = soft[h % 2]
                    dve.wait_ge(self.l, h + 1)
                    dve.scalar_tensor_tensor(buf[:, :], self.whole(h), 0.0, buf[:, :], ALU.max,
                                             ALU.add).then_inc(self.sp, 1)
                    dve.wait_ge(self.sp, h + 1)
                    for s in range(TT):
                        diagonal = buf[:, AREA[s]:AREA[s] + P]
                        dve.tensor_tensor(diagonal, diagonal, before, ALU.mult).then_inc(self.masked, 1)
                    dve.wait_ge(self.masked, 4 * h + 4)
                    if h:
                        dve.wait_ge(self.sums, h)
                    dve.tensor_copy(sp_hi[:, :], buf[:, :]).then_inc(self.hi, 1)
                    dve.wait_ge(self.hi, h + 1)
                    dve.tensor_tensor(sp_lo[:, :], buf[:, :], sp_hi[:, :].bitcast(F32),
                                      ALU.subtract).then_inc(self.ready, 1)
                    if h >= 2:
                        self.vector_output(dve, h - 2)
                self.vector_output(dve, HEADS - 2)
                self.vector_output(dve, HEADS - 1)

        stick = StickBreaking()

        class Merge:

            signals = [sem(f"merge_{x}") for x in ("opened", "gate", "part", "sum", "hi", "ready")]

            def __init__(self, n, bias, x_base, before, squares, next_gain):
                self.next_gain = next_gain
                self.base, self.out_base = BASE[f"merge{n}"], BASE[f"out{n}"]
                self.bias, self.x_base, self.before, self.squares = bias, x_base, before, squares
                self.first = DT * (n - 1)
                self.opened, self.gate, self.part, self.sum, self.hi, self.ready = Merge.signals

            def tensor(self, pe):
                def tile(b, k, before=()):
                    u, side = self.base + 3 * b, 4 * (b % 2)
                    pe.wait_ge(self.opened, self.first // DT * (DT + 2) + b + 1 + k * 2)
                    for g in range(2):
                        pe.wait_ge(lo_ready, u + g + 1 + k * 6)
                        linear(pe, bank(side + g), u + g, h_hi, h_lo, DT)
                    pe.wait_ge(lo_ready, u + 3 + k * 6)
                    for s, v in before:
                        pe.wait_ge(s, v)
                    linear(pe, bank(side + 2), u + 2, ya_hi, ya_lo, 4, signal=False)
                    linear(pe, bank(side + 3), u + 2, yb_hi, yb_lo, 4, first=4)

                tile(0, 0, self.before)
                tile(1, 0)
                with pe.Fori(0, DT // 2 - 1) as i:
                    for b in range(2):
                        tile(2 + b, i)

                def project(b, k, first=False):
                    pe.wait_ge(lo_ready, self.out_base + b + 1 + k)
                    pe.wait_ge(x_updated, self.x_base + b - 1 + k)
                    linear(pe, bank(b % 2), self.out_base + b, merged_hi, merged_lo, DT,
                           chunk_ready=self.ready if first else None, ready_base=self.first)

                project(0, 0, True)
                project(1, 0)
                with pe.Fori(0, DT // 2 - 1) as i:
                    for b in range(2):
                        project(2 + b, i * 2)

            def scalar(self, act):
                split_hi_to(act, self.base + 2)
                with act.Fori(0, DT // 2) as i:
                    for b in range(2):
                        u = self.base + 3 * b
                        for g in range(2):
                            act.wait_ge(unit_done, u + g + 1 + i * 6)
                            act.activation(gate[b][:, g, :], bank(4 * b + g), ACT.Sigmoid,
                                           bias=gate_bias[b][:, g:g + 1]).then_inc(self.gate, 1)
                            split_hi(act, u + g + 2, i * 6)
                        split_hi(act, u + 4, i * 6)
                next_hi[0] = self.base + 26
                split_hi_to(act, self.out_base + DT)

            def open_tile(self, dve, b, o, k):
                c = VEC[self.bias] + 2 * o
                src = vec[:, c:c + 2] if isinstance(k, int) else vec[:, bass.ds(c + k * 2, 2)]
                dve.tensor_copy(gate_bias[b][:, :], src).then_inc(self.opened, 1)

            def open_first(self, dve):
                for b in range(2):
                    self.open_tile(dve, b, b, 0)

            def vector(self, dve):
                with dve.Fori(0, DT // 2) as i:
                    for b in range(2):
                        u = self.base + 3 * b
                        dve.wait_ge(unit_done, u + 3 + i * 6)
                        dve.wait_ge(self.gate, 2 * self.first + 2 * b + 2 + i * 4)
                        for g in range(2):
                            dve.tensor_tensor(gated[:, g, :], gate[b][:, g, :], bank(4 * b + 2 + g),
                                              ALU.mult).then_inc(self.part, 1)
                        dve.wait_ge(self.part, 2 * self.first + 2 * b + 2 + i * 4)
                        dve.tensor_tensor(sum32[:, :], gated[:, 0, :], gated[:, 1, :], ALU.add).then_inc(self.sum, 1)
                        dve.wait_ge(self.sum, self.first + b + 1 + i * 2)
                        hi = merged_hi[:, bass.ds(i * 2 + b, 1), :].rearrange("p a t -> p (a t)")
                        lo = merged_lo[:, bass.ds(i * 2 + b, 1), :].rearrange("p a t -> p (a t)")
                        dve.tensor_copy(hi, sum32[:, :]).then_inc(self.hi, 1)
                        dve.wait_ge(self.hi, self.first + b + 1 + i * 2)
                        dve.tensor_tensor(lo, sum32[:, :], hi.bitcast(F32), ALU.subtract).then_inc(self.ready, 1)
                        dve.wait_ge(self.ready, self.first + b + 1 + i * 2)
                        self.open_tile(dve, b, b + 2, i * 2)
                update_loop(dve, self.out_base, (0, 1), 1.0, self.squares, self.next_gain)

        merge1 = Merge(1, "no_bias", XS["out1"], [(fox.out, HEADS), (stick.out, HEADS)], True, "ffn2_norm")
        norm_ffn2 = LateNorm(xT, DT, "ffn2_norm", SUMS["ffn2"], DT)
        ffn2 = FeedForward(2, norm_ffn2, XS["ffn2_0"], "ple_norm")


        class LayerEmbedding:

            def __init__(self, norm, x_base):
                self.norm, self.x_base, self.base = norm, x_base, BASE["ple"]
                self.landed, self.hi, self.p_ready, self.gate, self.sig, self.add = (
                    sem(f"ple_{x}") for x in ("landed", "p_hi", "p_ready", "gate", "sigmoid", "add"))

            def tensor(self, pe):
                def tile(b, k, first=False):
                    pe.wait_ge(lo_ready, self.base + b + 1 + k)
                    pe.wait_ge(x_updated, self.x_base + b - 1 + k)
                    linear(pe, bank(b % 2), self.base + b, h_hi, h_lo, DT, signal=False,
                           chunk_ready=self.norm.ready if first else None, ready_base=self.norm.base)
                    if first:
                        pe.wait_ge(self.p_ready, 1)
                    linear(pe, bank(2 + b % 2), self.base + b, p_hi, p_lo, 2, first=DT)

                tile(0, 0, True)
                self.norm.tensor(pe)
                tile(1, 0)
                with pe.Fori(0, DT // 2 - 1) as i:
                    for b in range(2):
                        tile(2 + b, i * 2)

            def load(self, act):
                act.wait_ge(merge1.ready, DT)
                act.dma_start(p32[:, :, :], p_in).then_inc(self.landed, 16)

            def scalar(self, act):
                act.wait_ge(self.landed, 16)
                act.activation(p_hi[:, :, :], p32[:, :, :], ACT.Copy).then_inc(self.hi, 1)

                self.norm.factor(act)
                act.preload_act_table(ACT.Sigmoid)

                def sigmoid(b, k):
                    act.wait_ge(self.gate, b + 1 + k)
                    act.activation(ple_gate[b][:, :], ple_gate[b][:, :], ACT.Sigmoid).then_inc(self.sig, 1)

                with act.Fori(0, DT // 2 - 1) as i:
                    for b in range(2):
                        split_hi(act, self.base + 2 + b, i * 2)
                        sigmoid(b, i * 2)
                next_hi[0] = self.base + DT
                for b in range(2):
                    sigmoid(b, DT - 2)

            def vector(self, dve):
                dve.wait_ge(self.hi, 1)
                dve.tensor_tensor(p_lo[:, :, :], p32[:, :, :], p_hi[:, :, :].bitcast(F32),
                                  ALU.subtract).then_inc(self.p_ready, 1)
                dve.wait_ge(self.norm.rstd, self.norm.i + 1)
                clear_sum(dve)
                dve.wait_ge(x_updated, counts["x"])
                c0 = dict(counts)
                with dve.Fori(0, DT // 2) as i:
                    for b in range(2):
                        dve.wait_ge(unit_done, self.base + b + 1 + i * 2)
                        dve.tensor_tensor(ple_gate[b][:, :], bank(b), rstd[:, :], ALU.mult).then_inc(self.gate, 1)
                        dve.wait_ge(self.sig, b + 1 + i * 2)
                        dve.tensor_tensor(ple_add[:, :], ple_gate[b][:, :], bank(2 + b), ALU.mult).then_inc(self.add, 1)
                        dve.wait_ge(self.add, b + 1 + i * 2)
                        x = xT[:, bass.ds(i * 2 + b, 1), :].rearrange("p a t -> p (a t)")
                        dve.tensor_tensor(x, x, ple_add[:, :], ALU.add).then_inc(x_updated, 1)
                        counts["x"] += 1
                        dve.wait_ge(x_updated, counts["x"] + i * 2)
                        add_square(dve, x, i * 2)
                counts.update({"x": c0["x"] + DT, "sq": c0["sq"] + DT, "sum": c0["sum"] + DT})

        norm_ple = LateNorm(xT, DT, "ple_norm", SUMS["ple"], 2 * DT)
        ple = LayerEmbedding(norm_ple, XS["ple"])
        norm_block2 = Norm(xT, DT, "g_norm", h_hi, h_lo, SUMS["block2"])

        norm_cq = Norm(lat32, 3, "g_cq", cq_hi, cq_lo, SUMS["block2"] + 4)
        norm_ckv = Norm(ckv32, 2, "g_ckv", ckv_hi, ckv_lo, SUMS["block2"] + 7)

        class LatentProjections:

            def __init__(self):
                (self.rope_landed, self.tabs, self.lat, self.q32, self.k32, self.sq, self.sum, self.std, self.rstd,
                 self.cos, self.sin, self.rot, self.f32, self.hi, self.ready, self.v) = (
                    sem(f"latent_{x}") for x in ("rope_landed", "tabs", "latents", "q32", "k32", "square", "sum",
                                                 "std", "rstd", "cos", "sin", "rotated", "f32", "hi", "ready", "v"))

            def tensor(self, pe):
                u = BASE["mla_cq"]
                for j in range(6):
                    pe.wait_ge(lo_ready, u + j + 1)
                    linear(pe, bank(j), u + j, h_hi, h_lo, DT, chunk_ready=norm_block2.ready if j == 0 else None,
                           ready_base=norm_block2.base)
                    if j == 3:
                        norm_cq.tensor(pe)
                norm_ckv.tensor(pe)
                pe.wait_ge(norm_cq.ready, norm_cq.base + 3)
                pe.wait_ge(norm_ckv.ready, norm_ckv.base + 2)
                pe.wait_ge(self.lat, 6)
                for h in range(HEADS + 1):
                    if h < HEADS:
                        u = BASE["mla_qk"] + h
                        pe.wait_ge(lo_ready, u + 1)
                        if h >= 2:
                            pe.wait_ge(self.q32, h - 1)
                            pe.wait_ge(self.k32, h - 1)
                        b = 2 * (h % 2)
                        linear(pe, bank(b), u, cq_hi, cq_lo, 3, signal=False)
                        linear(pe, bank(b + 1), u, ckv_hi, ckv_lo, 2, first=3)
                    if h:
                        for m in (2 * h - 2, 2 * h - 1):
                            pe.wait_ge(self.sq, m + 1)
                            if m >= 2:
                                pe.wait_ge(self.std, m - 1)
                            pe.matmul(bank(4 + m % 2), ones, head_sq[m % 2][:, :], start=True,
                                      stop=True).then_inc(self.sum, 1)
                pe.wait_ge(self.q32, HEADS)
                pe.wait_ge(self.k32, HEADS)
                pe.wait_ge(lo_ready, BASE["mla_v"] + 1)
                linear_by_token(pe, (0, 1, 2, 3), BASE["mla_v"], 0, 1, ckv_hi, ckv_lo)

            def load(self, act):
                act.wait_ge(merge1.ready, DT)
                act.dma_start(rope[:, :, :], rope_in).then_inc(self.rope_landed, 16)

            def scalar(self, act):
                u = BASE["mla_cq"]
                for j in range(6):
                    split_hi_to(act, u + j + 2)
                    act.wait_ge(unit_done, u + j + 1)
                    dst = (lat32[:, j, :] if j < 3 else ckv32[:, j - 3, :]) if j < 5 else krope[:, :]
                    act.activation(dst, bank(j), ACT.Copy).then_inc(self.lat, 1)
                    if j == 3:
                        split_hi_to(act, u + 6)
                        norm_cq.scalar(act)
                norm_ckv.scalar(act)
                for m in range(2 * HEADS + 2):
                    if m < 2 * HEADS:
                        h, p = m // 2, m % 2
                        u = BASE["mla_qk"] + h
                        if p == 0:
                            act.wait_ge(unit_done, u + 1)
                            if m == 0:
                                act.wait_ge(norm_cq.ready, norm_cq.base + 3)
                            else:
                                act.wait_ge(self.sin, 2 * m - 2)
                            act.activation(head32[0][:, :], bank(2 * (h % 2)), ACT.Copy).then_inc(self.q32, 1)
                    if m >= 2:
                        i = m - 2
                        act.wait_ge(self.f32, i + 1)
                        dst = (mq_hi, mk_hi)[i % 2]
                        act.activation(dst[:, i // 2, :], head_out[i % 3][:, :], ACT.Copy).then_inc(self.hi, 1)
                    if m < 2 * HEADS:
                        act.wait_ge(*((self.k32, h + 1) if p else (self.q32, h + 1)))
                        if m >= 2:
                            act.wait_ge(self.sum, m - 1)
                        act.activation(head_sq[p][:, :], head32[p][:, :], ACT.Square).then_inc(self.sq, 1)
                    if 1 <= m <= 2 * HEADS:
                        i = m - 1
                        act.wait_ge(self.sum, i + 1)
                        act.activation(std[:, :], bank(4 + i % 2), ACT.Ln, scale=1.0 / QKD,
                                       bias=col("eps")).then_inc(self.std, 1)
                        act.wait_ge(self.std, i + 1)
                        if i:
                            act.wait_ge(self.f32, i)
                        act.activation(rstd[:, :], std[:, :], ACT.Exp, scale=-0.5).then_inc(self.rstd, 1)
                    if m < 2 * HEADS and m % 2 == 0:
                        split_hi_to(act, BASE["mla_qk"] + m // 2 + 3)
                split_hi_to(act, BASE["mla_v"] + 1)
                act.wait_ge(unit_done, BASE["mla_v"] + 1)
                act.wait_ge(self.ready, 2 * HEADS)
                for t in range(TT):
                    act.activation(mv32[:, t, :], bank(t), ACT.Copy).then_inc(self.v, 1)
                split_hi_to(act, BASE["mla_v"] + 3)

            def vector(self, dve):
                dve.wait_ge(self.rope_landed, 16)
                for i, (which, gain) in enumerate(((0, "g_qn"), (1, "g_qn"), (0, "g_kn"), (1, "g_kn"))):
                    dve.tensor_scalar(tabs[:, i, :], rope[:, which, :], col(gain), None, ALU.mult).then_inc(self.tabs, 1)
                for norm, n, x in ((norm_cq, 3, lat32), (norm_ckv, 2, ckv32)):
                    clear_sum(dve)
                    for k in range(n):
                        dve.wait_ge(self.lat, (0 if n == 3 else 3) + k + 1)
                        add_square(dve, x[:, k, :])
                    norm.vector(dve)
                dve.wait_ge(self.tabs, 4)
                dve.wait_ge(self.lat, 6)
                dve.wait_ge(norm_ckv.ready, norm_ckv.base + 2)
                for m in range(2 * HEADS + 1):
                    if m < 2 * HEADS:
                        self.rotate(dve, m)
                    if 1 <= m <= 2 * HEADS:
                        i = m - 1
                        dve.wait_ge(self.rstd, i + 1)
                        dve.wait_ge(self.rot, i + 1)
                        out32 = head_out[i % 3]
                        dve.tensor_tensor(out32[:, :], out32[:, :], rstd[:, :], ALU.mult).then_inc(self.f32, 1)

            def pool(self, pool):
                for m in range(2 * HEADS + 2):
                    if m >= 2:
                        i = m - 2
                        hi, lo = ((mq_hi, mq_lo), (mk_hi, mk_lo))[i % 2]
                        pool.wait_ge(self.hi, i + 1)
                        pool.tensor_tensor(lo[:, i // 2, :], head_out[i % 3][:, :], hi[:, i // 2, :].bitcast(F32),
                                           ALU.subtract).then_inc(self.ready, 1)
                    if m % 2 == 0 and m < 2 * HEADS:
                        u = BASE["mla_qk"] + m // 2 + 2
                        stream_lo(pool, u, u + 1)

            def rotate(self, dve, m):
                h, p = m // 2, m % 2
                if p == 0:
                    dve.wait_ge(unit_done, BASE["mla_qk"] + h + 1)
                    if h:
                        dve.wait_ge(self.sq, m)
                        dve.wait_ge(self.cos, m)
                        dve.wait_ge(self.sin, 2 * m)
                    dve.tensor_tensor(head32[1][:, :], bank(2 * (h % 2) + 1), krope[:, :],
                                      ALU.add).then_inc(self.k32, 1)
                out32 = head_out[m % 3]
                dve.wait_ge(*((self.k32, h + 1) if p else (self.q32, h + 1)))
                if m >= 3:
                    dve.wait_ge(self.ready, m - 2)
                dve.tensor_tensor(out32[:, :], head32[p][:, :], tabs[:, 2 * p, :], ALU.mult).then_inc(self.cos, 1)
                sw, rows = swapped[p], slice(64, P)
                if m >= 2:
                    dve.wait_ge(self.rot, m - 1)
                for a in (64, 96):
                    dve.tensor_tensor(sw[160 - a:192 - a, :], head32[p][a:a + 32, :], tabs[a:a + 32, 2 * p + 1, :],
                                      ALU.mult).then_inc(self.sin, 1)
                dve.wait_ge(self.cos, m + 1)
                dve.wait_ge(self.sin, 2 * m + 2)
                dve.tensor_tensor(out32[rows, :], out32[rows, :], sw[rows, :], ALU.add).then_inc(self.rot, 1)

        latent = LatentProjections()
        mla = SoftmaxAttention("mla", lambda h: (mq_hi[:, h, :], mq_lo[:, h, :]),
                               lambda h: (mk_hi[:, h, :], mk_lo[:, h, :]),
                               lambda h, s: mv32[:, s, (h // 2) * P:(h // 2 + 1) * P],
                               (mprob, mprob_odd), mprobT, QKD ** -0.5, False, False)

        class AttentionGate:

            def __init__(self):
                self.sig, self.silu, self.f32, self.hi, self.ready = (
                    sem(f"attention_gate_{x}") for x in ("sigmoid", "silu", "f32", "hi", "ready"))

            def tensor(self, pe, j):
                u = BASE["mla_z"] + j
                pe.wait_ge(lo_ready, u + 1)
                pe.wait_ge(mla.exped, TT * (HEADS - 1) + j + 1)
                linear(pe, bank(j), u, h_hi, h_lo, DT)

            def scalar(self, act):
                for j in range(5):
                    if j < 4:
                        act.wait_ge(unit_done, BASE["mla_z"] + j + 1)
                        act.wait_ge(*((self.silu, j - 1) if j >= 2 else (filters.ready, 7 + j)))
                        act.activation(stage32[j % 2][:, :], bank(j), ACT.Sigmoid).then_inc(self.sig, 1)
                    if j == 3:
                        split_hi_to(act, BASE["mla_z"] + 7)
                    if j:
                        act.wait_ge(self.f32, j)
                        act.activation(ya_hi[:, j - 1, :], std[:, :], ACT.Copy).then_inc(self.hi, 1)

            def vector(self, dve):
                dve.wait_ge(mla.out, HEADS)
                for j in range(4):
                    dve.wait_ge(self.sig, j + 1)
                    dve.tensor_tensor(square[:, :], stage32[j % 2][:, :], bank(j), ALU.mult).then_inc(self.silu, 1)
                    dve.wait_ge(self.silu, j + 1)
                    dve.tensor_tensor(std[:, :], square[:, :], y32[:, j, :], ALU.mult).then_inc(self.f32, 1)
                    dve.wait_ge(self.hi, j + 1)
                    dve.tensor_tensor(ya_lo[:, j, :], std[:, :], ya_hi[:, j, :].bitcast(F32),
                                      ALU.subtract).then_inc(self.ready, 1)
                    dve.wait_ge(self.ready, j + 1)

        attention_gate = AttentionGate()

        class Filters:

            TILES = [(0, 0), (0, 1), (1, 2), (1, 3), (0, 2), (0, 3), (1, 0), (1, 1)]
            EARLY = [(0, 1), (2, 3), (4,), (5, 6, 7)]
            BANKS = [6, 0, 2, 6, 0, 2, 0, 6]

            def __init__(self):
                (self.landed, self.skip_landed, self.layer, self.arg, self.turn, self.act, self.tile, self.f32,
                 self.bias, self.hi, self.ready, self.even, self.spec) = (
                    sem(f"filter_{x}") for x in ("landed", "skip_landed", "layer", "argument", "turn", "sine", "tile",
                                                 "f32", "bias", "hi", "ready", "even", "spectrum"))

            def load(self, act):
                act.wait_ge(mla.scores, TT * HEADS)
                for dst, src in ((posT[:, :], pos_in), (wf1[:, :], wf1_in), (wf2[:, :], wf2_in), (wf3[:, :], wf3_in),
                                 (decay[:, :, :], decay_in)):
                    act.dma_start(dst, src).then_inc(self.landed, 16)

            def load_skip(self, act):
                act.wait_ge(mla.summed, TT * HEADS)
                act.dma_start(hyb[:, :, :], hyb_in).then_inc(self.skip_landed, 16)

            def kf(self, o, i):
                if o and i < 5:
                    return kf_early[i][0][:, :], kf_early[i][1][:, :]
                return kf_hi[:, i, :], kf_lo[:, i, :]

            def tensor_layer(self, pe, i):
                if i == 0:
                    pe.wait_ge(self.landed, 80)
                    pe.wait_ge(mla.copied0, 2 * HEADS)
                    pe.matmul(bank(4)[0:64, :], wf1[:, :], posT[:, :], start=True, stop=True).then_inc(self.layer, 1)
                else:
                    pe.wait_ge(self.act, 1)
                    pe.matmul(bank(4)[0:64, :], wf2[:, :], hid[0][:, :], start=True, stop=True).then_inc(self.layer, 1)

            def tensor_tile(self, pe, o, i):
                n = 8 * o + i
                if n == 0:
                    pe.wait_ge(self.act, 2)
                elif n == 1:
                    pe.wait_ge(mla.copied1, 2 * HEADS)
                else:
                    pe.wait_ge(self.f32, n - 1)
                side, t = self.TILES[i]
                c = (2 * o + side) * T
                pe.matmul(bank(4 + n % 2), hid[1][:, t * P:(t + 1) * P], wf3[:, c:c + T],
                          start=True, stop=True).then_inc(self.tile, 1)

            def tensor_unit(self, pe, o, m):
                n = 4 * o + m
                u = BASE["spectra"] + n
                pe.wait_ge(lo_ready, u + 1)
                before = [i for i in range(n) if self.BANKS[i] == self.BANKS[n]]
                if before:
                    pe.wait_ge(self.spec, 2 * before[-1] + 2)
                elif n == 0:
                    pe.wait_ge(mla.out, HEADS)
                else:
                    pe.wait_ge(attention_gate.silu, self.BANKS[n] + 2)
                for odd in range(2):
                    for c, (w_hi, w_lo) in enumerate(weight_chunks(u, 4 * odd, 4)):
                        i = 4 * odd + c
                        if m == 0:
                            pe.wait_ge(self.ready, 8 * o + i + 1)
                        k_hi_, k_lo_ = self.kf(o, i)
                        last = products(pe, bank(self.BANKS[n] + odd), [(w_hi, w_lo, k_hi_, k_lo_)],
                                        start=c == 0, stop=c == 3)
                last.then_inc(unit_done, 1)

            def tensor(self, pe):
                for o in range(2):
                    for m in range(4):
                        self.tensor_unit(pe, o, m)
                        if o == 0:
                            for i in self.EARLY[m]:
                                self.tensor_tile(pe, 1, i)

            def scalar_sine(self, act, i):
                act.wait_ge(self.turn, 5 * i + 5)
                act.activation(hid[i][:, :], sumsq[0:64, :], ACT.Sin).then_inc(self.act, 1)

            def scalar_tile(self, act, o, i):
                n = 8 * o + i
                act.wait_ge(self.f32, n + 1)
                if i == 0:
                    act.wait_ge(self.bias, o + 1)
                if o and i >= 5:
                    act.wait_ge(unit_done, BASE["spectra"] + 4)
                act.activation(self.kf(o, i)[0], stage32[n % 2][:, :], ACT.Copy).then_inc(self.hi, 1)

            def scalar_unit(self, act, o, m):
                n = 4 * o + m
                u = BASE["spectra"] + n
                split_hi_to(act, u + 2)
                act.wait_ge(unit_done, u + 1)
                part, j = m // 2, m % 2
                act.activation(spec[o][:, 4 * part + j, :], bank(self.BANKS[n]), ACT.Copy).then_inc(self.even, 1)

            def scalar(self, act):
                for m in range(4):
                    self.scalar_unit(act, 0, m)
                    for i in self.EARLY[m]:
                        self.scalar_tile(act, 1, i)
                for m in range(4):
                    self.scalar_unit(act, 1, m)

            def vector_layer(self, dve, i):
                a, r = rstd[0:64, :], sumsq[0:64, :]
                c1 = 6.28125
                dve.wait_ge(self.layer, i + 1)
                dve.tensor_scalar(a, bank(4)[0:64, :], col(f"b_f{i + 1}", p=64), col(f"freq_{i + 1}", p=64), ALU.add,
                                  ALU.mult).then_inc(self.arg, 1)
                dve.wait_ge(self.arg, i + 1)

                def turn(ins):
                    ins.then_inc(self.turn, 1)
                    counts["turn"] = counts.get("turn", 0) + 1
                    dve.wait_ge(self.turn, counts["turn"])

                if i:
                    dve.wait_ge(self.act, 1)
                turn(dve.tensor_scalar(r, a, 1.0 / (2 * math.pi), BIG, ALU.mult, ALU.add))
                turn(dve.tensor_scalar(r, r, BIG, None, ALU.subtract))
                turn(dve.scalar_tensor_tensor(a, r, -c1, a, ALU.mult, ALU.add))
                turn(dve.scalar_tensor_tensor(r, r, -(2 * math.pi - c1), a, ALU.mult, ALU.add))
                turn(dve.tensor_scalar(r, r, 3.1415925, -3.1415925, ALU.min, ALU.max))

            def vector_tile(self, dve, o, i):
                n = 8 * o + i
                if n >= 2:
                    dve.wait_ge(self.ready, n - 1)
                dve.wait_ge(self.tile, n + 1)
                f32 = stage32[n % 2]
                dve.tensor_tensor(f32[:, :], bank(4 + n % 2), decay[:, self.TILES[i][1], :],
                                  ALU.mult).then_inc(self.f32, 1)
                if i == 0:
                    dve.wait_ge(self.f32, n + 1)
                    dve.wait_ge(self.skip_landed, 16)
                    dve.tensor_tensor(f32[0:1, :], f32[0:1, :], hyb[0:1, o, :], ALU.add).then_inc(self.bias, 1)
                    dve.wait_ge(self.bias, o + 1)

            def vector_tile_lo(self, dve, o, i):
                n = 8 * o + i
                hi, lo = self.kf(o, i)
                dve.wait_ge(self.hi, n + 1)
                dve.tensor_tensor(lo, stage32[n % 2][:, :], hi.bitcast(F32), ALU.subtract).then_inc(self.ready, 1)

            def vector_tiles(self, dve, o, tiles):
                for j, i in enumerate(tiles):
                    self.vector_tile(dve, o, i)
                    if j:
                        self.vector_tile_lo(dve, o, i - 1)
                self.vector_tile_lo(dve, o, tiles[-1])

            def vector_unit(self, dve, o, m):
                n = 4 * o + m
                part, j = m // 2, m % 2
                low, high, odd = spec[o][:, 4 * part + j, :], spec[o][:, 4 * part + 2 + j, :], bank(self.BANKS[n] + 1)
                dve.wait_ge(self.even, n + 1)
                a, b = (odd, low) if part else (low, odd)
                dve.tensor_tensor(high, a, b, ALU.subtract).then_inc(self.spec, 1)
                dve.wait_ge(self.spec, 2 * n + 1)
                dve.tensor_tensor(low, low, odd, ALU.add).then_inc(self.spec, 1)

            def vector(self, dve):
                for m in range(4):
                    self.vector_unit(dve, 0, m)
                    self.vector_tiles(dve, 1, self.EARLY[m])
                for m in range(4):
                    self.vector_unit(dve, 1, m)

        filters = Filters()

        def gate_and_filters_tensor(pe):
            filters.tensor_layer(pe, 0)
            attention_gate.tensor(pe, 1)
            filters.tensor_layer(pe, 1)
            attention_gate.tensor(pe, 2)
            for i in range(2):
                filters.tensor_tile(pe, 0, i)
            attention_gate.tensor(pe, 3)
            for i in range(2, 8):
                filters.tensor_tile(pe, 0, i)
            filters.tensor(pe)

        def gate_and_filters_scalar(act):
            filters.load_skip(act)
            split_hi_to(act, BASE["mla_z"] + 3)
            filters.scalar_sine(act, 0)
            split_hi_to(act, BASE["mla_z"] + 4)
            filters.scalar_sine(act, 1)
            for i in range(8):
                if i in (2, 6):
                    split_hi_to(act, BASE["mla_z"] + (5 if i == 2 else 6))
                filters.scalar_tile(act, 0, i)
            attention_gate.scalar(act)
            filters.scalar(act)

        def gate_and_filters_vector(dve):
            for i in range(2):
                filters.vector_layer(dve, i)
            filters.vector_tiles(dve, 0, range(8))
            attention_gate.vector(dve)
            filters.vector(dve)

        def long_unit(i, z):
            return BASE[f"long{i // 2}"] + (1, 5)[i % 2] + z

        class HyenaInputs:

            def __init__(self):
                (self.mid, self.left, self.conv, self.turned, self.hi, self.copied, self.ready, self.sig, self.silu,
                 self.x2z) = (
                    sem(f"hyena_{x}") for x in ("middle", "left", "conv", "transposed", "v_hi", "x1", "v_ready",
                                                "sigmoid", "silu", "x2z"))

            def target(self, j):
                return conv[j % 2][:, :] if j < 8 else x2z[:, j - 8, :]

            def tensor(self, pe):
                for j in range(9):
                    if j < 8:
                        u = BASE["hy_in"] + j
                        pe.wait_ge(lo_ready, u + 1)
                        if j < 4:
                            pe.wait_ge(filters.spec, 14 if j < 2 else 12)
                        else:
                            pe.wait_ge(self.conv, j - 3)
                        linear(pe, bank(j % 4), u, h_hi, h_lo, DT)
                    if 1 <= j <= 8:
                        i = j - 1
                        pe.wait_ge(self.conv, i + 1)
                        if i == 0:
                            pe.wait_ge(filters.spec, 16)
                        if i >= 2:
                            pe.wait_ge(*((self.ready, i - 1) if i < 6 else (self.copied, i - 5)))
                        for t in range(TT):
                            last = pe.transpose(psum[:, 512 * (4 + i % 2) + t * P:512 * (4 + i % 2) + (t + 1) * P],
                                                conv[i % 2][:, 256 * (t % 2) + t // 2:min(256 * (t % 2) + t // 2 + 256, T):2],
                                                ident)
                        last.then_inc(self.turned, 1)

            def middle(self, act, j, b):
                act.activation(self.target(j), b, ACT.Identity, scale=col("w_short", 3 * j + 1),
                               bias=col("b_short", j)).then_inc(self.mid, 1)

            def sides(self, dve, j, b):
                dst = self.target(j)
                dve.wait_ge(self.mid, j + 1)
                dve.scalar_tensor_tensor(dst[:, 1:T], b[:, 0:T - 1], col("w_short", 3 * j), dst[:, 1:T],
                                         ALU.mult, ALU.add).then_inc(self.left, 1)
                dve.wait_ge(self.left, j + 1)
                dve.scalar_tensor_tensor(dst[:, 0:T - 1], b[:, 1:T], col("w_short", 3 * j + 2), dst[:, 0:T - 1],
                                         ALU.mult, ALU.add).then_inc(self.conv, 1)

            def scalar_x2(self, act, i, b):
                act.wait_ge(unit_done, long_unit(i, 0) + 1)
                self.middle(act, 8 + i, b)

            def scalar_z(self, act, i, b):
                act.wait_ge(unit_done, long_unit(i, 1) + 1)
                if i:
                    act.wait_ge(self.x2z, i)
                else:
                    act.wait_ge(self.ready, 4)
                act.activation(zsilu, b, ACT.Sigmoid).then_inc(self.sig, 1)

            def vector_z(self, dve, i, b):
                dve.wait_ge(self.sig, i + 1)
                dve.tensor_tensor(zsilu, zsilu, b, ALU.mult).then_inc(self.silu, 1)
                dve.wait_ge(self.silu, i + 1)
                dve.wait_ge(self.conv, 9 + i)
                dve.tensor_tensor(x2z[:, i, :], x2z[:, i, :], zsilu, ALU.mult).then_inc(self.x2z, 1)

            def by_token(self, i, x):
                return x[:, :, (i % 4) * P:(i % 4 + 1) * P]

            def turned_bank(self, i):
                return bank(4 + i % 2).rearrange("p (t c) -> p t c", t=TT)

            def scalar(self, act):
                for j in range(9):
                    if j < 8:
                        split_hi_to(act, BASE["hy_in"] + j + 2)
                        act.wait_ge(unit_done, BASE["hy_in"] + j + 1)
                        if 2 <= j < 8:
                            act.wait_ge(self.turned, j - 1)
                        if j == 0:
                            act.wait_ge(filters.ready, 16)
                        self.middle(act, j, bank(j % 4))
                    if 1 <= j <= 8:
                        i = j - 1
                        act.wait_ge(self.turned, i + 1)
                        dst = self.by_token(i, v_hi if i < 4 else x1tok)
                        act.activation(dst, self.turned_bank(i), ACT.Copy).then_inc(self.hi if i < 4 else self.copied, 1)

            def vector(self, dve):
                for j in range(9):
                    if j < 8:
                        self.sides(dve, j, bank(j % 4))
                    if 1 <= j <= 4:
                        i = j - 1
                        dve.wait_ge(self.hi, i + 1)
                        dve.tensor_tensor(self.by_token(i, v_lo), self.turned_bank(i),
                                          self.by_token(i, v_hi).bitcast(F32), ALU.subtract).then_inc(self.ready, 1)

        hyena_in = HyenaInputs()

        class LongConvolution:

            signals = [sem(f"long_{x}") for x in ("even", "halves", "products", "upper_products", "spectrum", "f32",
                                                  "hi", "ready", "back", "gated", "gated_hi", "out")]

            def __init__(self, o):
                self.o = o
                (self.even, self.halves, self.prod, self.upper_prod, self.y, self.f32, self.hi, self.ready, self.back,
                 self.out32, self.out_hi, self.out) = LongConvolution.signals
                self.even_sum = conv
                self.low = (std, rstd)
                self.lower = prod
                self.upper = (square, sumsq, *stage32)
                self.parts = (prod[1], prod[3], prod[0], prod[2])

            def forth(self, j):
                return 4 * ((self.o + j) % 2)

            def unit_forth(self, j):
                return BASE[f"long{self.o}"] + 3 * j

            def unit_back(self, j):
                return BASE[f"long{self.o}"] + 4 + 3 * j

            def side_bank(self, z):
                return bank(self.forth(1) + 2 + z)

            def spectrum(self, j):
                return [spec[self.o][:, i + j, :] for i in (0, 4, 2, 6)]

            def tensor(self, pe):
                for j in range(2):
                    self.tensor_forth(pe, j)
                    if j:
                        self.tensor_back(pe, 0)
                        pe.wait_ge(self.halves, 8 * self.o + 8)
                    for z in range(2):
                        u = long_unit(2 * self.o + j, z)
                        pe.wait_ge(lo_ready, u + 1)
                        linear(pe, self.side_bank(z), u, h_hi, h_lo, DT)
                self.tensor_back(pe, 1)

            def tensor_forth(self, pe, j):
                o, u = self.o, self.unit_forth(j)
                pe.wait_ge(lo_ready, u + 1)
                if o and j:
                    pe.wait_ge(self.out32, 4)
                elif o == 0:
                    pe.wait_ge(hyena_in.ready, 4)
                    pe.wait_ge(*((hyena_in.copied, 4) if j else (hyena_in.conv, 8)))
                for g in range(4):
                    t = 2 * (g % 2)
                    if j and g >= 2:
                        pe.wait_ge(*((hyena_in.conv, 9 + 2 * o) if g == 2 else (hyena_in.silu, 1 + 2 * o)))
                    linear(pe, bank(self.forth(j) + g), u, v_hi[:, t:t + 2, :], v_lo[:, t:t + 2, :], 2, first=2 * g,
                           chunk_ready=self.out if o and j == 0 and g < 2 else None, ready_base=t, signal=g == 3)

            def tensor_back(self, pe, j):
                o, u = self.o, self.unit_back(j)
                s = u % 2
                pe.wait_ge(lo_ready, u + 1)
                pe.wait_ge(self.ready, 8 * o + 4 * j + 4)
                for t in range(4):
                    if o == 0:
                        y = 4 * (t // 2) + j
                        terms = [(whi[s][:, c * T + t * P:c * T + (t + 1) * P], wlo[s][:, c * T + t * P:c * T + (t + 1) * P],
                                  Y_hi[:, y + 2 * c, :], Y_lo[:, y + 2 * c, :]) for c in range(2)]
                        last = products(pe, bank(4 * o + t), terms, start=j == 0, stop=j == 1)
                    else:
                        for odd in range(2):
                            y, cols, a = 4 * odd + j, slice(t * P, (t + 1) * P), 256 * odd
                            terms = [(Y_hi[:, y + 2 * c, cols], Y_lo[:, y + 2 * c, cols],
                                      whi[s][:, c * T + a:c * T + a + 256], wlo[s][:, c * T + a:c * T + a + 256])
                                     for c in range(2)]
                            last = products(pe, bank(4 * o + t)[:, a:a + 256], terms, start=j == 0 and odd == 0,
                                            stop=j == 1, skip_group_check=True)
                    if j == 1 and t < 3:
                        last.then_inc(self.back, 1)
                last.then_inc(unit_done, 1)

            def scalar(self, act):
                o, base = self.o, BASE[f"long{self.o}"]
                for j in range(2):
                    n = 2 * o + j
                    split_hi_to(act, self.unit_forth(j) + 2)
                    act.wait_ge(unit_done, self.unit_forth(j) + 1)
                    if n:
                        act.wait_ge(self.upper_prod, 4 * n)
                    for i in range(2):
                        act.activation(self.even_sum[i][:, :], bank(self.forth(j) + 2 * i), ACT.Copy).then_inc(self.even, 1)
                    if j == 0:
                        split_hi_to(act, base + 3)
                        hyena_in.scalar_x2(act, n, self.side_bank(0))
                        split_hi_to(act, base + 4)
                    else:
                        split_hi_to(act, base + 7)
                    for g in range(4):
                        act.wait_ge(self.f32, 4 * n + g + 1)
                        act.activation(Y_hi[:, 2 * g + j, :], self.parts[g][:, :], ACT.Copy).then_inc(self.hi, 1)
                    if j:
                        hyena_in.scalar_x2(act, n, self.side_bank(0))
                        split_hi_to(act, base + 8)
                    hyena_in.scalar_z(act, n, self.side_bank(1))
                split_hi_to(act, base + 10)
                for j in range(4):
                    act.wait_ge(self.out32, 4 * o + j + 1)
                    act.activation(yb_hi[:, j, :], stage32[j % 2][:, :], ACT.Copy).then_inc(self.out_hi, 1)

            def multiply(self, eng, signal, k, x, dst):
                for d, (a, b) in zip(dst, ((0, 0), (1, 1), (0, 1), (1, 0))):
                    eng.tensor_tensor(d[:, :], k[a], x[b][:, :], ALU.mult).then_inc(signal, 1)

            def pool(self, pool):
                o = self.o
                for j in range(2):
                    n = 2 * o + j
                    if j == 0:
                        stream_lo(pool, BASE[f"long{o}"] + 2, BASE[f"long{o}"] + 3)
                    pool.wait_ge(self.halves, 4 * n + 4)
                    if n:
                        pool.wait_ge(self.f32, 4 * n)
                    self.multiply(pool, self.upper_prod, self.spectrum(j)[2:], self.even_sum, self.upper)
                    u = BASE[f"long{o}"]
                    stream_lo(pool, *((u + 3, u + 6) if j == 0 else (u + 6, u + 8)))

            def vector(self, dve):
                o = self.o
                low, high, lower, upper = self.low, self.even_sum, self.lower, self.upper
                for j in range(2):
                    n, b = 2 * o + j, self.forth(j)
                    dve.wait_ge(self.even, 2 * n + 2)
                    if n:
                        dve.wait_ge(self.prod, 4 * n)
                        dve.wait_ge(self.ready, 4 * n)
                    for i in range(2):
                        dve.tensor_tensor(low[i][:, :], high[i][:, :], bank(b + 2 * i + 1), ALU.add).then_inc(self.halves, 1)
                    dve.wait_ge(self.halves, 4 * n + 2)
                    dve.tensor_tensor(high[0][:, :], high[0][:, :], bank(b + 1), ALU.subtract).then_inc(self.halves, 1)
                    dve.tensor_tensor(high[1][:, :], bank(b + 3), high[1][:, :], ALU.subtract).then_inc(self.halves, 1)
                    self.multiply(dve, self.prod, self.spectrum(j)[:2], low, lower)
                    if j == 0:
                        hyena_in.sides(dve, 8 + n, self.side_bank(0))
                    for i, (half, signal) in enumerate(((lower, self.prod), (upper, self.upper_prod))):
                        dve.wait_ge(signal, 4 * n + 4)
                        dve.tensor_tensor(half[0][:, :], half[0][:, :], half[1][:, :], ALU.subtract).then_inc(self.y, 1)
                        dve.tensor_tensor(half[2][:, :], half[2][:, :], half[3][:, :], ALU.add).then_inc(self.y, 1)
                    dve.wait_ge(self.y, 4 * n + 4)
                    re, im, re_high, im_high = lower[0], lower[2], upper[0], upper[2]
                    for g, (a, c, op) in enumerate(((re, re_high, ALU.add), (im, im_high, ALU.subtract),
                                                    (re, re_high, ALU.subtract), (im, im_high, ALU.add))):
                        if g == 2:
                            dve.wait_ge(self.f32, 4 * n + 2)
                        dve.tensor_tensor(self.parts[g][:, :], a[:, :], c[:, :], op).then_inc(self.f32, 1)
                    for g in range(4):
                        dve.wait_ge(self.hi, 4 * n + g + 1)
                        dve.tensor_tensor(Y_lo[:, 2 * g + j, :], self.parts[g][:, :],
                                          Y_hi[:, 2 * g + j, :].bitcast(F32), ALU.subtract).then_inc(self.ready, 1)
                    if j:
                        hyena_in.sides(dve, 8 + n, self.side_bank(0))
                    hyena_in.vector_z(dve, n, self.side_bank(1))
                for j in range(5):
                    if j < 4:
                        dve.wait_ge(*((self.back, 3 * o + j + 1) if j < 3 else (unit_done, self.unit_back(1) + 1)))
                        if j >= 2:
                            dve.wait_ge(self.out, 4 * o + j - 1)
                        x, y, z = (x1tok, x2z)[o][:, j, :], bank(4 * o + j), stage32[j % 2][:, :]
                        if o:
                            x, z = (v.rearrange("p (t e) -> p e t", e=2) for v in (x, z))
                            y = y.rearrange("p (e t) -> p e t", e=2)
                        dve.tensor_tensor(z, x, y, ALU.mult).then_inc(self.out32, 1)
                    if j:
                        dve.wait_ge(self.out_hi, 4 * o + j)
                        dve.tensor_tensor(yb_lo[:, j - 1, :], stage32[(j - 1) % 2][:, :],
                                          yb_hi[:, j - 1, :].bitcast(F32), ALU.subtract).then_inc(self.out, 1)
                dve.wait_ge(self.out, 4 * o + 4)

        long0, long1 = LongConvolution(0), LongConvolution(1)
        merge2 = Merge(2, "b_gate", XS["out2"], [(attention_gate.ready, 4), (long1.out, 8)], False, None)

        block = ctx.enter_context(nc.Block())
        stored = sem("stored")

        @block.sync
        def _(sp):
            load_unit(sp, 0, 0, "k", 0)
            for i in range(4):
                sp.dma_start(xT[:, 2 * i:2 * i + 2, :], x_in[:, 2 * i:2 * i + 2, :]).then_inc(x_landed[i], 16)
            load_unit(sp, 1, 0, "k", 1)
            stream_loads(sp)
            sp.wait_ge(x_updated, XS["out2"] + DT)
            sp.dma_start(out, xT[:, :, :]).then_inc(stored, 16)
            sp.wait_ge(stored, 16)

        @block.gpsimd
        def _(pool):
            stream_lo(pool, 0, BASE["mla_qk"] + 2)
            latent.pool(pool)
            stream_lo(pool, BASE["mla_qk"] + HEADS + 2, BASE["long0"] + 2)
            long0.pool(pool)
            stream_lo(pool, BASE["long1"], BASE["long1"] + 2)
            long1.pool(pool)
            stream_lo(pool, BASE["merge2"], UNITS)

        @block.scalar
        def _(act):
            act.dma_start(vec[:, :], vec_in).then_inc(vec_landed, 16)
            act.dma_start(constf[:, :, :], constf_in).then_inc(const_landed, 16)
            split_hi_to(act, 1)
            for k in range(DT):
                act.wait_ge(x_landed[k // 2], 16)
                if k >= 2:
                    act.wait_ge(summed, k)
                act.activation(first_square[k % 2][:, :], xT[:, k, :], ACT.Square).then_inc(squared, 1)
                if k == 5:
                    split_hi_to(act, 2)
            act.wait_ge(vec_landed, 16)
            ffn1.scalar(act)
            act.dma_start(sel32[:, :, :], sel_in).then_inc(foxp.sel_landed, 16)
            act.dma_start(constr32[:, :, :], constr_in).then_inc(constr_landed, 16)
            split_hi_to(act, BASE["fox_q"] + 2)
            norm_mix.scalar(act)
            foxp.scalar(act)
            fox.scalar(act)
            stickp.scalar(act)
            stick.scalar(act)
            merge1.scalar(act)
            split_hi_to(act, BASE["ffn2_up0"] + 2)
            ple.load(act)
            ffn2.scalar(act)
            split_hi_to(act, BASE["ple"] + 2)
            ple.scalar(act)
            latent.load(act)
            split_hi_to(act, BASE["mla_cq"] + 2)
            norm_block2.scalar(act)
            latent.scalar(act)
            mla.scalar(act, filters.load)
            gate_and_filters_scalar(act)
            hyena_in.scalar(act)
            long0.scalar(act)
            long1.scalar(act)
            merge2.scalar(act)

        @block.vector
        def _(dve):
            dve.memset(small[:, :], 0.0).then_inc(x_updated, 2)
            clear_sum(dve)
            dve.wait_ge(vec_landed, 16)
            for k in range(DT):
                if k % 2 == 0:
                    dve.wait_ge(x_landed[k // 2], 16)
                split_gained(dve, xT[:, k, :], "ffn1_norm", k)
                dve.wait_ge(squared, k + 1)
                dve.wait_ge(summed, k + 1)
                dve.tensor_tensor(sumsq[:, :], sumsq[:, :], first_square[k % 2][:, :], ALU.add).then_inc(summed, 1)
            counts["sq"] += DT
            counts["sum"] += DT
            ffn1.vector(dve)
            norm_mix.vector(dve)
            foxp.vector(dve)
            fox.vector(dve)
            stickp.vector(dve)
            merge1.open_first(dve)
            stick.vector(dve)
            merge1.vector(dve)
            ffn2.vector(dve)
            ple.vector(dve)
            norm_block2.vector(dve)
            latent.vector(dve)
            mla.vector(dve)
            gate_and_filters_vector(dve)
            hyena_in.vector(dve)
            long0.vector(dve)
            merge2.open_first(dve)
            long1.vector(dve)
            merge2.vector(dve)

        @block.tensor
        def _(pe):
            ffn1.tensor(pe)
            norm_mix.tensor(pe)
            foxp.tensor(pe, norm_mix)
            fox.tensor(pe, [(constr_ready, 1), (foxp.sel, 1), (foxp.ready, 12), (foxp.forget, 6), (foxp.v, TT)],
                       stickp.tensor_unit)
            stickp.tensor(pe)
            stick.tensor(pe)
            merge1.tensor(pe)
            ffn2.tensor(pe)
            ple.tensor(pe)
            norm_block2.tensor(pe)
            latent.tensor(pe)
            mla.tensor(pe, [(latent.ready, 2 * HEADS), (latent.v, TT)], attention_gate.tensor)
            gate_and_filters_tensor(pe)
            hyena_in.tensor(pe)
            long0.tensor(pe)
            long1.tensor(pe)
            merge2.tensor(pe)


def _feature_units(w):
    kk, n = w.shape
    return w.reshape(kk // P, P, n // P, P).transpose(2, 1, 0, 3).reshape(n // P, P, kk)


def _token_units(w):
    kk, n = w.shape
    return w.reshape(kk // 256, 2, P, n).transpose(0, 2, 1, 3).reshape(kk // 256, P, 2 * n)


def _wide(u, n=1024):
    out = np.zeros((u.shape[0], P, n), np.float32)
    out[:, :, :u.shape[2]] = u
    return out


def _columns(v):
    return np.ascontiguousarray(v.reshape(-1, P).T)


def _rope_rows(a, axis=0):
    a = np.moveaxis(a, axis, 0)
    out = np.zeros((P,) + a.shape[1:], np.float32)
    out[0:64] = a[0:64]
    out[64:80] = a[64:80]
    out[96:112] = a[80:96]
    return np.moveaxis(out, 0, axis)


def _constants():
    i = np.arange(P)
    eye = np.eye(P, dtype=np.float32)
    blocks = (i[:, None] // HD == i[None, :] // HD).astype(np.float32)
    before = (i[:, None] < i[None, :]).astype(np.float32)
    constf = np.stack([eye, blocks, np.ones((P, P), np.float32), before], 1)
    tri = -(i[:, None] >= i[None, :]).astype(np.float32)
    mask_qk = np.where(i[None, :] > i[:, None], np.float32(NEG), np.float32(0))
    mask_kq = np.where(i[:, None] >= i[None, :], np.float32(NEG), np.float32(0))
    constr = np.stack([eye, tri, -np.ones((P, P), np.float32), mask_qk, mask_kq], 1)
    sel = np.zeros((P, HEADS, P), np.float32)
    for h in range(HEADS):
        sel[h, h, :] = 1
    pos = np.arange(T, dtype=np.float32)
    inv = (np.float32(ROPE_THETA) ** (-np.arange(0, ROPE, 2, dtype=np.float32) / np.float32(ROPE))).astype(np.float32)
    ang = (pos[:, None] * inv[None, :]).astype(np.float32)
    c, s = np.cos(ang).T, np.sin(ang).T
    rope = np.zeros((P, 2, T), np.float32)
    rope[0:64, 0] = 1
    rope[64:80, 0], rope[96:112, 0] = c, c
    rope[64:80, 1], rope[96:112, 1] = s, -s
    t = np.linspace(0.0, 1.0, T, dtype=np.float32)
    lo, hi = math.log(1e-2) / 1.5, math.log(1e-2) / 0.3
    deltas = np.abs(np.linspace(lo, hi, T, dtype=np.float32))
    parity = np.concatenate([np.arange(0, T, 2), np.arange(1, T, 2)])
    decay = np.exp(-t[:, None] * deltas).astype(np.float32)[parity].reshape(TT, P, T).transpose(1, 0, 2)
    bands = 16
    f = np.linspace(1e-4, bands - 1, bands, dtype=np.float32)
    a2 = (np.float32(2.0 * np.pi / T) * pos[:, None] * f[None, :]).astype(np.float32)
    posT = np.concatenate([t[:, None], np.cos(a2), -np.sin(a2)], -1).T.astype(np.float32)[:, parity]
    n = np.arange(T, dtype=np.float64)
    f = np.concatenate([np.arange(T // 2), T - 1 - np.arange(T // 2)])
    w = np.pi * (2 * f + 1) / (2 * T)
    th, th1 = n[:, None] * w, (n[:, None] + 1) * w
    fwd = np.concatenate([np.cos(th), -np.sin(th)], 1).astype(np.float32)
    neg = np.concatenate([np.cos(th1), np.sin(th1)], 1).astype(np.float32)
    inv_ = (np.concatenate([np.cos(th.T), -np.sin(th.T)], 0) / T).astype(np.float32)
    taps = np.concatenate([fwd[parity], neg[parity]], 0).reshape(8, P, 2 * T)
    lower = np.concatenate([np.arange(T // 2), T + np.arange(T // 2)])
    slots = [0, 1, 6, 7, 2, 3, 4, 5]
    spectra = _feature_units(taps[slots].reshape(2 * T, 2 * T)[:, lower])
    fwd_units = np.stack([np.concatenate([taps[t][:, c * T + j * P:c * T + (j + 1) * P] for c in range(2) for t in range(4)], 1)
                          for j in range(2)])
    inv_units = np.stack([np.concatenate([inv_[c * T + j * P:c * T + (j + 1) * P][:, parity] for c in range(2)], 1)
                          for j in range(2)])
    return constf, constr, sel, rope, decay, posT, spectra, fwd_units, inv_units


def kernel(**inputs):
    import concourse.bacc as _bacc
    from concourse.bass_utils import run_bass_kernel_spmd as _run

    g = {k: np.ascontiguousarray(v) for k, v in inputs.items()}
    constf, constr, sel, rope, decay, posT, spectra, fwd_units, inv_units = _constants()

    def cols(w, a, n):
        return w[:, a:a + n]

    ks, ds = [], []
    for n in ("1", "2"):
        up = np.stack([_feature_units(g[f"ffn{n}_w_gate"][0]), _feature_units(g[f"ffn{n}_w_up"][0])], 1)
        down = g[f"ffn{n}_w_down"][0]
        halves = []
        for half in range(2):
            halves.append(up[half * FH:(half + 1) * FH].reshape(2 * FH, P, D))
            ds.append(_feature_units(down[half * FH * P:(half + 1) * FH * P]))
        ks.append(halves)
    w1 = g["w_in"][0]
    fq, fk, fv, fl, sq, sk, sv, gf, gs = [w1[:, a:b] for a, b in zip(
        [0, 512, 1024, 1536, 1544, 2056, 2568, 3080, 4104], [512, 1024, 1536, 1544, 2056, 2568, 3080, 4104, 5128])]
    flp = np.zeros((D, P), np.float32)
    flp[:, 0:HEADS] = fl

    def merge_units(ga, gb, ba, bb):
        both = np.concatenate([_feature_units(ba), _feature_units(bb)], 2)
        return np.stack([_feature_units(ga), _feature_units(gb), both], 1).reshape(3 * DT, P, D)

    w2 = g["w_in_2"][0]
    edges = np.cumsum([0, 1536, 512, 384, 256, 32, 512, 1024, 1024])
    hy, zh, cq, ckv, kr, za, gh, ga = [w2[:, a:b] for a, b in zip(edges[:-1], edges[1:])]
    krp = np.zeros((D, P), np.float32)
    krp[:, 64:80], krp[:, 96:112] = kr[:, 0:16], kr[:, 16:32]
    uq = _rope_rows(g["w_uq_2"][0].reshape(384, HEADS, QKD), 2)
    ukv = g["w_ukv_2"][0].reshape(256, HEADS, P)
    uk = np.zeros((256, HEADS, P), np.float32)
    uk[:, :, 0:64] = ukv[:, :, 0:64]
    qk = np.concatenate([_feature_units(uq.reshape(384, D)), _feature_units(uk.reshape(256, D))], 2)
    uv = np.ascontiguousarray(ukv[:, :, 64:128]).reshape(256, 512)
    x2u, zu = _feature_units(hy[:, 2 * T:]), _feature_units(zh)
    longs = [a[i:i + 1] for o in (0, 1) for a, i in (
        (fwd_units, 0), (x2u, 2 * o), (zu, 2 * o), (fwd_units, 1), (inv_units, 0), (x2u, 2 * o + 1), (zu, 2 * o + 1),
        (inv_units, 1))]
    wk = np.concatenate([
        ks[0][0], ks[0][1],
        _feature_units(fq), _feature_units(fk), _feature_units(flp), _token_units(fv),
        _feature_units(sq), _feature_units(sk), _token_units(sv),
        merge_units(gf, gs, g["w_branch_fox"][0], g["w_branch_sb"][0]), _feature_units(g["w_out"][0]),
        ks[1][0], ks[1][1],
        _feature_units(cq), _feature_units(ckv), _feature_units(krp), _wide(qk), _token_units(uv), _feature_units(za),
        spectra, spectra, _feature_units(hy[:, :2 * T]), *longs,
        merge_units(ga, gh, g["w_attn_out_2"][0], g["w_hy_out_2"][0]), _feature_units(g["w_out_2"][0]),
    ], 0)
    assert wk.shape[0] == _at["k"]
    wd = np.concatenate(ds, 0)
    wp = np.concatenate([_feature_units(g["w_ple_gate"][0]), _feature_units(g["w_ple_proj"][0])], 2)

    vec = np.zeros((P, NVEC), np.float32)

    def put(name, v):
        vec[:v.shape[0], VEC[name]:VEC[name] + v.shape[1]] = v

    for name in ("ffn1_norm", "mix_norm", "ffn2_norm", "ple_norm"):
        put(name, _columns(g[name][0]))
    put("g_norm", _columns(g["g_norm_2"][0]))
    for name in ("q_norm", "k_norm"):
        put(name, np.concatenate([g[name][0], g[name][0]])[:, None])
    put("forget_bias", g["forget_bias"][0][:, None])
    bg = g["b_gate_2"][0]
    put("b_gate", np.stack([_columns(bg[D:]), _columns(bg[:D])], 2).reshape(P, 2 * DT))
    put("w_short", np.stack([_columns(g["w_short_2"][0][j]) for j in range(3)], 2).reshape(P, 36))
    put("b_short", _columns(g["b_short_2"][0]))
    put("g_cq", _columns(g["g_cq_2"][0]))
    put("g_ckv", _columns(g["g_ckv_2"][0]))
    for name in ("g_qn", "g_kn"):
        put(name, _rope_rows(g[name + "_2"][0])[:, None])
    for name in ("b_f1", "freq_1", "b_f2", "freq_2"):
        put(name, g[name + "_2"][0][:, None])
    vec[:, VEC["eps"]] = EPS

    arrays = {
        "wk": wk, "wd": wd, "wp": wp,
        "x": np.ascontiguousarray(g["x"][0].T).reshape(DT, P, T).transpose(1, 0, 2),
        "p": np.ascontiguousarray(g["p"][0, 0].T).reshape(2, P, T).transpose(1, 0, 2),
        "vec": vec, "constf": constf, "constr": constr, "sel": sel, "rope": rope, "decay": decay, "pos": posT,
        "wf1": g["w_f1_2"][0], "wf2": g["w_f2_2"][0], "wf3": g["w_f3_2"][0], "hyb": g["hy_bias_2"],
    }
    arrays = {k: np.ascontiguousarray(v) for k, v in arrays.items()}
    nc = _bacc.Bacc("TRN2", target_bir_lowering=False, num_devices=1)
    args = [nc.dram_tensor(f"{k}_dram", v.shape, F32, kind="ExternalInput").ap() for k, v in arrays.items()]
    args.append(nc.dram_tensor("out_dram", (P, DT, T), F32, kind="ExternalOutput").ap())
    build(nc, *args)
    r = _run(nc, [{f"{k}_dram": v for k, v in arrays.items()}], core_ids=[0])
    got = r.results[0]["out_dram"]
    return np.ascontiguousarray(got.transpose(1, 0, 2).reshape(D, T).T).reshape(1, T, D)
```
